# Optimizing a Trainium2 kernel written in Bass

```python
import jax, jax.numpy as jnp
from jax import lax
import numpy as np

D_MODEL = 1024
BATCH = 1
SEQ = 256
DEPTH = 1

GRID_W = 64
EPS = 1e-6

GLA_HEADS = 4
GLA_DK = 64
GLA_DV = 128
GLA_RANK = 16
GLA_NORMALIZER = 16.0
GLA_CHUNK = 64

ATT_HEADS = 8
ATT_KV_HEADS = 2
ATT_DH = 64
Q_BLOCK = 128
ROPE_THETA = 10000.0

N_EXPERTS = 32
TOP_K = 4
D_FF = D_MODEL
SWIGLU_ALPHA = 1.702
SWIGLU_LIMIT = 7.0
EXPERT_BLOCK = 256

GLA_QK = GLA_HEADS * GLA_DK
GLA_V = GLA_HEADS * GLA_DV
ATT_Q = ATT_HEADS * ATT_DH
ATT_KV = ATT_KV_HEADS * ATT_DH
D_MIX = GLA_V + ATT_Q
IN_SPLITS = (GLA_QK, GLA_QK, GLA_V, GLA_V, GLA_RANK, GLA_RANK, ATT_Q, ATT_KV, ATT_KV)
D_IN = GLA_QK * 2 + GLA_V * 2 + GLA_RANK * 2 + ATT_Q + ATT_KV * 2

kernel_name = "hybrid_gla_axialgqa_moe_encoder"

def rms_norm(x, g):
    xf = x.astype(jnp.float32)
    y = xf * lax.rsqrt(jnp.mean(xf * xf, axis=-1, keepdims=True) + EPS)
    return (y * g.astype(jnp.float32)).astype(x.dtype)

def split_cols(z, sizes):
    out, o = [], 0
    for s in sizes:
        out.append(z[..., o:o + s])
        o += s
    return out

def gla_chunked(q, k, v, g, strict):
    B, H, S, DK = q.shape
    DV = v.shape[-1]
    C = GLA_CHUNK
    N = S // C
    qf = q.astype(jnp.float32).reshape(B, H, N, C, DK)
    kf = k.astype(jnp.float32).reshape(B, H, N, C, DK)
    vf = v.astype(jnp.float32).reshape(B, H, N, C, DV)
    b = jnp.cumsum(g.astype(jnp.float32).reshape(B, H, N, C, DK), axis=3)
    b_last = b[:, :, :, C - 1:C]
    b_mid = b[:, :, :, C // 2 - 1:C // 2]
    scores = jnp.einsum('bhnid,bhnjd->bhnij', qf * jnp.exp(b - b_mid), kf * jnp.exp(b_mid - b))
    pos = jnp.arange(C)
    mask = (pos[:, None] > pos[None, :]) if strict else (pos[:, None] >= pos[None, :])
    scores = jnp.where(mask, scores, 0.0)
    o_intra = jnp.einsum('bhnij,bhnjv->bhniv', scores, vf)
    delta = jnp.einsum('bhncd,bhncv->bhndv', kf * jnp.exp(b_last - b), vf)
    decay = jnp.exp(b_last[:, :, :, 0])

    def step(state, inp):
        d, dl = inp
        return d[..., None] * state + dl, state

    s0 = jnp.zeros((B, H, DK, DV), jnp.float32)
    _, s_prev = lax.scan(step, s0, (jnp.moveaxis(decay, 2, 0), jnp.moveaxis(delta, 2, 0)))
    s_prev = jnp.moveaxis(s_prev, 0, 2)
    o_inter = jnp.einsum('bhncd,bhndv->bhncv', qf * jnp.exp(b), s_prev)
    return (o_intra + o_inter).reshape(B, H, S, DV)

def gla_group(q, k, v, r, zf, zb, w_gf, b_gf, w_gb, b_gb, head_g):
    B, S, _ = q.shape

    def heads(t, d):
        return t.reshape(B, S, GLA_HEADS, d).transpose(0, 2, 1, 3)

    g_fwd = jax.nn.log_sigmoid((zf @ w_gf + b_gf).astype(jnp.float32)) / GLA_NORMALIZER
    g_bwd = jax.nn.log_sigmoid((zb @ w_gb + b_gb).astype(jnp.float32)) / GLA_NORMALIZER
    qh = heads(q, GLA_DK) * (GLA_DK ** -0.5)
    kh = heads(k, GLA_DK)
    vh = heads(v, GLA_DV)
    o_f = gla_chunked(qh, kh, vh, heads(g_fwd, GLA_DK), strict=False)
    flip = lambda t: jnp.flip(t, axis=2)
    o_b = flip(gla_chunked(flip(qh), flip(kh), flip(vh), flip(heads(g_bwd, GLA_DK)), strict=True))
    o = rms_norm(o_f + o_b, head_g)
    o = o.transpose(0, 2, 1, 3).reshape(B, S, GLA_V)
    return (o * jax.nn.silu(r.astype(jnp.float32))).astype(q.dtype)

def rope_1d(x, pos):
    half = x.shape[-1] // 2
    inv = ROPE_THETA ** (-jnp.arange(half, dtype=jnp.float32) / half)
    ang = pos.astype(jnp.float32)[:, None] * inv[None, :]
    cos = jnp.cos(ang)[:, None, :]
    sin = jnp.sin(ang)[:, None, :]
    x1, x2 = x[..., :half], x[..., half:]
    return jnp.concatenate([x1 * cos - x2 * sin, x2 * cos + x1 * sin], axis=-1)

def axial_rope(x, row_pos, col_pos):
    h = x.shape[-1] // 2
    return jnp.concatenate([rope_1d(x[..., :h], row_pos), rope_1d(x[..., h:], col_pos)], axis=-1)

def gqa_group(q, k, v, q_g, k_g, row_pos, col_pos):
    B, S, _ = q.shape
    G = ATT_HEADS // ATT_KV_HEADS
    NB = S // Q_BLOCK
    qh = q.reshape(B, S, ATT_HEADS, ATT_DH)
    kh = k.reshape(B, S, ATT_KV_HEADS, ATT_DH)
    vh = v.reshape(B, S, ATT_KV_HEADS, ATT_DH)
    qf = axial_rope(rms_norm(qh, q_g).astype(jnp.float32), row_pos, col_pos) * (ATT_DH ** -0.5)
    kf = axial_rope(rms_norm(kh, k_g).astype(jnp.float32), row_pos, col_pos)
    qb = qf.reshape(B, NB, Q_BLOCK, ATT_KV_HEADS, G, ATT_DH).transpose(1, 0, 3, 4, 2, 5)
    kf = kf.transpose(0, 2, 1, 3)
    vf = vh.astype(jnp.float32).transpose(0, 2, 1, 3)

    def attend(q_blk):
        s = jnp.einsum('bkgqd,bksd->bkgqs', q_blk, kf)
        p = jax.nn.softmax(s, axis=-1)
        return jnp.einsum('bkgqs,bksd->bkgqd', p, vf)

    o = lax.map(attend, qb)
    o = o.transpose(1, 0, 4, 2, 3, 5).reshape(B, S, ATT_Q)
    return o.astype(q.dtype)

def moe_ffn(x, w_router, b_router, w1, b1, w2, b2):
    B, S, D = x.shape
    xt = x.reshape(-1, D)
    T = xt.shape[0]
    A = T * TOP_K
    logits = (xt @ w_router + b_router).astype(jnp.float32)
    top_val, top_idx = lax.top_k(logits, TOP_K)
    gates = jax.nn.softmax(top_val, axis=-1)
    flat_e = top_idx.reshape(-1)
    order = jnp.argsort(flat_e)
    sorted_e = flat_e[order]
    tok_sorted = order // TOP_K
    gate_sorted = gates.reshape(-1)[order]
    counts = jnp.bincount(flat_e, length=N_EXPERTS).astype(jnp.int32)
    padded = ((counts + EXPERT_BLOCK - 1) // EXPERT_BLOCK) * EXPERT_BLOCK
    starts_sorted = jnp.cumsum(counts) - counts
    pad_ends = jnp.cumsum(padded)
    starts_pad = pad_ends - padded
    dest = starts_pad[sorted_e] + (jnp.arange(A, dtype=jnp.int32) - starts_sorted[sorted_e])
    P = ((A + EXPERT_BLOCK - 1) // EXPERT_BLOCK) * EXPERT_BLOCK + N_EXPERTS * EXPERT_BLOCK
    n_blocks = P // EXPERT_BLOCK
    buf = jnp.zeros((P, D), xt.dtype).at[dest].set(xt[tok_sorted])
    block_start = jnp.arange(n_blocks, dtype=jnp.int32) * EXPERT_BLOCK
    block_expert = jnp.minimum(jnp.searchsorted(pad_ends, block_start, side='right'), N_EXPERTS - 1)

    def expert_block(args):
        xb, e = args
        h = (xb @ w1[e] + b1[e]).astype(jnp.float32)
        h_glu = jnp.minimum(h[:, :D_FF], SWIGLU_LIMIT)
        h_lin = jnp.clip(h[:, D_FF:], -SWIGLU_LIMIT, SWIGLU_LIMIT)
        act = (h_glu * jax.nn.sigmoid(SWIGLU_ALPHA * h_glu) * (h_lin + 1.0)).astype(xb.dtype)
        return act @ w2[e] + b2[e]

    yb = lax.map(expert_block, (buf.reshape(n_blocks, EXPERT_BLOCK, D), block_expert))
    y_assign = yb.reshape(P, D)[dest].astype(jnp.float32) * gate_sorted[:, None]
    y = jax.ops.segment_sum(y_assign, tok_sorted, num_segments=T)
    return y.reshape(B, S, D).astype(x.dtype)

def setup_inputs(seed: int = 0) -> dict:
    key = jax.random.key(seed)
    ks = jax.random.split(key, 20)
    f32 = jnp.float32
    L = DEPTH

    def nrm(k, shape, scale):
        return jax.random.normal(k, shape, f32) * scale

    def gain(k, shape):
        return 1.0 + 0.05 * jax.random.normal(k, shape, f32)

    return {
        "x": nrm(ks[0], (BATCH, SEQ, D_MODEL), 1.0),
        "mix_norm_g": gain(ks[1], (L, D_MODEL)),
        "w_in": nrm(ks[2], (L, D_MODEL, D_IN), D_MODEL ** -0.5),
        "w_gate_f": nrm(ks[3], (L, GLA_RANK, GLA_QK), GLA_RANK ** -0.5),
        "b_gate_f": nrm(ks[4], (L, GLA_QK), 0.1),
        "w_gate_b": nrm(ks[5], (L, GLA_RANK, GLA_QK), GLA_RANK ** -0.5),
        "b_gate_b": nrm(ks[6], (L, GLA_QK), 0.1),
        "gla_head_g": gain(ks[7], (L, GLA_DV)),
        "q_norm_g": gain(ks[8], (L, ATT_DH)),
        "k_norm_g": gain(ks[9], (L, ATT_DH)),
        "w_out": nrm(ks[10], (L, D_MIX, D_MODEL), D_MIX ** -0.5),
        "ffn_norm_g": gain(ks[11], (L, D_MODEL)),
        "w_router": nrm(ks[12], (L, D_MODEL, N_EXPERTS), D_MODEL ** -0.5),
        "b_router": nrm(ks[13], (L, N_EXPERTS), 0.01),
        "w1": nrm(ks[14], (L, N_EXPERTS, D_MODEL, 2 * D_FF), D_MODEL ** -0.5),
        "b1": nrm(ks[15], (L, N_EXPERTS, 2 * D_FF), 0.02),
        "w2": nrm(ks[16], (L, N_EXPERTS, D_FF, D_MODEL), D_FF ** -0.5),
        "b2": nrm(ks[17], (L, N_EXPERTS, D_MODEL), 0.02),
        "final_norm_g": gain(ks[18], (D_MODEL,)),
    }

def reference(x, mix_norm_g, w_in, w_gate_f, b_gate_f, w_gate_b, b_gate_b, gla_head_g,
              q_norm_g, k_norm_g, w_out, ffn_norm_g, w_router, b_router, w1, b1, w2, b2,
              final_norm_g):
    B, S, D = x.shape
    rows = S // GRID_W
    row_pos = jnp.repeat(jnp.arange(rows, dtype=jnp.int32), GRID_W)
    col_pos = jnp.tile(jnp.arange(GRID_W, dtype=jnp.int32), rows)
    h = x
    for l in range(DEPTH):
        n = rms_norm(h, mix_norm_g[l])
        z = n @ w_in[l]
        gq, gk, gv, gr, zf, zb, aq, ak, av = split_cols(z, IN_SPLITS)
        o_gla = gla_group(gq, gk, gv, gr, zf, zb, w_gate_f[l], b_gate_f[l],
                          w_gate_b[l], b_gate_b[l], gla_head_g[l])
        o_att = gqa_group(aq, ak, av, q_norm_g[l], k_norm_g[l], row_pos, col_pos)
        h = h + jnp.concatenate([o_gla, o_att], axis=-1) @ w_out[l]
        h = h + moe_ffn(rms_norm(h, ffn_norm_g[l]), w_router[l], b_router[l],
                        w1[l], b1[l], w2[l], b2[l])
    return rms_norm(h, final_norm_g)


_drawn_inputs = setup_inputs


def setup_inputs(seed=0):
    import zlib

    import numpy as np

    out = dict(_drawn_inputs(seed))
    spreads = {}
    factors = {'q_norm_g': 4.03, 'k_norm_g': 3.393, 'b1': 5.42, 'b2': 6.244}
    for name, (base, spread) in spreads.items():
        noise = np.random.default_rng([zlib.crc32(name.encode()), seed]).standard_normal(out[name].shape)
        drawn = base * np.exp(spread * noise) if base else spread * noise
        out[name] = __import__('jax').numpy.asarray(drawn.astype(out[name].dtype))
    for name, factor in factors.items():
        out[name] = (out[name] * factor).astype(out[name].dtype)
    return out
```

```python
from contextlib import ExitStack

import numpy as np

import concourse.bass as bass
from concourse import mybir

F32 = mybir.dt.float32
I32 = mybir.dt.int32
U32 = mybir.dt.uint32
ALU = mybir.AluOpType
ACT = mybir.ActivationFunctionType
AX = mybir.AxisListType

P = 128
SEQ = 256
TILES = SEQ // P
D = 1024
KD = D // P
EPS = 1e-6
GRID_W = 64

GLA_HEADS, DK, DV, RANK, CHUNK = 4, 64, 128, 16, 64
GLA_NORMALIZER = 16.0
CHUNKS = SEQ // CHUNK
HEADS, KV_HEADS, DH = 8, 2, 64
ROPE_THETA = 10000.0
EXPERTS, TOP_K, FF = 32, 4, 1024
ALPHA, LIMIT = 1.702, 7.0

GLA_QK, GLA_V, ATT_Q, ATT_KV = GLA_HEADS * DK, GLA_HEADS * DV, HEADS * DH, KV_HEADS * DH
C_GQ = 0
C_GK = C_GQ + GLA_QK
C_GV = C_GK + GLA_QK
C_GR = C_GV + GLA_V
C_ZG = C_GR + GLA_V
C_AQ = C_ZG + 2 * RANK
C_AK = C_AQ + ATT_Q
C_AV = C_AK + ATT_KV
D_IN = C_AV + ATT_KV

CAP = 64
GROUPS = P // CAP
ROUNDS = SEQ // CAP
FG = FF // GROUPS
SUB = FG // P
SLOTS = 16
SLOT = 2048
W1_CHUNKS = KD
W2_CHUNKS = SUB
PER_EXPERT = W1_CHUNKS + W2_CHUNKS
UNROLL = 4
PER_BODY = UNROLL * PER_EXPERT
assert PER_BODY % SLOTS == 0 and EXPERTS % UNROLL == 0 and GROUPS * 1024 == SLOT
LOADS_PER_BODY = PER_BODY // SLOTS
EARLY = 9
TABLE = ROUNDS * EXPERTS + UNROLL


def shape_constants():
    p = np.arange(P)
    ident = np.eye(P)
    iota = np.tile(np.arange(CAP), (P, GROUPS))
    before = (p[:, None] < p[None, :]) * 1.0
    ones = np.ones((P, P))
    keep = np.tile((np.arange(2 * SEQ) % CHUNK != 0) * 1.0, (P, 1))
    half = DH // 4
    inv = ROPE_THETA ** (-np.arange(half, dtype=np.float32) / np.float32(half))
    token = np.arange(TILES)[None, :] * P + p[:, None]
    ang = np.stack([token // GRID_W, token % GRID_W], -1)[..., None].astype(np.float32) * inv.astype(np.float32)
    cos = np.cos(ang.astype(np.float32))
    sin = np.sin(ang.astype(np.float32))
    cos = np.stack([cos, cos], 3).reshape(P, TILES * DH)
    sin = np.stack([-sin, sin], 3).reshape(P, TILES * DH)
    return {
        "c_keep": [ident, iota, before, ones],
        "c_front": [keep, cos, sin],
    }


def encoder_layer(nc, x, w_in, w_out, w_router, w1, b1, w2, b2, gate_w, columns, rows, final_g,
                  c_keep, c_front, later, split, out):
    ctx = ExitStack()
    with ctx:
        def sb(name, shape, dt=F32):
            return ctx.enter_context(nc.sbuf_tensor(name, shape, dt))[tuple(slice(None) for _ in shape)]

        def sem(name):
            return ctx.enter_context(nc.semaphore(name))

        ring = sb("ring", [P, SLOTS * SLOT])
        h = sb("h", [P, TILES, D])
        tok = sb("tok", [P, TILES, D])
        ckeep = sb("ckeep", [P, 4 * P])
        ident, iota, before, ones = (ckeep[:, i * P:(i + 1) * P] for i in range(4))
        b2_sb = sb("b2_sb", [EXPERTS, D])
        split_sb = sb("split_sb", [GROUPS, P])
        wr_sb = sb("wr_sb", [P, KD, EXPERTS])
        col = sb("col", [P, 2 * KD + 4])
        mix_g, ffn_g, gate_b = col[:, 0:KD], col[:, KD:2 * KD], col[:, 2 * KD:2 * KD + 4]
        later_sb = sb("later_sb", [P, CHUNK], I32)
        stat = sb("stat", [P, 128])
        extra = sb("extra", [1, 4], I32)
        work = sb("work", [P, 13900])

        class Carve:

            def __init__(self, base, start=0):
                self.base, self.at = base, start

            def __call__(self, *shape):
                n = int(np.prod(shape))
                piece = self.base[:, self.at:self.at + n]
                self.at += n
                if len(shape) == 2:
                    piece = piece.rearrange("p (a b) -> p a b", b=shape[1])
                elif len(shape) == 3:
                    piece = piece.rearrange("p (a b c) -> p a b c", b=shape[1], c=shape[2])
                return piece

        front = Carve(work)
        turned = front(KD, SEQ)
        gqk = front(2, 2 * SEQ)
        zg = front(SEQ)
        wg = front(4 * P)
        cfront = front(2 * SEQ + 2 * TILES * DH)
        keep = cfront[:, 0:2 * SEQ]
        cos = cfront[:, 2 * SEQ:2 * SEQ + TILES * DH].rearrange("p (t d) -> p t d", d=DH)
        sin = cfront[:, 2 * SEQ + TILES * DH:2 * SEQ + 2 * TILES * DH].rearrange("p (t d) -> p t d", d=DH)
        QK = ATT_Q + ATT_KV
        at_raw = front.at
        raw = front(TILES, QK)
        at_rot = front.at
        rot = front(TILES, QK)
        swp = front(TILES, QK)
        tab = front(2, 2, TILES * DH)
        row = front(2 * DH + DV + EXPERTS)
        q_g, k_g, head_g, router_b = row[:, 0:DH], row[:, DH:2 * DH], row[:, 2 * DH:2 * DH + DV], row[:, 2 * DH + DV:]
        qkT = front(5, SEQ)
        av = front(TILES, ATT_KV)
        gv = front(TILES, GLA_V)
        sg = front(TILES, GLA_V)
        att2 = front(2, 2 * SEQ)
        assert front.at <= 13900
        reuse = Carve(work, at_raw)
        att01 = reuse(2, 2 * SEQ)
        reuse = Carve(work, at_rot)
        prob = reuse(2, 2 * SEQ)
        probT = reuse(2, 2 * SEQ)
        mix = [att01[:, 0, :], att01[:, 1, :], att2[:, 0, :], att2[:, 1, :]]
        scratch = Carve(ring, 14 * SLOT)
        gA, gM, gB, gX = (scratch(4, SEQ) for _ in range(4))
        decayed = Carve(ring, KD * D_IN)
        kk = decayed(4, 7, CHUNK)
        assert decayed.at <= (EARLY + 1) * SLOT
        w_in_sb = ring[:, 0:KD * D_IN].rearrange("p (k n) -> p k n", n=D_IN)
        w_out_sb = ring[:, 10 * SLOT:14 * SLOT].rearrange("p (k n) -> p k n", n=D)

        back = Carve(work, KD * SEQ)
        logit = back(TILES, EXPERTS)
        top = back(TILES, 8)
        topi = back(TILES * 8)
        topf = back(TILES, 8)
        hit = back(TILES, TOP_K * EXPERTS)
        chosen = back(TILES, EXPERTS)
        weight = back(TILES, EXPERTS)
        rank = back(TILES, EXPERTS)
        rank_t = back(TILES, TABLE)
        gate_t = back(TILES, TABLE)
        gateT = back(SEQ)
        b1_sb = back(2, 2 * FG)
        onehot = back(TILES, CAP)
        gated = back(TILES, P)
        gatedT = back(TILES, P)
        xg = back(KD * CAP)
        glu = back(FG)
        lin = back(FG)
        sig = back(FG)
        hid = back(FG)
        hidT = back(SUB, P)
        res = back(D)
        assert back.at <= 13900

        bank = [ctx.enter_context(nc.psum_tensor(f"bank{i}", [P, 512], F32))[:, :] for i in range(8)]

        names = """x0_in x1_in ident_in const_in wout_in b2_in gate_in fin_g_in stored
            sq_done var_done rstd_done n_done nT_ps nT_v nT_a pass1 pass2 pass3
            zg_sb gqk_sb raw_sb raw_sq hss_done hvar_done hrstd_done rope_done
            gates_ps gates_sb gabs gln arg_done exp_done dec_done gla_ready kk_done
            gv_sb gr_exp sg_done qkT_ps qkT_sb
            score_ps nmax_done prob_done probT_ps probT_sb oatt_ps oatt_sb
            mix_ps mix_sb ogla_ps ogla_sq ogla_var ogla_rstd ogla_sb
            oT_ps oT_sb h_ps h_done hsq var2 rstd2 n2_done n2T_ps n2T_sb
            logit_ps logit_done top_done wexp_done chosen_done rank_ps tables_done gateT_ps gateT_sb extra_done
            onehot_ready gathered xg_ready w1_done glu_ready sig_ready hid_ready combined
            gated_ready gatedT_ps gatedT_sb hidT_ps hidT_sb out_a out_v chunk_used
            y_done ysq var3 rstd3 fin_done
            act_step dve_step pool_step""".split()
        S = type("Semaphores", (), {n: sem(n) for n in names})
        win_in = [sem(f"win_in{k}") for k in range(KD)]
        slot_in = [sem(f"slot_in{s}") for s in range(SLOTS)]
        b1_in = [sem(f"b1_in{i}") for i in range(2)]

        block = ctx.enter_context(nc.Block())

        def slot(c):
            return ring[:, (c % SLOTS) * SLOT:(c % SLOTS + 1) * SLOT]

        def w2_slot(c):
            return slot(c).rearrange("p (j n) -> p j n", n=D)

        @block.sync
        def _(sp):
            sp.dma_start(h[:, 0, :], x[0:P, :]).then_inc(S.x0_in, 16)
            sp.dma_start(h[:, 1, :], x[P:SEQ, :]).then_inc(S.x1_in, 16)
            for k in range(KD):
                sp.dma_start(w_in_sb[:, k, :], w_in[k * P:(k + 1) * P, :]).then_inc(win_in[k], 16)
            sp.dma_start(w_out_sb, w_out.rearrange("(k p) n -> p k n", p=P)).then_inc(S.wout_in, 16)

            def load(c, e, r):
                if r < W1_CHUNKS:
                    sp.dma_start(slot(c), w1[e, r * P:(r + 1) * P, :]).then_inc(slot_in[c % SLOTS], 16)
                else:
                    s = r - W1_CHUNKS
                    sp.dma_start(w2_slot(c), w2[e].rearrange("(j s p) n -> s p j n", j=GROUPS, p=P)[s])\
                        .then_inc(slot_in[c % SLOTS], 16)

            def load_b1(n, e):
                sp.dma_start(b1_sb[0:GROUPS, n % 2, :].rearrange("j (g f) -> j g f", g=2),
                             b1[e].rearrange("(g j f) -> j g f", g=2, j=GROUPS)).then_inc(b1_in[n % 2], 16)

            for c in range(EARLY):
                sp.wait_ge(S.pass3, min(KD, ((c + 1) * SLOT - 1) // D_IN + 1))
                load(c, 0, c)
            sp.wait_ge(S.gateT_sb, 1)
            sp.wait_ge(S.h_ps, 1)
            load_b1(0, 0)
            for c in range(EARLY, SLOTS):
                load(c, c // PER_EXPERT, c % PER_EXPERT)
            load_b1(1, 1)

            rounds = sp.value_load(extra[0:1, 0:1], min_val=0, max_val=ROUNDS - 1)

            def refill(it, used, e):
                c = SLOTS + used
                q, r = divmod(c, PER_EXPERT)
                if r == 0:
                    sp.wait_ge(S.w1_done, it * UNROLL + (q - 1))
                    load_b1(q, e)
                sp.wait_ge(S.chunk_used, it * PER_BODY + (used + 1))
                load(c, e, r)

            bodies = EXPERTS // UNROLL
            with sp.Fori(0, rounds * bodies + (bodies - 1)) as it:
                for used in range(PER_BODY):
                    refill(it, used, (it * UNROLL + (SLOTS + used) // PER_EXPERT) % EXPERTS)
            last = rounds * bodies + (bodies - 1)
            for used in range(PER_BODY - SLOTS):
                refill(last, used, EXPERTS - UNROLL + (SLOTS + used) // PER_EXPERT)
            sp.wait_ge(S.chunk_used, last * PER_BODY + (PER_BODY - SLOTS + 1))
            sp.dma_start(slot(0)[:, 0:D], final_g).then_inc(S.fin_g_in, 16)
            for t in range(TILES):
                sp.wait_ge(S.fin_done, t + 1)
                sp.dma_start(out[t * P:(t + 1) * P, :], tok[:, t, :]).then_inc(S.stored, 16)
            sp.wait_ge(S.stored, 16 * TILES)

        @block.gpsimd
        def _(pool):
            minus_half = stat[:, 64:96]
            pool.memset(minus_half, -0.5).then_inc(S.pool_step, 1)
            pool.wait_ge(S.pool_step, 1)
            pool.wait_ge(S.var_done, 1)
            pool.tensor_tensor(stat[:, 4:6], stat[:, 2:4], minus_half[:, 0:2], ALU.pow).then_inc(S.rstd_done, 1)
            pool.wait_ge(S.hvar_done, 1)
            pool.tensor_tensor(stat[:, 28:48], stat[:, 8:28], minus_half[:, 0:20], ALU.pow).then_inc(S.hrstd_done, 1)
            pool.wait_ge(S.ogla_var, 1)
            pool.tensor_tensor(stat[:, 56:64], stat[:, 48:56], minus_half[:, 0:8], ALU.pow).then_inc(S.ogla_rstd, 1)
            for t in range(TILES):
                pool.wait_ge(S.var2, t + 1)
                pool.tensor_tensor(stat[:, 4 + t:5 + t], stat[:, 2 + t:3 + t], minus_half[:, 0:1], ALU.pow)\
                    .then_inc(S.rstd2, 1)
            for t in range(TILES):
                pool.wait_ge(S.var3, t + 1)
                pool.tensor_tensor(stat[:, 4 + t:5 + t], stat[:, 2 + t:3 + t], minus_half[:, 0:1], ALU.pow)\
                    .then_inc(S.rstd3, 1)

        @block.scalar
        def _(act):
            act.dma_start(ckeep, c_keep).then_inc(S.ident_in, 16)
            act.dma_start(col, columns).then_inc(S.ident_in, 16)
            act.dma_start(cfront, c_front).then_inc(S.const_in, 16)
            act.dma_start(wg[0:2 * RANK, :], gate_w).then_inc(S.const_in, 16)
            act.dma_start(row, rows).then_inc(S.const_in, 16)
            act.dma_start(later_sb, later).then_inc(S.const_in, 16)
            act.dma_start(wr_sb, w_router.rearrange("p (k e) -> p k e", e=EXPERTS)).then_inc(S.const_in, 16)
            act.dma_start(split_sb, split).then_inc(S.const_in, 16)
            act.dma_start(b2_sb, b2).then_inc(S.const_in, 16)

            for t, loaded in enumerate((S.x0_in, S.x1_in)):
                act.wait_ge(loaded, 16)
                nc.scalar.activation((rot if t == 0 else swp)[:, :, :].rearrange("p a b -> p (a b)")[:, 0:D], h[:, t, :],
                                     ACT.Square, accum_out=stat[:, t:t + 1]).then_inc(S.sq_done, 1)
            act.wait_ge(S.rstd_done, 1)
            nc.scalar.activation(tok[:, 1, :], h[:, 1, :], ACT.Copy, scale=stat[:, 5:6]).then_inc(S.n_done, 1)
            act.wait_ge(S.ident_in, 32)
            for k in (2, 3, 6, 7):
                act.wait_ge(S.nT_ps, k // 2 + 1)
                nc.scalar.activation(turned[:, k, :], bank[7][:, (k % 2) * SEQ:(k % 2 + 1) * SEQ], ACT.Copy,
                                     scale=mix_g[:, k:k + 1]).then_inc(S.nT_a, 1)

            act.wait_ge(S.pass1, 1)
            nc.scalar.activation(zg[0:2 * RANK, :], bank[2][0:2 * RANK, 0:SEQ], ACT.Copy).then_inc(S.zg_sb, 1)
            nc.scalar.activation(gqk[:, 0, :], bank[0][:, :], ACT.Copy, scale=DK ** -0.5).then_inc(S.gqk_sb, 1)
            nc.scalar.activation(gqk[:, 1, :], bank[1][:, :], ACT.Copy).then_inc(S.gqk_sb, 1)
            act.wait_ge(S.raw_sb, 3 * TILES)
            nc.scalar.activation(rot, raw, ACT.Square).then_inc(S.raw_sq, 1)
            act.wait_ge(S.gates_sb, 1)
            nc.scalar.activation(gA, gM, ACT.Abs).then_inc(S.gabs, 1)
            act.wait_ge(S.gabs, 1)
            nc.scalar.activation(gA, gA, ACT.Exp, scale=-1.0).then_inc(S.gabs, 1)
            act.wait_ge(S.gabs, 2)
            nc.scalar.activation(gA, gA, ACT.Ln, bias=1.0).then_inc(S.gln, 1)
            act.wait_ge(S.pass2, KD)
            for t in range(TILES):
                nc.scalar.activation(gv[:, t, :], bank[6 + t][:, :], ACT.Copy).then_inc(S.gv_sb, 1)
            act.wait_ge(S.arg_done, 1)
            nc.scalar.activation(gX, gA, ACT.Exp, scale=1.0 / GLA_NORMALIZER).then_inc(S.exp_done, 1)
            act.wait_ge(S.exp_done, 1)
            nc.scalar.activation(gA, gA, ACT.Exp, scale=-1.0 / GLA_NORMALIZER).then_inc(S.exp_done, 1)
            act.wait_ge(S.arg_done, 2)
            nc.scalar.activation(gB, gB, ACT.Exp, scale=1.0 / GLA_NORMALIZER).then_inc(S.exp_done, 1)
            nc.scalar.activation(gM, gM, ACT.Exp, scale=1.0 / GLA_NORMALIZER).then_inc(S.exp_done, 1)
            act.wait_ge(S.pass3, KD)
            for t in range(TILES):
                nc.scalar.activation(sg[:, t, :], bank[3 + t][:, :], ACT.Exp, scale=-1.0).then_inc(S.gr_exp, 1)

            def weights_out(hd):
                act.wait_ge(S.probT_ps, hd + 1)
                if hd >= 2:
                    act.wait_ge(S.oatt_ps, hd - 1)
                nc.scalar.activation(probT[:, hd % 2, :], bank[6 + hd % 2][:, :], ACT.Copy).then_inc(S.probT_sb, 1)

            for hd in range(HEADS):
                act.wait_ge(S.nmax_done, hd + 1)
                if hd >= 2:
                    act.wait_ge(S.probT_ps, hd - 1)
                for t in range(TILES):
                    nc.scalar.activation(prob[:, hd % 2, t * SEQ:(t + 1) * SEQ],
                                         bank[(5, 2)[hd % 2]][:, t * SEQ:(t + 1) * SEQ], ACT.Exp,
                                         bias=stat[:, 96 + 2 * hd + t:97 + 2 * hd + t],
                                         accum_out=stat[:, 112 + t * HEADS + hd:113 + t * HEADS + hd])\
                        .then_inc(S.prob_done, 1)
                if hd >= 1:
                    weights_out(hd - 1)
            weights_out(HEADS - 1)

            for hd in range(0, GLA_HEADS, 2):
                act.wait_ge(S.mix_ps, hd + 1)
                nc.scalar.activation(mix[hd], bank[5][:, :], ACT.Copy).then_inc(S.mix_sb, 1)
            act.wait_ge(S.ogla_ps, 1)
            for t in range(TILES):
                nc.scalar.activation(tok[:, t, 0:GLA_V], bank[6 + t][:, :], ACT.Square).then_inc(S.ogla_sq, 1)

            for i, b in ((1, 4), (3, 6)):
                act.wait_ge(S.oT_ps, i + 1)
                k0 = 4 if i == 1 else 0
                nc.scalar.activation(turned[:, k0:k0 + 4, P:SEQ],
                                     bank[b + 1][:, :].rearrange("p (k t) -> p k t", t=P), ACT.Copy)\
                    .then_inc(S.oT_sb, 1)

            for t in range(TILES):
                act.wait_ge(S.h_done, t + 1)
                nc.scalar.activation(tok[:, t, :], h[:, t, :], ACT.Square,
                                     accum_out=stat[:, t:t + 1]).then_inc(S.hsq, 1)
            act.wait_ge(S.rstd2, 2)
            act.wait_ge(S.hsq, 2)
            nc.scalar.activation(tok[:, 1, :], h[:, 1, :], ACT.Copy, scale=stat[:, 5:6]).then_inc(S.n2_done, 1)
            for k in (2, 3, 6, 7):
                act.wait_ge(S.n2T_ps, k // 2 + 1)
                nc.scalar.activation(turned[:, k, :], bank[4 + k // 2][:, (k % 2) * SEQ:(k % 2 + 1) * SEQ], ACT.Copy,
                                     scale=ffn_g[:, k:k + 1]).then_inc(S.n2T_sb, 1)
            act.wait_ge(S.top_done, 1)
            for t in range(TILES):
                nc.scalar.activation(weight[:, t, :], logit[:, t, :], ACT.Exp, bias=stat[:, 6 + t:7 + t])\
                    .then_inc(S.wexp_done, 1)

            rounds_sb_ready = S.extra_done
            act.wait_ge(rounds_sb_ready, 1)
            rounds = act.value_load(extra[0:1, 0:1], min_val=0, max_val=ROUNDS - 1)

            def expert(n):
                act.wait_ge(S.glu_ready, n + 1)
                nc.scalar.activation(sig, glu, ACT.Sigmoid, scale=ALPHA).then_inc(S.sig_ready, 1)
                act.wait_ge(S.gatedT_ps, n + 1)
                nc.scalar.activation(gatedT, bank[7][:, 0:SEQ].rearrange("p (t q) -> p t q", q=P), ACT.Copy)\
                    .then_inc(S.gatedT_sb, 1)
                act.wait_ge(S.hidT_ps, n + 1)
                nc.scalar.activation(hidT, bank[7][:, :].rearrange("p (s q) -> p s q", q=P), ACT.Copy)\
                    .then_inc(S.hidT_sb, 1)
                act.wait_ge(S.chunk_used, (n + 1) * PER_EXPERT)
                nc.scalar.activation(res[:, 0:512], bank[4][:, :], ACT.Copy).then_inc(S.out_a, 1)

            for n in range(UNROLL):
                expert(n)
            bodies = EXPERTS // UNROLL
            with act.Fori(1, rounds * bodies + bodies) as it:
                for q in range(UNROLL):
                    expert(it * UNROLL + q)

            for t in range(TILES):
                act.wait_ge(S.y_done, t + 1)
                nc.scalar.activation(tok[:, t, :], h[:, t, :], ACT.Square,
                                     accum_out=stat[:, t:t + 1]).then_inc(S.ysq, 1)

        @block.vector
        def _(dve):
            steps = [0]

            def step(ins):
                steps[0] += 1
                ins.then_inc(S.dve_step, 1)
                dve.wait_ge(S.dve_step, steps[0])

            def mean_eps(out_, in_, n):
                return nc.vector.tensor_scalar(out_, in_, 1.0 / n, EPS, ALU.mult, ALU.add)

            dve.wait_ge(S.sq_done, 2)
            mean_eps(stat[:, 2:4], stat[:, 0:2], D).then_inc(S.var_done, 1)
            dve.wait_ge(S.rstd_done, 1)
            nc.vector.tensor_scalar(tok[:, 0, :], h[:, 0, :], stat[:, 4:5], None, ALU.mult).then_inc(S.n_done, 1)
            dve.wait_ge(S.ident_in, 32)
            for k in (0, 1, 4, 5):
                dve.wait_ge(S.nT_ps, k // 2 + 1)
                nc.vector.tensor_scalar(turned[:, k, :], bank[6][:, (k % 2) * SEQ:(k % 2 + 1) * SEQ], mix_g[:, k:k + 1], None,
                                        ALU.mult).then_inc(S.nT_v, 1)
            dve.wait_ge(S.const_in, 16 * 7)
            for i, g in enumerate((q_g, k_g)):
                scale = DH ** -0.5 if i == 0 else 1.0
                for t in range(TILES):
                    nc.vector.scalar_tensor_tensor(tab[:, i, 0, t * DH:(t + 1) * DH], cos[:, t, :], scale, g,
                                                   ALU.mult, ALU.mult)
                    gs = g.rearrange("p (a f d) -> p a f d", a=2, f=2)
                    for f in range(2):
                        last = nc.vector.scalar_tensor_tensor(
                            tab[:, i, 1, t * DH:(t + 1) * DH].rearrange("p (a f d) -> p a f d", a=2, f=2)[:, :, f, :],
                            sin[:, t, :].rearrange("p (a f d) -> p a f d", a=2, f=2)[:, :, f, :], scale,
                            gs[:, :, 1 - f, :], ALU.mult, ALU.mult)
            step(last)

            dve.wait_ge(S.pass1, 1)
            for t in range(TILES):
                nc.vector.tensor_copy(raw[:, t, 0:ATT_Q].rearrange("p (b k d) -> p k b d", k=KV_HEADS, d=DH),
                                      bank[3 + t][:, :].rearrange("p (k b d) -> p k b d", k=KV_HEADS, d=DH))\
                    .then_inc(S.raw_sb, 1)
                nc.vector.tensor_copy(raw[:, t, ATT_Q:QK], bank[5][:, t * SEQ:t * SEQ + ATT_KV]).then_inc(S.raw_sb, 1)
                nc.vector.tensor_copy(av[:, t, :], bank[5][:, t * SEQ + ATT_KV:(t + 1) * SEQ]).then_inc(S.raw_sb, 1)
            dve.wait_ge(S.gates_ps, 1)
            for g in range(4):
                last = nc.vector.tensor_scalar(gM[:, g, :], bank[g // 2][:, (g % 2) * SEQ:(g % 2 + 1) * SEQ],
                                               gate_b[:, g:g + 1], None, ALU.add)
            last.then_inc(S.gates_sb, 1)
            NH = HEADS + KV_HEADS
            dve.wait_ge(S.raw_sq, 1)
            step(nc.vector.tensor_reduce(stat[:, 28:48], rot.rearrange("p t (h d) -> p (t h) d", d=DH), AX.X, ALU.add))
            mean_eps(stat[:, 8:28], stat[:, 28:48], DH).then_inc(S.hvar_done, 1)
            dve.wait_ge(S.gln, 1)
            step(nc.vector.scalar_tensor_tensor(gM, gM, 0.0, gA, ALU.min, ALU.subtract))
            flat = [t.rearrange("p g t -> p (g t)") for t in (gM, gB, gA)]
            half = 2 * SEQ
            nc.vector.tensor_tensor_scan(flat[1][:, 0:half], keep, flat[0][:, 0:half], 0.0, ALU.mult, ALU.add)
            step(nc.vector.tensor_tensor_scan(flat[1][:, 2 * half - 1:half - 1:-1], keep, flat[0][:, 2 * half - 1:half - 1:-1],
                                              0.0, ALU.mult, ALU.add))

            def chunked(buf, direction):
                return buf[:, 2 * direction:2 * direction + 2, :].rearrange("p g (c i) -> p (g c) i", i=CHUNK)

            mid = (CHUNK // 2 - 1, CHUNK // 2)
            edge = (CHUNK - 1, 0)
            shape = [P, 2 * CHUNKS, CHUNK]
            for d in range(2):
                b = chunked(gB, d)
                last = nc.vector.tensor_tensor(chunked(gA, d), b, b[:, :, mid[d]:mid[d] + 1].broadcast_to(shape), ALU.subtract)
            last.then_inc(S.arg_done, 1)
            for d in range(2):
                b = chunked(gB, d)
                last = nc.vector.tensor_tensor(chunked(gM, d), b[:, :, edge[d]:edge[d] + 1].broadcast_to(shape), b, ALU.subtract)
            last.then_inc(S.arg_done, 1)

            tabs = tab.rearrange("p i s (t d) -> p i s t d", d=DH)
            for t in range(TILES):
                for i, (h0, n) in enumerate(((0, HEADS), (HEADS, KV_HEADS))):
                    src = raw[:, t, h0 * DH:(h0 + n) * DH].rearrange("p (h d) -> p h d", d=DH)
                    dst = rot[:, t, h0 * DH:(h0 + n) * DH].rearrange("p (h d) -> p h d", d=DH)
                    sw = swp[:, t, h0 * DH:(h0 + n) * DH].rearrange("p (h d) -> p h d", d=DH)
                    nc.vector.tensor_tensor(dst, src, tabs[:, i, 0, t:t + 1, :].broadcast_to([P, n, DH]), ALU.mult)
                    for f in range(2):
                        part = sw.rearrange("p h (a f d) -> p h a f d", a=2, f=2)[:, :, :, f, :]
                        other = src.rearrange("p h (a f d) -> p h a f d", a=2, f=2)[:, :, :, 1 - f, :]
                        table = tabs[:, i, 1, t:t + 1, :].rearrange("p o (a f d) -> p o a f d", a=2, f=2)[:, :, :, f, :]
                        last = nc.vector.tensor_tensor(part, other, table.broadcast_to([P, n, 2, DH // 4]), ALU.mult)
            step(last)
            step(nc.vector.tensor_tensor(rot, rot, swp, ALU.add))
            dve.wait_ge(S.hrstd_done, 1)
            nc.vector.tensor_tensor(rot.rearrange("p t (h d) -> p (t h) d", d=DH), rot.rearrange("p t (h d) -> p (t h) d", d=DH),
                                    stat[:, 28:48].rearrange("p (h o) -> p h o", o=1).broadcast_to([P, TILES * NH, DH]),
                                    ALU.mult).then_inc(S.rope_done, 1)

            q2, k2 = gqk[:, 0, :], gqk[:, 1, :]
            dve.wait_ge(S.gqk_sb, 2)

            def pairs(buf, d):
                return buf[:, 2 * d:2 * d + 2, :].rearrange("p g t -> p (g t)")

            dve.wait_ge(S.exp_done, 4)
            for d in range(2):
                nc.vector.tensor_tensor(pairs(gX, d), pairs(gX, d), q2, ALU.mult).then_inc(S.gla_ready, 1)
                nc.vector.tensor_tensor(pairs(gA, d), pairs(gA, d), k2, ALU.mult).then_inc(S.gla_ready, 1)
            dec = stat[:, 0:4 * CHUNKS]
            for d in range(2):
                last = nc.vector.tensor_copy(dec[:, 8 * d:8 * d + 8].rearrange("p (c o) -> p c o", o=1),
                                             chunked(gB, d)[:, :, edge[d]:edge[d] + 1])
            step(last)
            for d in range(2):
                nc.vector.tensor_tensor(pairs(gB, d), pairs(gB, d), q2, ALU.mult).then_inc(S.gla_ready, 1)
            k4 = k2.rearrange("p (g c i) -> p g c i", g=2, i=CHUNK)
            for d in range(2):
                last = nc.vector.tensor_tensor(kk[:, 2 * d:2 * d + 2, :, :].rearrange("p g s i -> p g s i")[:, :, 0:5:2, :],
                                               gM[:, 2 * d:2 * d + 2, :].rearrange("p g (c i) -> p g c i", i=CHUNK)[:, :, d:d + 3, :],
                                               k4[:, :, d:d + 3, :], ALU.mult)
            step(last)
            dec4 = dec.rearrange("p (d g c) -> p d g c", d=2, g=2)

            def carry(d, to, of, c):
                return nc.vector.tensor_tensor(kk[:, 2 * d:2 * d + 2, to, :], kk[:, 2 * d:2 * d + 2, of, :],
                                               dec4[:, d, :, c:c + 1].broadcast_to([P, 2, CHUNK]), ALU.mult)

            carry(0, 1, 0, 1)
            carry(0, 6, 2, 2)
            carry(1, 5, 2, 1)
            step(carry(1, 3, 4, 2))
            carry(0, 5, 1, 2)
            carry(1, 6, 3, 1).then_inc(S.kk_done, 1)

            for i, b in enumerate((5, 2, 5)):
                dve.wait_ge(S.qkT_ps, i + 1)
                n = 2 if i < 2 else 1
                nc.vector.tensor_copy(qkT[:, 2 * i:2 * i + n, :],
                                      bank[b][:, 0:n * SEQ].rearrange("p (b t) -> p b t", t=SEQ)).then_inc(S.qkT_sb, 1)

            def swish():
                dve.wait_ge(S.gr_exp, TILES)
                step(nc.vector.tensor_scalar(sg, sg, 1.0, None, ALU.add))
                step(nc.vector.reciprocal(sg, sg))
                for t in range(TILES):
                    last = nc.vector.tensor_tensor(sg[:, t, :], bank[3 + t][:, :], sg[:, t, :], ALU.mult)
                step(last)
                sg8 = sg.rearrange("p t (h d) -> p (t h) d", d=DV)
                nc.vector.tensor_tensor(sg8, sg8, head_g.rearrange("p (o d) -> p o d", o=1).broadcast_to([P, TILES * GLA_HEADS, DV]),
                                        ALU.mult).then_inc(S.sg_done, 1)

            def weights_out(hd):
                dve.wait_ge(S.probT_ps, hd + 1)
                if hd >= 2:
                    dve.wait_ge(S.oatt_ps, hd - 1)
                nc.vector.tensor_copy(probT[:, hd % 2, :], bank[6 + hd % 2][:, :]).then_inc(S.probT_sb, 1)

            for hd in range(HEADS):
                dve.wait_ge(S.score_ps, hd + 1)
                nm = stat[:, 96 + 2 * hd:98 + 2 * hd]
                step(nc.vector.tensor_reduce(nm, bank[(5, 2)[hd % 2]][:, :].rearrange("p (t s) -> p t s", s=SEQ), AX.X, ALU.max))
                nc.vector.tensor_scalar(nm, nm, -1.0, None, ALU.mult).then_inc(S.nmax_done, 1)
                if hd == 0:
                    swish()
            dve.wait_ge(S.prob_done, 2 * HEADS)
            sums = stat[:, 112:128]
            step(nc.vector.reciprocal(sums, sums))
            dve.wait_ge(S.oatt_ps, HEADS)
            for t in range(TILES):
                nc.vector.tensor_tensor(tok[:, t, GLA_V:D].rearrange("p (h d) -> p h d", d=DH),
                                        bank[t][:, :].rearrange("p (h d) -> p h d", d=DH),
                                        sums[:, t * HEADS:(t + 1) * HEADS].rearrange("p (h o) -> p h o", o=1)
                                        .broadcast_to([P, HEADS, DH]), ALU.mult).then_inc(S.oatt_sb, 1)

            for hd in range(GLA_HEADS):
                dve.wait_ge(S.mix_ps, hd + 1)
                if hd % 2:
                    step(nc.vector.tensor_copy(mix[hd], bank[2][:, :]))
                else:
                    dve.wait_ge(S.mix_sb, hd // 2 + 1)
                for par in range(2):
                    rows_ = slice(par * CHUNK, (par + 1) * CHUNK)
                    blocks = mix[hd].rearrange("p (s c i) -> p s c i", s=TILES, i=CHUNK)
                    for st in range(TILES):
                        last = nc.vector.copy_predicated(
                            blocks[rows_, st, 2 * st + par, :],
                            later_sb[rows_, :],
                            bank[3 + hd % 2][rows_, (hd // 2 * 2 + st) * CHUNK:(hd // 2 * 2 + st + 1) * CHUNK])
                last.then_inc(S.ogla_sb, 1)

            dve.wait_ge(S.ogla_sq, TILES)
            g8 = tok[:, :, 0:GLA_V].rearrange("p t (h d) -> p t h d", d=DV)
            for t in range(TILES):
                last = nc.vector.tensor_reduce(stat[:, 56 + 4 * t:60 + 4 * t], g8[:, t, :, :], AX.X, ALU.add)
            step(last)
            mean_eps(stat[:, 48:56], stat[:, 56:64], DV).then_inc(S.ogla_var, 1)
            dve.wait_ge(S.ogla_rstd, 1)
            dve.wait_ge(S.sg_done, 1)
            for t in range(TILES):
                last = nc.vector.tensor_tensor(g8[:, t, :, :], bank[6 + t][:, :].rearrange("p (h d) -> p h d", d=DV),
                                               stat[:, 56 + 4 * t:60 + 4 * t].rearrange("p (h o) -> p h o", o=1)
                                               .broadcast_to([P, GLA_HEADS, DV]), ALU.mult)
            step(last)
            for t in range(TILES):
                nc.vector.tensor_tensor(tok[:, t, 0:GLA_V], tok[:, t, 0:GLA_V], sg[:, t, :], ALU.mult)\
                    .then_inc(S.ogla_sb, 1)

            for i, b in ((0, 4), (2, 6)):
                dve.wait_ge(S.oT_ps, i + 1)
                k0 = 4 if i == 0 else 0
                nc.vector.tensor_copy(turned[:, k0:k0 + 4, 0:P], bank[b][:, :].rearrange("p (k t) -> p k t", t=P))\
                    .then_inc(S.oT_sb, 1)

            dve.wait_ge(S.h_ps, 1)
            for t in range(TILES):
                for nb in range(2):
                    last = nc.vector.tensor_tensor(h[:, t, nb * 512:(nb + 1) * 512], bank[2 * t + nb][:, :],
                                                   h[:, t, nb * 512:(nb + 1) * 512], ALU.add)
                last.then_inc(S.h_done, 1)
            for t in range(TILES):
                dve.wait_ge(S.hsq, t + 1)
                mean_eps(stat[:, 2 + t:3 + t], stat[:, t:t + 1], D).then_inc(S.var2, 1)
            dve.wait_ge(S.rstd2, 1)
            nc.vector.tensor_scalar(tok[:, 0, :], h[:, 0, :], stat[:, 4:5], None, ALU.mult).then_inc(S.n2_done, 1)
            for k in (0, 1, 4, 5):
                dve.wait_ge(S.n2T_ps, k // 2 + 1)
                nc.vector.tensor_scalar(turned[:, k, :], bank[4 + k // 2][:, (k % 2) * SEQ:(k % 2 + 1) * SEQ], ffn_g[:, k:k + 1], None,
                                        ALU.mult).then_inc(S.n2T_sb, 1)

            dve.wait_ge(S.logit_ps, 1)
            step(nc.vector.tensor_tensor(logit, bank[0][:, 0:TILES * EXPERTS].rearrange("p (t e) -> p t e", e=EXPERTS),
                                         router_b.rearrange("p (o e) -> p o e", o=1).broadcast_to([P, TILES, EXPERTS]), ALU.add))
            for t in range(TILES):
                last = nc.vector.max(top[:, t, :], logit[:, t, :])
            step(last)
            for t in range(TILES):
                last = nc.vector.tensor_scalar(stat[:, 6 + t:7 + t], top[:, t, 0:1], -1.0, None, ALU.mult)
            last.then_inc(S.top_done, 1)
            topu = topi.bitcast(U32).rearrange("p (t k) -> p t k", k=8)
            for t in range(TILES):
                last = nc.vector.max_index(topu[:, t, :], top[:, t, :], logit[:, t, :])
            step(last)
            step(nc.vector.tensor_copy(topf, topu))
            for t in range(TILES):
                last = nc.vector.tensor_tensor(hit[:, t, :].rearrange("p (k e) -> p k e", e=EXPERTS),
                                               iota[:, 0:EXPERTS].rearrange("p (o e) -> p o e", o=1).broadcast_to([P, TOP_K, EXPERTS]),
                                               topf[:, t, 0:TOP_K].rearrange("p (k o) -> p k o", o=1).broadcast_to([P, TOP_K, EXPERTS]),
                                               ALU.is_equal)
            step(last)
            for t in range(TILES):
                last = nc.vector.tensor_reduce(chosen[:, t, :], hit[:, t, :].rearrange("p (k e) -> p e k", e=EXPERTS), AX.X, ALU.add)
            last.then_inc(S.chosen_done, 1)
            dve.wait_ge(S.chosen_done, 1)
            dve.wait_ge(S.wexp_done, TILES)
            step(nc.vector.tensor_tensor(weight, weight, chosen, ALU.mult))
            step(nc.vector.tensor_reduce(stat[:, 8:10], weight, AX.X, ALU.add))
            step(nc.vector.reciprocal(stat[:, 10:12], stat[:, 8:10]))
            nc.vector.memset(rank_t, -1.0)
            step(nc.vector.memset(gate_t, 0.0))
            for t in range(TILES):
                for r in range(ROUNDS):
                    last = nc.vector.tensor_scalar(gate_t[:, t, r * EXPERTS:(r + 1) * EXPERTS], weight[:, t, :],
                                                   stat[:, 10 + t:11 + t], None, ALU.mult)
            last.then_inc(S.tables_done, 1)
            dve.wait_ge(S.rank_ps, 1)
            ranks = bank[1][:, 0:TILES * EXPERTS].rearrange("p (t e) -> p t e", e=EXPERTS)
            step(nc.vector.scalar_tensor_tensor(rank, ranks, 1.0, chosen, ALU.add, ALU.mult))
            for r in range(ROUNDS):
                last = nc.vector.tensor_scalar(rank_t[:, :, r * EXPERTS:(r + 1) * EXPERTS], rank, -1.0 - CAP * r, None, ALU.add)
            step(last)
            step(nc.vector.tensor_reduce(stat[0:1, 12:13], bank[1][0:1, 2 * EXPERTS:3 * EXPERTS], AX.X, ALU.max))
            for r in range(1, ROUNDS):
                last = nc.vector.tensor_scalar(stat[0:1, 12 + r:13 + r], stat[0:1, 12:13], CAP * r + 0.5, None, ALU.is_gt)
            step(last)
            step(nc.vector.tensor_reduce(stat[0:1, 16:17], stat[0:1, 13:12 + ROUNDS], AX.X, ALU.add))
            nc.vector.tensor_copy(extra[0:1, 0:1], stat[0:1, 16:17]).then_inc(S.extra_done, 1)
            dve.wait_ge(S.gateT_ps, 1)
            nc.vector.tensor_copy(gateT[0:EXPERTS, :], bank[7][0:EXPERTS, 0:SEQ]).then_inc(S.gateT_sb, 1)
            dve.wait_ge(S.extra_done, 1)
            rounds = dve.value_load(extra[0:1, 0:1], min_val=0, max_val=ROUNDS - 1)
            base = steps[0]

            def gather_mask(n):
                for t in range(TILES):
                    last = nc.vector.tensor_scalar(onehot[:, t, :], iota[:, 0:CAP], rank_t[:, t, bass.ds(n, 1)], None,
                                                   ALU.is_equal)
                last.then_inc(S.onehot_ready, 1)

            def gathered_out(n):
                dve.wait_ge(S.gathered, n + 1)
                nc.vector.tensor_tensor(xg.rearrange("p (k c) -> p k c", c=CAP), bank[6][:, :].rearrange("p (k c) -> p k c", c=CAP),
                                        ffn_g.rearrange("p (k o) -> p k o", o=1).broadcast_to([P, KD, CAP]), ALU.mult)\
                    .then_inc(S.xg_ready, 1)

            def expert(n):
                dve.wait_ge(S.gatedT_ps, n)
                for t in range(TILES):
                    last = nc.vector.tensor_scalar(gated[:, t, :], iota, rank_t[:, t, bass.ds(n, 1)],
                                                   gate_t[:, t, bass.ds(n, 1)], ALU.is_equal, ALU.mult)
                last.then_inc(S.gated_ready, 1)
                dve.wait_ge(S.gathered, n + 1)
                gather_mask(n + 1)
                dve.wait_ge(S.w1_done, n + 1)
                nc.vector.tensor_scalar(glu, bank[4][:, :], LIMIT, None, ALU.min).then_inc(S.glu_ready, 1)
                nc.vector.tensor_scalar(lin, bank[5][:, :], LIMIT, -LIMIT, ALU.min, ALU.max).then_inc(S.dve_step, 1)
                dve.wait_ge(S.dve_step, n * 2 + (base + 1))
                nc.vector.scalar_tensor_tensor(lin, lin, 1.0, glu, ALU.add, ALU.mult).then_inc(S.dve_step, 1)
                dve.wait_ge(S.dve_step, n * 2 + (base + 2))
                dve.wait_ge(S.sig_ready, n + 1)
                nc.vector.tensor_tensor(hid, lin, sig, ALU.mult).then_inc(S.hid_ready, 1)
                gathered_out(n + 1)
                dve.wait_ge(S.chunk_used, (n + 1) * PER_EXPERT)
                nc.vector.tensor_copy(res[:, 512:D], bank[5][:, :]).then_inc(S.out_v, 1)

            gather_mask(0)
            gathered_out(0)
            for n in range(UNROLL):
                expert(n)
            bodies = EXPERTS // UNROLL
            with dve.Fori(1, rounds * bodies + bodies) as it:
                for q in range(UNROLL):
                    expert(it * UNROLL + q)

            dve.wait_ge(S.combined, rounds * EXPERTS + EXPERTS)
            for t in range(TILES):
                for nb in range(2):
                    last = nc.vector.tensor_tensor(h[:, t, nb * 512:(nb + 1) * 512], bank[2 * t + nb][:, :],
                                                   h[:, t, nb * 512:(nb + 1) * 512], ALU.add)
                last.then_inc(S.y_done, 1)
            for t in range(TILES):
                dve.wait_ge(S.ysq, t + 1)
                mean_eps(stat[:, 2 + t:3 + t], stat[:, t:t + 1], D).then_inc(S.var3, 1)
            dve.wait_ge(S.fin_g_in, 16)
            for t in range(TILES):
                dve.wait_ge(S.rstd3, t + 1)
                nc.vector.scalar_tensor_tensor(tok[:, t, :], h[:, t, :], stat[:, 4 + t:5 + t], slot(0)[:, 0:D],
                                               ALU.mult, ALU.mult).then_inc(S.fin_done, 1)

        @block.tensor
        def _(pe):
            mm = nc.tensor.matmul
            pe.wait_ge(S.ident_in, 32)
            pe.wait_ge(S.n_done, 2)
            for pair in range(KD // 2):
                if pair >= 2:
                    pe.wait_ge(S.nT_v if pair == 2 else S.nT_a, 2)
                for k in (2 * pair, 2 * pair + 1):
                    for t in range(TILES):
                        o = (k % 2) * SEQ + t * P
                        last = nc.tensor.transpose(bank[6 + pair % 2][:, o:o + P], tok[:, t, k * P:(k + 1) * P], ident)
                last.then_inc(S.nT_ps, 1)

            def xT(k, t=None):
                return turned[:, k, :] if t is None else turned[:, k, t * P:(t + 1) * P]

            for k in range(KD):
                pe.wait_ge(win_in[k], 16)
                pe.wait_ge(*((S.nT_v, S.nT_v, S.nT_a, S.nT_a)[k % 4], (1, 2, 1, 2, 3, 4, 3, 4)[k]))
                a, z = k == 0, k == KD - 1

                def put(o, l, r, first):
                    return mm(o, l, r, start=a and first, stop=z, skip_group_check=True)

                w = w_in_sb[:, k, :]
                put(bank[2][0:2 * RANK, 0:SEQ], w[:, C_ZG:C_AQ], xT(k), True)
                for i, c0 in enumerate((C_GQ, C_GK)):
                    for pair in range(2):
                        put(bank[i][:, pair * SEQ:(pair + 1) * SEQ], w[:, c0 + pair * P:c0 + (pair + 1) * P], xT(k), pair == 0)
                for t in range(TILES):
                    put(bank[3 + t][:, :], xT(k, t), w[:, C_AQ:C_AK], True)
                    last = put(bank[5][:, t * SEQ:(t + 1) * SEQ], xT(k, t), w[:, C_AK:D_IN], t == 0)
            last.then_inc(S.pass1, 1)

            def gates():
                pe.wait_ge(S.zg_sb, 1)
                pe.wait_ge(S.gqk_sb, 2)
                pe.wait_ge(S.const_in, 16 * 7)
                for g in range(4):
                    last = mm(bank[g // 2][:, (g % 2) * SEQ:(g % 2 + 1) * SEQ], wg[0:2 * RANK, g * P:(g + 1) * P],
                              zg[0:2 * RANK, :], start=True, stop=True)
                last.then_inc(S.gates_ps, 1)

            for k in range(KD):
                for t in range(TILES):
                    last = mm(bank[6 + t][:, :], xT(k, t), w_in_sb[:, k, C_GV:C_GR], start=k == 0, stop=k == KD - 1)
                last.then_inc(S.pass2, 1)
                if k == 0:
                    gates()
            pe.wait_ge(S.raw_sb, 3 * TILES)
            for k in range(KD):
                for t in range(TILES):
                    last = mm(bank[3 + t][:, :], xT(k, t), w_in_sb[:, k, C_GR:C_ZG], start=k == 0, stop=k == KD - 1)
                last.then_inc(S.pass3, 1)

            pe.wait_ge(S.rope_done, 1)
            for b in range(5):
                if b == 4:
                    pe.wait_ge(S.qkT_sb, 1)
                for t in range(TILES):
                    o = (b % 2) * SEQ + t * P
                    last = nc.tensor.transpose(bank[(5, 2, 5)[b // 2]][:, o:o + P], rot[:, t, b * P:(b + 1) * P], ident)
                if b != 0 and b != 2:
                    last.then_inc(S.qkT_ps, 1)

            def scores(hd):
                kv, b = divmod(hd, HEADS // KV_HEADS)
                if hd == 0:
                    pe.wait_ge(S.qkT_sb, 3)
                else:
                    pe.wait_ge(S.prob_done, 2 * (hd - 1))
                rows_ = slice(kv * DH, (kv + 1) * DH)
                for t in range(TILES):
                    last = mm(bank[(5, 2)[hd % 2]][:, t * SEQ:(t + 1) * SEQ], qkT[rows_, b, t * P:(t + 1) * P],
                              qkT[rows_, 4, :], start=True, stop=True)
                last.then_inc(S.score_ps, 1)

            def turn_weights(hd):
                pe.wait_ge(S.prob_done, 2 * hd + 2)
                if hd >= 2:
                    pe.wait_ge(S.probT_sb, hd - 1)
                else:
                    pe.wait_ge(S.gv_sb, TILES)
                for st in range(TILES):
                    for t in range(TILES):
                        o = st * SEQ + t * P
                        s = t * SEQ + st * P
                        last = nc.tensor.transpose(bank[6 + hd % 2][:, o:o + P], prob[:, hd % 2, s:s + P], ident)
                last.then_inc(S.probT_ps, 1)

            def values(hd):
                kv = hd // (HEADS // KV_HEADS)
                pe.wait_ge(S.probT_sb, hd + 1)
                if hd == 0:
                    pe.wait_ge(S.gates_sb, 1)
                for t in range(TILES):
                    for st in range(TILES):
                        last = mm(bank[t][:, hd * DH:(hd + 1) * DH], probT[:, hd % 2, st * SEQ + t * P:st * SEQ + (t + 1) * P],
                                  av[:, st, kv * DH:(kv + 1) * DH], start=st == 0, stop=st == TILES - 1)
                last.then_inc(S.oatt_ps, 1)

            for i in range(HEADS + 2):
                if i < HEADS:
                    scores(i)
                if 1 <= i <= HEADS:
                    turn_weights(i - 1)
                if i >= 2:
                    values(i - 2)

            pe.wait_ge(S.gla_ready, 6)
            pe.wait_ge(S.kk_done, 1)
            pe.wait_ge(S.sg_done, 1)
            pe.wait_ge(S.prob_done, 2 * HEADS)
            for hd in range(GLA_HEADS):
                pair, par = divmod(hd, 2)
                rows_ = slice(par * DK, (par + 1) * DK)
                if hd >= 2:
                    pe.wait_ge(S.ogla_sb, hd - 1)
                bk = bank[(5, 2)[par]]

                def tokens(buf, d, c):
                    return buf[rows_, 2 * d + pair, c * CHUNK:(c + 1) * CHUNK]

                def place(st, lo, n, i):
                    return bk[lo:lo + n, st * SEQ + i * CHUNK:st * SEQ + (i + 1) * CHUNK]

                def old(d, at, n):
                    return kk[rows_, 2 * d + pair, at:at + n, :].rearrange("p s i -> p (s i)")

                for c in range(CHUNKS):
                    mm(place(c // 2, (c % 2) * CHUNK, CHUNK, c), tokens(gA, 0, c), tokens(gX, 0, c), start=True, stop=True)
                    mm(bank[3 + par][(c % 2) * CHUNK:(c % 2 + 1) * CHUNK, (pair * 2 + c // 2) * CHUNK:(pair * 2 + c // 2 + 1) * CHUNK],
                       tokens(gA, 1, c), tokens(gX, 1, c), start=True, stop=True)
                for st, lo, n, i, d, at in ((0, 0, 64, 1, 0, 0), (0, 0, 128, 2, 0, 1), (0, 0, 128, 3, 0, 5), (1, 0, 64, 3, 0, 4),
                                            (1, 64, 64, 2, 1, 4), (1, 0, 128, 1, 1, 2), (1, 0, 128, 0, 1, 5), (0, 64, 64, 0, 1, 0)):
                    last = mm(place(st, lo, n, i), old(d, at, n // CHUNK), tokens(gB, d, i), start=True, stop=True)
                last.then_inc(S.mix_ps, 1)
            pe.wait_ge(S.probT_sb, HEADS)
            for hd in range(GLA_HEADS):
                pe.wait_ge(S.ogla_sb, hd + 1)
                for t in range(TILES):
                    for st in range(TILES):
                        last = mm(bank[6 + t][:, hd * DV:(hd + 1) * DV], mix[hd][:, st * SEQ + t * P:st * SEQ + (t + 1) * P],
                                  gv[:, st, hd * DV:(hd + 1) * DV], start=st == 0, stop=st == TILES - 1)
            last.then_inc(S.ogla_ps, 1)

            def turn_heads(i, k0, t, b):
                for k in range(4):
                    last = nc.tensor.transpose(bank[b][:, k * P:(k + 1) * P], tok[:, t, (k0 + k) * P:(k0 + k + 1) * P], ident)
                last.then_inc(S.oT_ps, 1)

            def project(k0, first):
                for k in range(k0, k0 + 4):
                    for t in range(TILES):
                        for nb in range(2):
                            last = mm(bank[2 * t + nb][:, :], xT(k, t), w_out_sb[:, k, nb * 512:(nb + 1) * 512],
                                      start=first and k == k0, stop=not first and k == k0 + 3)
                return last

            pe.wait_ge(S.oatt_sb, TILES)
            turn_heads(0, 4, 0, 4)
            turn_heads(1, 4, 1, 5)
            pe.wait_ge(S.wout_in, 16)
            pe.wait_ge(S.oT_sb, 2)
            project(4, True)
            pe.wait_ge(S.ogla_sb, GLA_HEADS + TILES)
            turn_heads(2, 0, 0, 6)
            turn_heads(3, 0, 1, 7)
            pe.wait_ge(S.oT_sb, 4)
            project(0, False).then_inc(S.h_ps, 1)

            pe.wait_ge(S.n2_done, 2)
            for pair in range(KD // 2):
                for k in (2 * pair, 2 * pair + 1):
                    for t in range(TILES):
                        o = (k % 2) * SEQ + t * P
                        last = nc.tensor.transpose(bank[4 + pair][:, o:o + P], tok[:, t, k * P:(k + 1) * P], ident)
                last.then_inc(S.n2T_ps, 1)
            pe.wait_ge(S.n2T_sb, KD)
            for t in range(TILES):
                for k in range(KD):
                    last = mm(bank[0][:, t * EXPERTS:(t + 1) * EXPERTS], xT(k, t), wr_sb[:, k, :], start=k == 0, stop=k == KD - 1)
            last.then_inc(S.logit_ps, 1)
            pe.wait_ge(S.chosen_done, 1)
            mm(bank[1][:, 0:EXPERTS], before, chosen[:, 0, :], start=True, stop=True)
            mm(bank[1][:, EXPERTS:2 * EXPERTS], ones, chosen[:, 0, :], start=True, stop=False)
            mm(bank[1][:, EXPERTS:2 * EXPERTS], before, chosen[:, 1, :], start=False, stop=True)
            mm(bank[1][:, 2 * EXPERTS:3 * EXPERTS], ones, chosen[:, 0, :], start=True, stop=False)
            mm(bank[1][:, 2 * EXPERTS:3 * EXPERTS], ones, chosen[:, 1, :], start=False, stop=True).then_inc(S.rank_ps, 1)
            pe.wait_ge(S.tables_done, 1)
            for t in range(TILES):
                last = nc.tensor.transpose(bank[7][0:EXPERTS, t * P:(t + 1) * P], gate_t[:, t, 0:EXPERTS], ident)
            last.then_inc(S.gateT_ps, 1)
            pe.wait_ge(S.gateT_sb, 1)
            pe.wait_ge(S.extra_done, 1)
            for t in range(TILES):
                for nb in range(2):
                    mm(bank[2 * t + nb][:, :], gateT[0:EXPERTS, t * P:(t + 1) * P], b2_sb[:, nb * 512:(nb + 1) * 512],
                       start=True, stop=False, skip_group_check=True)
            rounds = pe.value_load(extra[0:1, 0:1], min_val=0, max_val=ROUNDS - 1)

            def gather(n):
                pe.wait_ge(S.onehot_ready, n + 1)
                pe.wait_ge(S.xg_ready, n)
                for k in range(KD):
                    for t in range(TILES):
                        last = mm(bank[6][:, k * CAP:(k + 1) * CAP], tok[:, t, k * P:(k + 1) * P], onehot[:, t, :],
                                  start=t == 0, stop=t == TILES - 1)
                last.then_inc(S.gathered, 1)

            def combine(n):
                for t in range(TILES):
                    for nb in range(2):
                        last = mm(bank[2 * t + nb][:, :], gatedT[:, t, :], res[:, nb * 512:(nb + 1) * 512],
                                  start=False, stop=False, skip_group_check=True)
                last.then_inc(S.combined, 1)

            def expert(n, q, it, first=False):
                loads = it * LOADS_PER_BODY
                pe.wait_ge(S.xg_ready, n + 1)
                pe.wait_ge(S.out_a, n)
                pe.wait_ge(S.out_v, n)
                for k in range(W1_CHUNKS):
                    c = q * PER_EXPERT + k
                    pe.wait_ge(slot_in[c % SLOTS], (loads + (c // SLOTS + 1)) * 16)
                    for j in range(GROUPS):
                        for g in range(2):
                            last = mm(bank[4 + g][j * CAP:(j + 1) * CAP, :], xg[:, k * CAP:(k + 1) * CAP],
                                      slot(c)[:, g * FF + j * FG:g * FF + (j + 1) * FG], start=k == 0, stop=False,
                                      skip_group_check=True)
                    last.then_inc(S.chunk_used, 1)
                pe.wait_ge(b1_in[q % 2], (it * (UNROLL // 2) + (q // 2 + 1)) * 16)
                for g in range(2):
                    last = mm(bank[4 + g][:, :], split_sb, b1_sb[0:GROUPS, q % 2, g * FG:(g + 1) * FG], start=False, stop=True,
                              skip_group_check=True)
                last.then_inc(S.w1_done, 1)
                if not first:
                    combine(n - 1)
                gather(n + 1)
                pe.wait_ge(S.gated_ready, n + 1)
                pe.wait_ge(S.hidT_sb, n)
                for t in range(TILES):
                    last = nc.tensor.transpose(bank[7][:, t * P:(t + 1) * P], gated[:, t, :], ident)
                last.then_inc(S.gatedT_ps, 1)
                pe.wait_ge(S.hid_ready, n + 1)
                pe.wait_ge(S.gatedT_sb, n + 1)
                for s in range(SUB):
                    last = nc.tensor.transpose(bank[7][:, s * P:(s + 1) * P], hid[:, s * P:(s + 1) * P], ident)
                last.then_inc(S.hidT_ps, 1)
                pe.wait_ge(S.hidT_sb, n + 1)
                for s in range(W2_CHUNKS):
                    c = q * PER_EXPERT + W1_CHUNKS + s
                    pe.wait_ge(slot_in[c % SLOTS], (loads + (c // SLOTS + 1)) * 16)
                    for j in range(GROUPS):
                        for nb in range(2):
                            last = mm(bank[4 + nb][j * CAP:(j + 1) * CAP, :], hidT[:, s, j * CAP:(j + 1) * CAP],
                                      w2_slot(c)[:, j, nb * 512:(nb + 1) * 512], start=s == 0, stop=s == SUB - 1,
                                      skip_group_check=True)
                    last.then_inc(S.chunk_used, 1)

            gather(0)
            for q in range(UNROLL):
                expert(q, q, 0, first=q == 0)
            bodies = EXPERTS // UNROLL
            with pe.Fori(1, rounds * bodies + bodies) as it:
                for q in range(UNROLL):
                    expert(it * UNROLL + q, q, it)
            pe.wait_ge(S.out_a, rounds * EXPERTS + EXPERTS)
            pe.wait_ge(S.out_v, rounds * EXPERTS + EXPERTS)
            combine(EXPERTS - 1)


def kernel(x, mix_norm_g, w_in, w_gate_f, b_gate_f, w_gate_b, b_gate_b, gla_head_g, q_norm_g, k_norm_g,
           w_out, ffn_norm_g, w_router, b_router, w1, b1, w2, b2, final_norm_g):
    import concourse.bacc as bacc
    from concourse.bass_utils import run_bass_kernel_spmd

    def by_partition(v):
        return np.asarray(v).reshape(-1, P).T

    gate_w = np.zeros((2 * RANK, 2 * GLA_QK), np.float32)
    gate_w[0:RANK, 0:GLA_QK] = np.asarray(w_gate_f)[0]
    gate_w[RANK:, GLA_QK:] = np.asarray(w_gate_b)[0]
    columns = np.concatenate([by_partition(v) for v in (mix_norm_g, ffn_norm_g, b_gate_f, b_gate_b)], 1)
    rows = np.concatenate([np.asarray(v).reshape(-1) for v in (q_norm_g, k_norm_g, gla_head_g, b_router)])
    consts = {k: np.concatenate(v, 1).astype(np.float32) for k, v in shape_constants().items()}
    i = np.arange(P)
    arrays = {
        "x": np.asarray(x)[0],
        "w_in": np.asarray(w_in)[0],
        "w_out": np.asarray(w_out)[0],
        "w_router": np.asarray(w_router)[0].reshape(KD, P, EXPERTS).transpose(1, 0, 2).reshape(P, KD * EXPERTS),
        "w1": np.asarray(w1)[0],
        "b1": np.asarray(b1)[0],
        "w2": np.asarray(w2)[0],
        "b2": np.asarray(b2)[0],
        "gate_w": gate_w,
        "columns": columns,
        "rows": np.broadcast_to(rows, (P, rows.size)),
        "final_g": np.broadcast_to(np.asarray(final_norm_g), (P, D)),
        "c_keep": consts["c_keep"],
        "c_front": consts["c_front"],
        "later": ((i % CHUNK)[:, None] > np.arange(CHUNK)[None, :]).astype(np.int32),
        "split": (i[None, :] // CAP == np.arange(GROUPS)[:, None]).astype(np.float32),
    }
    nc = bacc.Bacc("TRN2", target_bir_lowering=False, num_devices=1)
    feeds, aps = {}, {}
    for name, a in arrays.items():
        a = np.ascontiguousarray(a)
        feeds[f"in_{name}_dram"] = a
        aps[name] = nc.dram_tensor(f"in_{name}_dram", a.shape, mybir.dt.from_np(a.dtype), kind="ExternalInput").ap()
    aps["out"] = nc.dram_tensor("out_dram", (SEQ, D), F32, kind="ExternalOutput").ap()
    encoder_layer(nc, **aps)
    r = run_bass_kernel_spmd(nc, [feeds], core_ids=[0])
    return r.results[0]["out_dram"].reshape(1, SEQ, D)
```

```python
from contextlib import ExitStack

import numpy as np

import concourse.bass as bass
from concourse import mybir

F32 = mybir.dt.float32
I32 = mybir.dt.int32
U32 = mybir.dt.uint32
BF16 = mybir.dt.bfloat16
ALU = mybir.AluOpType
ACT = mybir.ActivationFunctionType
AX = mybir.AxisListType

P = 128
SEQ = 256
TILES = SEQ // P
D = 1024
KD = D // P
EPS = 1e-6
GRID_W = 64

GLA_HEADS, DK, DV, RANK, CHUNK = 4, 64, 128, 16, 64
GLA_NORMALIZER = 16.0
CHUNKS = SEQ // CHUNK
HEADS, KV_HEADS, DH = 8, 2, 64
ROPE_THETA = 10000.0
EXPERTS, TOP_K, FF = 32, 4, 1024
ALPHA, LIMIT = 1.702, 7.0

GLA_QK, GLA_V, ATT_Q, ATT_KV = GLA_HEADS * DK, GLA_HEADS * DV, HEADS * DH, KV_HEADS * DH
C_GQ = 0
C_GK = C_GQ + GLA_QK
C_GV = C_GK + GLA_QK
C_GR = C_GV + GLA_V
C_ZG = C_GR + GLA_V
C_AQ = C_ZG + 2 * RANK
C_AK = C_AQ + ATT_Q
C_AV = C_AK + ATT_KV
D_IN = C_AV + ATT_KV

CAP = 64
GROUPS = P // CAP
ROUNDS = SEQ // CAP
FG = FF // GROUPS
SUB = FG // P
SLOTS = 16
SLOT = 2048
W1_CHUNKS = KD
W2_CHUNKS = SUB
PER_EXPERT = W1_CHUNKS + W2_CHUNKS
UNROLL = 4
PER_BODY = UNROLL * PER_EXPERT
assert PER_BODY % SLOTS == 0 and EXPERTS % UNROLL == 0 and GROUPS * 1024 == SLOT
LOADS_PER_BODY = PER_BODY // SLOTS
TABLE = ROUNDS * EXPERTS + UNROLL
PARTS = 3


def shape_constants():
    p = np.arange(P)
    ident = np.eye(P)
    iota = np.tile(np.arange(CAP), (P, GROUPS))
    before = (p[:, None] < p[None, :]) * 1.0
    ones = np.ones((P, P))
    keep = np.tile((np.arange(2 * SEQ) % CHUNK != 0) * 1.0, (P, 1))
    half = DH // 4
    inv = ROPE_THETA ** (-np.arange(half, dtype=np.float32) / np.float32(half))
    token = np.arange(TILES)[None, :] * P + p[:, None]
    ang = np.stack([token // GRID_W, token % GRID_W], -1)[..., None].astype(np.float32) * inv.astype(np.float32)
    cos = np.cos(ang.astype(np.float32))
    sin = np.sin(ang.astype(np.float32))
    cos = np.stack([cos, cos], 3).reshape(P, TILES * DH)
    sin = np.stack([-sin, sin], 3).reshape(P, TILES * DH)
    return {
        "c_keep": [ident, iota, before, ones],
        "c_front": [keep, cos, sin],
    }


def encoder_layer(nc, x, w_in, w_out, w_router, w1, b1, w2, b2, gate_w, columns, rows, final_g,
                  c_keep, c_front, later, split, out):
    ctx = ExitStack()
    with ctx:
        def sb(name, shape, dt=F32):
            return ctx.enter_context(nc.sbuf_tensor(name, shape, dt))[tuple(slice(None) for _ in shape)]

        def sem(name):
            return ctx.enter_context(nc.semaphore(name))

        ring = sb("ring", [P, SLOTS * SLOT])
        h = sb("h", [P, TILES, D])
        tok = sb("tok", [P, TILES, D])
        ckeep = sb("ckeep", [P, 4 * P])
        ident, iota, before, ones = (ckeep[:, i * P:(i + 1) * P] for i in range(4))
        b2_sb = sb("b2_sb", [EXPERTS, D])
        split_sb = sb("split_sb", [GROUPS, P])
        wr_sb = sb("wr_sb", [P, KD, EXPERTS])
        col = sb("col", [P, 2 * KD + 4])
        mix_g, ffn_g, gate_b = col[:, 0:KD], col[:, KD:2 * KD], col[:, 2 * KD:2 * KD + 4]
        later_sb = sb("later_sb", [P, CHUNK], I32)
        stat = sb("stat", [P, 144])
        extra = sb("extra", [1, 4], I32)
        work = sb("work", [P, 13900])

        class Carve:

            def __init__(self, base, start=0):
                self.base, self.at = base, start

            def __call__(self, *shape):
                n = int(np.prod(shape))
                piece = self.base[:, self.at:self.at + n]
                self.at += n
                if len(shape) == 2:
                    piece = piece.rearrange("p (a b) -> p a b", b=shape[1])
                elif len(shape) == 3:
                    piece = piece.rearrange("p (a b c) -> p a b c", b=shape[1], c=shape[2])
                return piece

        front = Carve(work)
        turned = front(KD, SEQ)
        gqk = front(2, 2 * SEQ)
        zg = front(SEQ)
        wg = front(4 * P)
        cfront = front(2 * SEQ + 2 * TILES * DH)
        keep = cfront[:, 0:2 * SEQ]
        cos = cfront[:, 2 * SEQ:2 * SEQ + TILES * DH].rearrange("p (t d) -> p t d", d=DH)
        sin = cfront[:, 2 * SEQ + TILES * DH:2 * SEQ + 2 * TILES * DH].rearrange("p (t d) -> p t d", d=DH)
        QK = ATT_Q + ATT_KV
        at_raw = front.at
        raw = front(TILES, QK)
        at_rot = front.at
        rot = front(TILES, QK)
        swp = front(TILES, QK)
        tab = front(2, 2, TILES * DH)
        row = front(2 * DH + DV + EXPERTS)
        q_g, k_g, head_g, router_b = row[:, 0:DH], row[:, DH:2 * DH], row[:, 2 * DH:2 * DH + DV], row[:, 2 * DH + DV:]
        qkT = front(5, SEQ)
        av = front(TILES, ATT_KV)
        gv = front(TILES, GLA_V)
        at_sg = front.at
        sg = front(TILES, GLA_V)
        att2 = front(2, 2 * SEQ)
        assert front.at <= 13900
        reuse = Carve(work, at_raw)
        att01 = reuse(2, 2 * SEQ)
        reuse = Carve(work, at_sg)
        diag = reuse(SEQ)
        rms = reuse(SEQ)
        reuse = Carve(work, at_rot)
        prob = reuse(2, 2 * SEQ)
        probT = reuse(2, 2 * SEQ)
        mix = [att01[:, 0, :], att01[:, 1, :], att2[:, 0, :], att2[:, 1, :]]
        scratch = Carve(ring, 10 * SLOT)
        gA, gM, gB, gX = (scratch(4, SEQ) for _ in range(4))
        decayed = Carve(ring, KD * D_IN)
        kk = decayed(4, 7, CHUNK)
        assert decayed.at <= 10 * SLOT
        w_in_sb = ring[:, 0:KD * D_IN].rearrange("p (k n) -> p k n", n=D_IN)
        w_out_att = ring[:, 12 * SLOT:14 * SLOT].rearrange("p (k n) -> p k n", n=D)
        w_out_gla = ring[:, 14 * SLOT:16 * SLOT].rearrange("p (k n) -> p k n", n=D)

        back = Carve(work, KD * SEQ)
        logit = back(TILES, EXPERTS)
        top = back(TILES, 8)
        topi = back(TILES * 8)
        topf = back(TILES, 8)
        hit = back(TILES, TOP_K * EXPERTS)
        chosen = back(TILES, EXPERTS)
        weight = back(TILES, EXPERTS)
        rank = back(TILES, EXPERTS)
        rank_t = back(TILES, TABLE)
        gate_t = back(TILES, TABLE)
        gateT = back(SEQ)
        b1_sb = back(2, 2 * FG)
        onehot = back(TILES * CAP // 2).bitcast(BF16).rearrange("p (t c) -> p t c", c=CAP)
        parts = back(TILES * PARTS * D // 2).bitcast(BF16).rearrange("p (t i d) -> p t i d", i=PARTS, d=D)
        gated = back(TILES, P)
        gatedT = back(TILES, P)
        xg = back(KD * CAP)
        at_glu = back.at
        glu = back(FG)
        lin = back(FG)
        sig = back(FG)
        hid = back(FG)
        hidT = back(SUB, P)
        res = back(D // GROUPS)
        reuse = Carve(work, at_glu)
        left = reuse(TILES, D)
        assert back.at <= 13900

        bank = [ctx.enter_context(nc.psum_tensor(f"bank{i}", [P, 512], F32))[:, :] for i in range(8)]

        names = """x0_in x1_in ident_in col_in const_in w_out_att_in w_out_gla_in fin_g_in stored
            sq_done var_done rstd_done xT_ps xT_v xT_a diag_done rms_ps rms_sb pass1 pass2 pass3
            zg_sb gqk_sb raw_sb raw_sq hss_done hvar_done hrstd_done tab_done rope_done wr_done
            gates_ps gates_sb gabs gln arg_done exp_done gla_ready kk_done
            gv_sb gr_sig swish_ps sg_done qkT_ps qkT_sb
            score_ps nmax_done prob_done probT_ps probT_sb oatt_ps oatt_sb att_used
            mix_ps mix_sb mix_done ogla_ps ogla_sq ogla_var ogla_rstd ogla_sb
            attT_ps attT_v attT_a glaT_ps glaT_v glaT_a h_ps h_done hsq var2 rstd2 hT_ps hT_v hT_a
            n2_done part0 left1 part1 part2
            logit_ps top_done wexp_done chosen_done rank_ps tables_done gateT_ps gateT_sb extra_done
            onehot_ready gathered xg_ready w1_done glu_ready sig_ready hid_ready combined
            gated_ready gatedT_ps gatedT_sb hidT_ps hidT_sb res_ready chunk_used
            y_done ysq var3 rstd3 fin_done
            act_step dve_step pool_step""".split()
        S = type("Semaphores", (), {n: sem(n) for n in names})
        win_in = [sem(f"win_in{k}") for k in range(KD)]
        slot_in = [sem(f"slot_in{s}") for s in range(SLOTS)]
        b1_in = [sem(f"b1_in{i}") for i in range(2)]

        Y = (0, 1, 3, 4)
        block = ctx.enter_context(nc.Block())

        def slot(c):
            return ring[:, (c % SLOTS) * SLOT:(c % SLOTS + 1) * SLOT]

        def w2_slot(c):
            return slot(c).rearrange("p (j n) -> p j n", n=D)

        @block.sync
        def _(sp):
            sp.dma_start(h[:, 0, :], x[0:P, :]).then_inc(S.x0_in, 16)
            sp.dma_start(ckeep, c_keep).then_inc(S.ident_in, 16)
            sp.dma_start(h[:, 1, :], x[P:SEQ, :]).then_inc(S.x1_in, 16)
            sp.dma_start(col, columns).then_inc(S.col_in, 16)
            for k in range(KD):
                sp.dma_start(w_in_sb[:, k, :], w_in[k * P:(k + 1) * P, :]).then_inc(win_in[k], 16)
                if k == 2:
                    sp.dma_start(cfront, c_front).then_inc(S.const_in, 16)
                    sp.dma_start(row, rows).then_inc(S.const_in, 16)
                    sp.dma_start(wg[0:2 * RANK, :], gate_w).then_inc(S.const_in, 16)
            sp.dma_start(later_sb, later).then_inc(S.const_in, 16)
            sp.dma_start(wr_sb, w_router.rearrange("p (k e) -> p k e", e=EXPERTS)).then_inc(S.const_in, 16)
            sp.dma_start(split_sb, split).then_inc(S.const_in, 16)
            sp.dma_start(b2_sb, b2).then_inc(S.const_in, 16)
            sp.dma_start(w_out_att, w_out[GLA_V:D, :].rearrange("(k p) n -> p k n", p=P)).then_inc(S.w_out_att_in, 16)
            sp.dma_start(w_out_gla, w_out[0:GLA_V, :].rearrange("(k p) n -> p k n", p=P)).then_inc(S.w_out_gla_in, 16)

            def load(c, e, r):
                if r < W1_CHUNKS:
                    sp.dma_start(slot(c), w1[e, r * P:(r + 1) * P, :]).then_inc(slot_in[c % SLOTS], 16)
                else:
                    s = r - W1_CHUNKS
                    sp.dma_start(w2_slot(c), w2[e].rearrange("(j s p) n -> s p j n", j=GROUPS, p=P)[s])\
                        .then_inc(slot_in[c % SLOTS], 16)

            def load_b1(n, e):
                sp.dma_start(b1_sb[0:GROUPS, n % 2, :].rearrange("j (g f) -> j g f", g=2),
                             b1[e].rearrange("(g j f) -> j g f", g=2, j=GROUPS)).then_inc(b1_in[n % 2], 16)

            for c in range(SLOTS):
                if c < 9:
                    sp.wait_ge(S.pass3, min(KD, ((c + 1) * SLOT - 1) // D_IN + 1))
                elif c < 12:
                    sp.wait_ge(S.mix_ps, 2 * GLA_HEADS)
                elif c < 14:
                    sp.wait_ge(S.att_used, 1)
                else:
                    sp.wait_ge(S.h_ps, TILES)
                load(c, c // PER_EXPERT, c % PER_EXPERT)
            load_b1(0, 0)
            load_b1(1, 1)
            sp.wait_ge(S.extra_done, 1)

            rounds = sp.value_load(extra[0:1, 0:1], min_val=0, max_val=ROUNDS - 1)

            def refill(it, used, e):
                c = SLOTS + used
                q, r = divmod(c, PER_EXPERT)
                if r == 0:
                    sp.wait_ge(S.w1_done, it * UNROLL + (q - 1))
                    load_b1(q, e)
                sp.wait_ge(S.chunk_used, it * PER_BODY + (used + 1))
                load(c, e, r)

            bodies = EXPERTS // UNROLL
            with sp.Fori(0, rounds * bodies + (bodies - 1)) as it:
                for used in range(PER_BODY):
                    refill(it, used, (it * UNROLL + (SLOTS + used) // PER_EXPERT) % EXPERTS)
            last = rounds * bodies + (bodies - 1)
            for used in range(PER_BODY - SLOTS):
                refill(last, used, EXPERTS - UNROLL + (SLOTS + used) // PER_EXPERT)
            sp.wait_ge(S.chunk_used, last * PER_BODY + (PER_BODY - SLOTS + 1))
            sp.dma_start(slot(0)[:, 0:D], final_g).then_inc(S.fin_g_in, 16)
            for t in range(TILES):
                sp.wait_ge(S.fin_done, t + 1)
                sp.dma_start(out[t * P:(t + 1) * P, :], tok[:, t, :]).then_inc(S.stored, 16)
            sp.wait_ge(S.stored, 16 * TILES)

        @block.gpsimd
        def _(pool):
            minus_half = stat[:, 64:96]
            pool.memset(minus_half, -0.5).then_inc(S.pool_step, 1)
            pool.wait_ge(S.pool_step, 1)

            def rsqrt(to, of, n):
                return pool.tensor_tensor(to, of, minus_half[:, 0:n], ALU.pow)

            for t in range(TILES):
                pool.wait_ge(S.var_done, t + 1)
                rsqrt(stat[:, 4 + t:5 + t], stat[:, 2 + t:3 + t], 1).then_inc(S.rstd_done, 1)
            pool.wait_ge(S.const_in, 16 * 7)
            pool.wait_ge(S.col_in, 16)
            pool.tensor_tensor(wr_sb, wr_sb, ffn_g.rearrange("p (k o) -> p k o", o=1).broadcast_to([P, KD, EXPERTS]), ALU.mult)\
                .then_inc(S.wr_done, 1)
            pool.wait_ge(S.hvar_done, 1)
            rsqrt(stat[:, 28:48], stat[:, 8:28], 20).then_inc(S.hrstd_done, 1)
            pool.wait_ge(S.swish_ps, TILES)
            sg8 = sg.rearrange("p t (h d) -> p (t h) d", d=DV)
            pool.tensor_tensor(sg8, sg8, head_g.rearrange("p (o d) -> p o d", o=1).broadcast_to([P, TILES * GLA_HEADS, DV]),
                               ALU.mult).then_inc(S.sg_done, 1)
            pool.wait_ge(S.ogla_var, 1)
            rsqrt(stat[:, 56:64], stat[:, 48:56], 8).then_inc(S.ogla_rstd, 1)
            for t in range(TILES):
                pool.wait_ge(S.var2, t + 1)
                rsqrt(stat[:, 4 + t:5 + t], stat[:, 2 + t:3 + t], 1).then_inc(S.rstd2, 1)
            for t in range(TILES):
                pool.wait_ge(S.n2_done, t + 1)
                pool.wait_ge(S.part0, t + 1)
                pool.tensor_tensor(left[:, t, :], tok[:, t, :], parts[:, t, 0, :], ALU.subtract).then_inc(S.left1, 1)
            for t in range(TILES):
                pool.wait_ge(S.part1, t + 1)
                pool.tensor_tensor(parts[:, t, 2, :], left[:, t, :], parts[:, t, 1, :], ALU.subtract).then_inc(S.part2, 1)
            for t in range(TILES):
                pool.wait_ge(S.var3, t + 1)
                rsqrt(stat[:, 4 + t:5 + t], stat[:, 2 + t:3 + t], 1).then_inc(S.rstd3, 1)

        @block.scalar
        def _(act):
            act.wait_ge(S.x0_in, 16)
            nc.scalar.activation(rot.rearrange("p a b -> p (a b)")[:, 0:D], h[:, 0, :], ACT.Square,
                                 accum_out=stat[:, 0:1]).then_inc(S.sq_done, 1)
            act.wait_ge(S.col_in, 16)
            for k in (2, 3, 6, 7):
                act.wait_ge(S.xT_ps, k // 2 + 1)
                nc.scalar.activation(turned[:, k, :], bank[7][:, (k % 2) * SEQ:(k % 2 + 1) * SEQ], ACT.Copy,
                                     scale=mix_g[:, k:k + 1]).then_inc(S.xT_a, 1)
            act.wait_ge(S.rms_ps, 1)
            nc.scalar.activation(rms, bank[6][:, 0:SEQ], ACT.Copy).then_inc(S.rms_sb, 1)

            act.wait_ge(S.rstd_done, TILES)
            act.wait_ge(S.pass1, 1)
            for t in range(TILES):
                inv = stat[:, 4 + t:5 + t]
                nc.scalar.activation(raw[:, t, 0:ATT_Q].rearrange("p (b k d) -> p k b d", k=KV_HEADS, d=DH),
                                     bank[3 + t][:, :].rearrange("p (k b d) -> p k b d", k=KV_HEADS, d=DH), ACT.Copy,
                                     scale=inv).then_inc(S.raw_sb, 1)
            for t in range(TILES):
                inv = stat[:, 4 + t:5 + t]
                nc.scalar.activation(raw[:, t, ATT_Q:QK], bank[5][:, t * SEQ:t * SEQ + ATT_KV], ACT.Copy,
                                     scale=inv).then_inc(S.raw_sb, 1)
                nc.scalar.activation(av[:, t, :], bank[5][:, t * SEQ + ATT_KV:(t + 1) * SEQ], ACT.Copy,
                                     scale=inv).then_inc(S.raw_sb, 1)
            act.wait_ge(S.gates_sb, 1)
            nc.scalar.activation(gA, gM, ACT.Abs).then_inc(S.gabs, 1)
            act.wait_ge(S.gabs, 1)
            nc.scalar.activation(gA, gA, ACT.Exp, scale=-1.0).then_inc(S.gabs, 1)
            act.wait_ge(S.gabs, 2)
            nc.scalar.activation(gA, gA, ACT.Ln, bias=1.0).then_inc(S.gln, 1)
            act.wait_ge(S.raw_sb, 3 * TILES)
            nc.scalar.activation(rot, raw, ACT.Square).then_inc(S.raw_sq, 1)
            act.wait_ge(S.arg_done, 1)
            nc.scalar.activation(gX, gA, ACT.Exp, scale=1.0 / GLA_NORMALIZER).then_inc(S.exp_done, 1)
            act.wait_ge(S.exp_done, 1)
            nc.scalar.activation(gA, gA, ACT.Exp, scale=-1.0 / GLA_NORMALIZER).then_inc(S.exp_done, 1)
            act.wait_ge(S.arg_done, 2)
            nc.scalar.activation(gB, gB, ACT.Exp, scale=1.0 / GLA_NORMALIZER).then_inc(S.exp_done, 1)
            nc.scalar.activation(gM, gM, ACT.Exp, scale=1.0 / GLA_NORMALIZER).then_inc(S.exp_done, 1)
            act.wait_ge(S.pass2, KD)
            for t in range(TILES):
                nc.scalar.activation(gv[:, t, :], bank[6 + t][:, :], ACT.Copy, scale=stat[:, 4 + t:5 + t]).then_inc(S.gv_sb, 1)
            act.wait_ge(S.pass3, KD)
            for t in range(TILES):
                nc.scalar.activation(sg[:, t, :], bank[3 + t][:, :], ACT.Sigmoid, scale=stat[:, 4 + t:5 + t]).then_inc(S.gr_sig, 1)

            def weights_out(hd):
                act.wait_ge(S.probT_ps, hd + 1)
                if hd >= 2:
                    act.wait_ge(S.oatt_ps, hd - 1)
                nc.scalar.activation(probT[:, hd % 2, :], bank[6 + hd % 2][:, :], ACT.Copy).then_inc(S.probT_sb, 1)

            for hd in range(HEADS):
                if hd in (2, 6):
                    g = hd // 2 - 1
                    act.wait_ge(S.mix_ps, 2 * g + 2)
                    nc.scalar.activation(mix[g], bank[3][:, :], ACT.Copy).then_inc(S.mix_sb, 1)
                act.wait_ge(S.nmax_done, hd + 1)
                if hd >= 2:
                    act.wait_ge(S.probT_ps, hd - 1)
                for t in range(TILES):
                    nc.scalar.activation(prob[:, hd % 2, t * SEQ:(t + 1) * SEQ],
                                         bank[(5, 2)[hd % 2]][:, t * SEQ:(t + 1) * SEQ], ACT.Exp,
                                         bias=stat[:, 96 + 2 * hd + t:97 + 2 * hd + t],
                                         accum_out=stat[:, 112 + t * HEADS + hd:113 + t * HEADS + hd])\
                        .then_inc(S.prob_done, 1)
                if hd >= 1:
                    weights_out(hd - 1)
            weights_out(HEADS - 1)

            act.wait_ge(S.ogla_ps, 1)
            for t in range(TILES):
                nc.scalar.activation(tok[:, t, 0:GLA_V], bank[6 + t][:, :], ACT.Square).then_inc(S.ogla_sq, 1)
            for ready, done, k0 in ((S.attT_ps, S.attT_a, 4), (S.glaT_ps, S.glaT_a, 0)):
                act.wait_ge(ready, 2)
                nc.scalar.activation(turned[:, k0:k0 + 4, P:SEQ], bank[2][:, :].rearrange("p (k t) -> p k t", t=P),
                                     ACT.Copy).then_inc(done, 1)

            for t in range(TILES):
                act.wait_ge(S.h_done, 2 * t + 2)
                nc.scalar.activation(left[:, t, :], h[:, t, :], ACT.Square, accum_out=stat[:, t:t + 1]).then_inc(S.hsq, 1)
                act.wait_ge(S.hT_ps, 2 * t + 2)
                nc.scalar.activation(turned[:, 4:8, t * P:(t + 1) * P], bank[(2, 7)[t]][:, :].rearrange("p (k t) -> p k t", t=P),
                                     ACT.Copy).then_inc(S.hT_a, 1)
            for t in range(TILES):
                act.wait_ge(S.rstd2, t + 1)
                nc.scalar.activation(parts[:, t, 0, :], h[:, t, :], ACT.Copy, scale=stat[:, 4 + t:5 + t]).then_inc(S.part0, 1)
                nc.scalar.activation(tok[:, t, :], h[:, t, :], ACT.Copy, scale=stat[:, 4 + t:5 + t]).then_inc(S.n2_done, 1)
            for t in range(TILES):
                act.wait_ge(S.left1, t + 1)
                nc.scalar.activation(parts[:, t, 1, :], left[:, t, :], ACT.Copy).then_inc(S.part1, 1)
            act.wait_ge(S.top_done, 1)
            for t in range(TILES):
                nc.scalar.activation(weight[:, t, :], logit[:, t, :], ACT.Exp, bias=stat[:, 6 + t:7 + t])\
                    .then_inc(S.wexp_done, 1)

            def expert(n):
                act.wait_ge(S.glu_ready, n + 1)
                nc.scalar.activation(sig, glu, ACT.Sigmoid, scale=ALPHA).then_inc(S.sig_ready, 1)
                act.wait_ge(S.gatedT_ps, n + 1)
                nc.scalar.activation(gatedT, bank[7][:, 0:SEQ].rearrange("p (t q) -> p t q", q=P), ACT.Copy)\
                    .then_inc(S.gatedT_sb, 1)
                act.wait_ge(S.hidT_ps, n + 1)
                nc.scalar.activation(hidT, bank[7][:, :].rearrange("p (s q) -> p s q", q=P), ACT.Copy)\
                    .then_inc(S.hidT_sb, 1)
                act.wait_ge(S.chunk_used, (n + 1) * PER_EXPERT)
                nc.scalar.activation(res, bank[2][:, :], ACT.Copy).then_inc(S.res_ready, 1)

            for n in range(UNROLL):
                expert(n)
            bodies = EXPERTS // UNROLL
            act.wait_ge(S.extra_done, 1)
            rounds = act.value_load(extra[0:1, 0:1], min_val=0, max_val=ROUNDS - 1)
            with act.Fori(1, rounds * bodies + bodies) as it:
                for q in range(UNROLL):
                    expert(it * UNROLL + q)

            for t in range(TILES):
                act.wait_ge(S.y_done, t + 1)
                nc.scalar.activation(tok[:, t, :], h[:, t, :], ACT.Square,
                                     accum_out=stat[:, t:t + 1]).then_inc(S.ysq, 1)

        @block.vector
        def _(dve):
            steps = [0]

            def step(ins):
                steps[0] += 1
                ins.then_inc(S.dve_step, 1)
                dve.wait_ge(S.dve_step, steps[0])

            def mean_eps(out_, in_, n):
                return nc.vector.tensor_scalar(out_, in_, 1.0 / n, EPS, ALU.mult, ALU.add)

            dve.wait_ge(S.x1_in, 16)
            step(nc.vector.scalar_tensor_tensor(swp.rearrange("p a b -> p (a b)")[:, 0:D], h[:, 1, :], 1.0, h[:, 1, :],
                                                ALU.mult, ALU.mult, accum_out=stat[:, 1:2]))
            dve.wait_ge(S.sq_done, 1)
            for t in range(TILES):
                mean_eps(stat[:, 2 + t:3 + t], stat[:, t:t + 1], D).then_inc(S.var_done, 1)
            dve.wait_ge(S.col_in, 16)
            for k in (0, 1, 4, 5):
                dve.wait_ge(S.xT_ps, k // 2 + 1)
                nc.vector.tensor_scalar(turned[:, k, :], bank[6][:, (k % 2) * SEQ:(k % 2 + 1) * SEQ], mix_g[:, k:k + 1], None,
                                        ALU.mult).then_inc(S.xT_v, 1)
            dve.wait_ge(S.rstd_done, TILES)
            dve.wait_ge(S.ident_in, 16)
            for t in range(TILES):
                last = nc.vector.tensor_scalar(diag[:, t * P:(t + 1) * P], ident, stat[:, 4 + t:5 + t], None, ALU.mult)
            last.then_inc(S.diag_done, 1)
            dve.wait_ge(S.const_in, 16 * 7)
            for i, g in enumerate((q_g, k_g)):
                scale = DH ** -0.5 if i == 0 else 1.0
                for t in range(TILES):
                    nc.vector.scalar_tensor_tensor(tab[:, i, 0, t * DH:(t + 1) * DH], cos[:, t, :], scale, g,
                                                   ALU.mult, ALU.mult)
                    gs = g.rearrange("p (a f d) -> p a f d", a=2, f=2)
                    for f in range(2):
                        last = nc.vector.scalar_tensor_tensor(
                            tab[:, i, 1, t * DH:(t + 1) * DH].rearrange("p (a f d) -> p a f d", a=2, f=2)[:, :, f, :],
                            sin[:, t, :].rearrange("p (a f d) -> p a f d", a=2, f=2)[:, :, f, :], scale,
                            gs[:, :, 1 - f, :], ALU.mult, ALU.mult)
            step(last)

            dve.wait_ge(S.pass1, 1)
            dve.wait_ge(S.rms_sb, 1)
            nc.vector.tensor_tensor(zg[0:2 * RANK, :], bank[2][0:2 * RANK, 0:SEQ], rms[0:2 * RANK, :], ALU.mult).then_inc(S.zg_sb, 1)
            rms2 = rms.rearrange("p (o t) -> p o t", o=1).broadcast_to([P, 2, SEQ])
            for i, scale in enumerate((DK ** -0.5, 1.0)):
                nc.vector.scalar_tensor_tensor(gqk[:, i, :].rearrange("p (g t) -> p g t", g=2),
                                               bank[i][:, :].rearrange("p (g t) -> p g t", g=2), scale, rms2,
                                               ALU.mult, ALU.mult).then_inc(S.gqk_sb, 1)
            dve.wait_ge(S.gates_ps, 1)
            for g in range(4):
                last = nc.vector.tensor_scalar(gM[:, g, :], bank[g // 2][:, (g % 2) * SEQ:(g % 2 + 1) * SEQ],
                                               gate_b[:, g:g + 1], None, ALU.add)
            last.then_inc(S.gates_sb, 1)
            NH = HEADS + KV_HEADS
            dve.wait_ge(S.gln, 1)
            step(nc.vector.scalar_tensor_tensor(gM, gM, 0.0, gA, ALU.min, ALU.subtract))
            flat = [t.rearrange("p g t -> p (g t)") for t in (gM, gB, gA)]
            half = 2 * SEQ
            nc.vector.tensor_tensor_scan(flat[1][:, 0:half], keep, flat[0][:, 0:half], 0.0, ALU.mult, ALU.add)
            step(nc.vector.tensor_tensor_scan(flat[1][:, 2 * half - 1:half - 1:-1], keep, flat[0][:, 2 * half - 1:half - 1:-1],
                                              0.0, ALU.mult, ALU.add))

            def chunked(buf, direction):
                return buf[:, 2 * direction:2 * direction + 2, :].rearrange("p g (c i) -> p (g c) i", i=CHUNK)

            mid = (CHUNK // 2 - 1, CHUNK // 2)
            edge = (CHUNK - 1, 0)
            shape = [P, 2 * CHUNKS, CHUNK]
            for d in range(2):
                b = chunked(gB, d)
                last = nc.vector.tensor_tensor(chunked(gA, d), b, b[:, :, mid[d]:mid[d] + 1].broadcast_to(shape), ALU.subtract)
            last.then_inc(S.arg_done, 1)
            for d in range(2):
                b = chunked(gB, d)
                last = nc.vector.tensor_tensor(chunked(gM, d), b[:, :, edge[d]:edge[d] + 1].broadcast_to(shape), b, ALU.subtract)
            last.then_inc(S.arg_done, 1)

            dve.wait_ge(S.raw_sq, 1)
            step(nc.vector.tensor_reduce(stat[:, 28:48], rot.rearrange("p t (h d) -> p (t h) d", d=DH), AX.X, ALU.add))
            mean_eps(stat[:, 8:28], stat[:, 28:48], DH).then_inc(S.hvar_done, 1)
            tabs = tab.rearrange("p i s (t d) -> p i s t d", d=DH)
            for t in range(TILES):
                for i, (h0, n) in enumerate(((0, HEADS), (HEADS, KV_HEADS))):
                    src = raw[:, t, h0 * DH:(h0 + n) * DH].rearrange("p (h d) -> p h d", d=DH)
                    dst = rot[:, t, h0 * DH:(h0 + n) * DH].rearrange("p (h d) -> p h d", d=DH)
                    sw = swp[:, t, h0 * DH:(h0 + n) * DH].rearrange("p (h d) -> p h d", d=DH)
                    nc.vector.tensor_tensor(dst, src, tabs[:, i, 0, t:t + 1, :].broadcast_to([P, n, DH]), ALU.mult)
                    for f in range(2):
                        part = sw.rearrange("p h (a f d) -> p h a f d", a=2, f=2)[:, :, :, f, :]
                        other = src.rearrange("p h (a f d) -> p h a f d", a=2, f=2)[:, :, :, 1 - f, :]
                        table = tabs[:, i, 1, t:t + 1, :].rearrange("p o (a f d) -> p o a f d", a=2, f=2)[:, :, :, f, :]
                        last = nc.vector.tensor_tensor(part, other, table.broadcast_to([P, n, 2, DH // 4]), ALU.mult)
            step(last)
            step(nc.vector.tensor_tensor(rot, rot, swp, ALU.add))
            dve.wait_ge(S.hrstd_done, 1)
            nc.vector.tensor_tensor(rot.rearrange("p t (h d) -> p (t h) d", d=DH), rot.rearrange("p t (h d) -> p (t h) d", d=DH),
                                    stat[:, 28:48].rearrange("p (h o) -> p h o", o=1).broadcast_to([P, TILES * NH, DH]),
                                    ALU.mult).then_inc(S.rope_done, 1)

            q2, k2 = gqk[:, 0, :], gqk[:, 1, :]
            dve.wait_ge(S.gqk_sb, 2)

            def pairs(buf, d):
                return buf[:, 2 * d:2 * d + 2, :].rearrange("p g t -> p (g t)")

            dve.wait_ge(S.exp_done, 4)
            for d in range(2):
                nc.vector.tensor_tensor(pairs(gX, d), pairs(gX, d), q2, ALU.mult).then_inc(S.gla_ready, 1)
                nc.vector.tensor_tensor(pairs(gA, d), pairs(gA, d), k2, ALU.mult).then_inc(S.gla_ready, 1)
            dec = stat[:, 128:128 + 4 * CHUNKS]
            for d in range(2):
                last = nc.vector.tensor_copy(dec[:, 8 * d:8 * d + 8].rearrange("p (c o) -> p c o", o=1),
                                             chunked(gB, d)[:, :, edge[d]:edge[d] + 1])
            step(last)
            for d in range(2):
                nc.vector.tensor_tensor(pairs(gB, d), pairs(gB, d), q2, ALU.mult).then_inc(S.gla_ready, 1)
            k4 = k2.rearrange("p (g c i) -> p g c i", g=2, i=CHUNK)
            for d in range(2):
                last = nc.vector.tensor_tensor(kk[:, 2 * d:2 * d + 2, :, :].rearrange("p g s i -> p g s i")[:, :, 0:5:2, :],
                                               gM[:, 2 * d:2 * d + 2, :].rearrange("p g (c i) -> p g c i", i=CHUNK)[:, :, d:d + 3, :],
                                               k4[:, :, d:d + 3, :], ALU.mult)
            step(last)
            dec4 = dec.rearrange("p (d g c) -> p d g c", d=2, g=2)

            def carry(d, to, of, c):
                return nc.vector.tensor_tensor(kk[:, 2 * d:2 * d + 2, to, :], kk[:, 2 * d:2 * d + 2, of, :],
                                               dec4[:, d, :, c:c + 1].broadcast_to([P, 2, CHUNK]), ALU.mult)

            carry(0, 1, 0, 1)
            carry(0, 6, 2, 2)
            carry(1, 5, 2, 1)
            step(carry(1, 3, 4, 2))
            carry(0, 5, 1, 2)
            carry(1, 6, 3, 1).then_inc(S.kk_done, 1)

            for i, b in enumerate((5, 2, 5)):
                dve.wait_ge(S.qkT_ps, i + 1)
                n = 2 if i < 2 else 1
                nc.vector.tensor_copy(qkT[:, 2 * i:2 * i + n, :],
                                      bank[b][:, 0:n * SEQ].rearrange("p (b t) -> p b t", t=SEQ)).then_inc(S.qkT_sb, 1)

            dve.wait_ge(S.gr_sig, TILES)
            for t in range(TILES):
                nc.vector.scalar_tensor_tensor(sg[:, t, :], bank[3 + t][:, :], stat[:, 4 + t:5 + t], sg[:, t, :],
                                               ALU.mult, ALU.mult).then_inc(S.swish_ps, 1)

            def gla_scores(hd):
                dve.wait_ge(S.mix_ps, 2 * hd + 2)
                if hd % 2:
                    step(nc.vector.tensor_copy(mix[hd], bank[3][:, :]))
                else:
                    dve.wait_ge(S.mix_sb, hd // 2 + 1)
                for par in range(2):
                    rows_ = slice(par * CHUNK, (par + 1) * CHUNK)
                    blocks = mix[hd].rearrange("p (s c i) -> p s c i", s=TILES, i=CHUNK)
                    for st in range(TILES):
                        last = nc.vector.copy_predicated(blocks[rows_, st, 2 * st + par, :], later_sb[rows_, :],
                                                         bank[4][rows_, st * CHUNK:(st + 1) * CHUNK])
                last.then_inc(S.mix_done, 1)

            for hd in range(HEADS):
                if hd >= 2 and hd % 2 == 0:
                    gla_scores(hd // 2 - 1)
                dve.wait_ge(S.score_ps, hd + 1)
                nm = stat[:, 96 + 2 * hd:98 + 2 * hd]
                step(nc.vector.tensor_reduce(nm, bank[(5, 2)[hd % 2]][:, :].rearrange("p (t s) -> p t s", s=SEQ), AX.X, ALU.max))
                nc.vector.tensor_scalar(nm, nm, -1.0, None, ALU.mult).then_inc(S.nmax_done, 1)
            gla_scores(GLA_HEADS - 1)
            dve.wait_ge(S.prob_done, 2 * HEADS)
            sums = stat[:, 112:128]
            step(nc.vector.reciprocal(sums, sums))
            dve.wait_ge(S.oatt_ps, HEADS)
            for t in range(TILES):
                nc.vector.tensor_tensor(tok[:, t, GLA_V:D].rearrange("p (h d) -> p h d", d=DH),
                                        bank[t][:, :].rearrange("p (h d) -> p h d", d=DH),
                                        sums[:, t * HEADS:(t + 1) * HEADS].rearrange("p (h o) -> p h o", o=1)
                                        .broadcast_to([P, HEADS, DH]), ALU.mult).then_inc(S.oatt_sb, 1)
            dve.wait_ge(S.attT_ps, 1)
            nc.vector.tensor_copy(turned[:, 4:8, 0:P], bank[5][:, :].rearrange("p (k t) -> p k t", t=P)).then_inc(S.attT_v, 1)

            dve.wait_ge(S.ogla_sq, TILES)
            g8 = tok[:, :, 0:GLA_V].rearrange("p t (h d) -> p t h d", d=DV)
            for t in range(TILES):
                last = nc.vector.tensor_reduce(stat[:, 56 + 4 * t:60 + 4 * t], g8[:, t, :, :], AX.X, ALU.add)
            step(last)
            mean_eps(stat[:, 48:56], stat[:, 56:64], DV).then_inc(S.ogla_var, 1)
            dve.wait_ge(S.ogla_rstd, 1)
            dve.wait_ge(S.sg_done, 1)
            for t in range(TILES):
                last = nc.vector.tensor_tensor(g8[:, t, :, :], bank[6 + t][:, :].rearrange("p (h d) -> p h d", d=DV),
                                               stat[:, 56 + 4 * t:60 + 4 * t].rearrange("p (h o) -> p h o", o=1)
                                               .broadcast_to([P, GLA_HEADS, DV]), ALU.mult)
            step(last)
            for t in range(TILES):
                nc.vector.tensor_tensor(tok[:, t, 0:GLA_V], tok[:, t, 0:GLA_V], sg[:, t, :], ALU.mult)\
                    .then_inc(S.ogla_sb, 1)
            dve.wait_ge(S.glaT_ps, 1)
            nc.vector.tensor_copy(turned[:, 0:4, 0:P], bank[5][:, :].rearrange("p (k t) -> p k t", t=P)).then_inc(S.glaT_v, 1)

            for t in range(TILES):
                dve.wait_ge(S.h_ps, t + 1)
                for nb in range(2):
                    nc.vector.tensor_tensor(h[:, t, nb * 512:(nb + 1) * 512], bank[Y[2 * t + nb]][:, :],
                                            h[:, t, nb * 512:(nb + 1) * 512], ALU.add).then_inc(S.h_done, 1)
                dve.wait_ge(S.hT_ps, 2 * t + 1)
                nc.vector.tensor_copy(turned[:, 0:4, t * P:(t + 1) * P], bank[(5, 6)[t]][:, :].rearrange("p (k t) -> p k t", t=P))\
                    .then_inc(S.hT_v, 1)
                dve.wait_ge(S.hsq, t + 1)
                mean_eps(stat[:, 2 + t:3 + t], stat[:, t:t + 1], D).then_inc(S.var2, 1)

            dve.wait_ge(S.logit_ps, 1)
            dve.wait_ge(S.rstd2, TILES)
            for t in range(TILES):
                last = nc.vector.scalar_tensor_tensor(logit[:, t, :], bank[5][:, t * EXPERTS:(t + 1) * EXPERTS],
                                                      stat[:, 4 + t:5 + t], router_b, ALU.mult, ALU.add)
            step(last)
            for t in range(TILES):
                last = nc.vector.max(top[:, t, :], logit[:, t, :])
            step(last)
            for t in range(TILES):
                last = nc.vector.tensor_scalar(stat[:, 6 + t:7 + t], top[:, t, 0:1], -1.0, None, ALU.mult)
            last.then_inc(S.top_done, 1)
            topu = topi.bitcast(U32).rearrange("p (t k) -> p t k", k=8)
            for t in range(TILES):
                last = nc.vector.max_index(topu[:, t, :], top[:, t, :], logit[:, t, :])
            step(last)
            step(nc.vector.tensor_copy(topf, topu))
            for t in range(TILES):
                last = nc.vector.tensor_tensor(hit[:, t, :].rearrange("p (k e) -> p k e", e=EXPERTS),
                                               iota[:, 0:EXPERTS].rearrange("p (o e) -> p o e", o=1).broadcast_to([P, TOP_K, EXPERTS]),
                                               topf[:, t, 0:TOP_K].rearrange("p (k o) -> p k o", o=1).broadcast_to([P, TOP_K, EXPERTS]),
                                               ALU.is_equal)
            step(last)
            for t in range(TILES):
                last = nc.vector.tensor_reduce(chosen[:, t, :], hit[:, t, :].rearrange("p (k e) -> p e k", e=EXPERTS), AX.X, ALU.add)
            last.then_inc(S.chosen_done, 1)
            step(nc.vector.memset(rank_t, -1.0))
            dve.wait_ge(S.rank_ps, 1)
            ranks = bank[2][:, 0:TILES * EXPERTS].rearrange("p (t e) -> p t e", e=EXPERTS)
            step(nc.vector.scalar_tensor_tensor(rank, ranks, 1.0, chosen, ALU.add, ALU.mult))
            step(nc.vector.tensor_scalar(rank_t[:, :, 0:EXPERTS], rank, -1.0, None, ALU.add))

            def tables():
                dve.wait_ge(S.wexp_done, TILES)
                step(nc.vector.tensor_tensor(weight, weight, chosen, ALU.mult))
                step(nc.vector.tensor_reduce(stat[:, 8:10], weight, AX.X, ALU.add))
                step(nc.vector.reciprocal(stat[:, 10:12], stat[:, 8:10]))
                step(nc.vector.memset(gate_t, 0.0))
                for t in range(TILES):
                    for r in range(ROUNDS):
                        last = nc.vector.tensor_scalar(gate_t[:, t, r * EXPERTS:(r + 1) * EXPERTS], weight[:, t, :],
                                                       stat[:, 10 + t:11 + t], None, ALU.mult)
                last.then_inc(S.tables_done, 1)
                for r in range(1, ROUNDS):
                    last = nc.vector.tensor_scalar(rank_t[:, :, r * EXPERTS:(r + 1) * EXPERTS], rank, -1.0 - CAP * r, None, ALU.add)
                step(last)
                step(nc.vector.tensor_reduce(stat[0:1, 12:13], bank[2][0:1, 2 * EXPERTS:3 * EXPERTS], AX.X, ALU.max))
                for r in range(1, ROUNDS):
                    last = nc.vector.tensor_scalar(stat[0:1, 12 + r:13 + r], stat[0:1, 12:13], CAP * r + 0.5, None, ALU.is_gt)
                step(last)
                step(nc.vector.tensor_reduce(stat[0:1, 16:17], stat[0:1, 13:12 + ROUNDS], AX.X, ALU.add))
                nc.vector.tensor_copy(extra[0:1, 0:1], stat[0:1, 16:17]).then_inc(S.extra_done, 1)
                dve.wait_ge(S.tables_done, 1)

            def gather_mask(n):
                for t in range(TILES):
                    last = nc.vector.tensor_scalar(onehot[:, t, :], iota[:, 0:CAP], rank_t[:, t, bass.ds(n, 1)], None,
                                                   ALU.is_equal)
                last.then_inc(S.onehot_ready, 1)

            def gathered_out(n):
                dve.wait_ge(S.gathered, n + 1)
                nc.vector.tensor_tensor(xg.rearrange("p (k c) -> p k c", c=CAP), bank[6][:, :].rearrange("p (k c) -> p k c", c=CAP),
                                        ffn_g.rearrange("p (k o) -> p k o", o=1).broadcast_to([P, KD, CAP]), ALU.mult)\
                    .then_inc(S.xg_ready, 1)

            def expert(n):
                dve.wait_ge(S.gatedT_ps, n)
                for t in range(TILES):
                    last = nc.vector.tensor_scalar(gated[:, t, :], iota, rank_t[:, t, bass.ds(n, 1)],
                                                   gate_t[:, t, bass.ds(n, 1)], ALU.is_equal, ALU.mult)
                last.then_inc(S.gated_ready, 1)
                dve.wait_ge(S.gathered, n + 1)
                gather_mask(n + 1)
                dve.wait_ge(S.w1_done, n + 1)
                nc.vector.tensor_scalar(glu, bank[2][:, :], LIMIT, None, ALU.min).then_inc(S.glu_ready, 1)
                nc.vector.tensor_scalar(lin, bank[5][:, :], LIMIT, -LIMIT, ALU.min, ALU.max).then_inc(S.dve_step, 1)
                dve.wait_ge(S.dve_step, n * 2 + (base + 1))
                nc.vector.scalar_tensor_tensor(lin, lin, 1.0, glu, ALU.add, ALU.mult).then_inc(S.dve_step, 1)
                dve.wait_ge(S.dve_step, n * 2 + (base + 2))
                dve.wait_ge(S.sig_ready, n + 1)
                nc.vector.tensor_tensor(hid, lin, sig, ALU.mult).then_inc(S.hid_ready, 1)
                gathered_out(n + 1)

            gather_mask(0)
            tables()
            gathered_out(0)
            dve.wait_ge(S.gateT_ps, 1)
            nc.vector.tensor_copy(gateT[0:EXPERTS, :], bank[7][0:EXPERTS, 0:SEQ]).then_inc(S.gateT_sb, 1)
            base = steps[0]
            for n in range(UNROLL):
                expert(n)
            bodies = EXPERTS // UNROLL
            dve.wait_ge(S.extra_done, 1)
            rounds = dve.value_load(extra[0:1, 0:1], min_val=0, max_val=ROUNDS - 1)
            with dve.Fori(1, rounds * bodies + bodies) as it:
                for q in range(UNROLL):
                    expert(it * UNROLL + q)

            for t in range(TILES):
                dve.wait_ge(S.combined, rounds * EXPERTS + (EXPERTS + t))
                for nb in range(2):
                    last = nc.vector.tensor_tensor(h[:, t, nb * 512:(nb + 1) * 512], bank[Y[2 * t + nb]][:, :],
                                                   h[:, t, nb * 512:(nb + 1) * 512], ALU.add)
                last.then_inc(S.y_done, 1)
            dve.wait_ge(S.fin_g_in, 16)
            for t in range(TILES):
                dve.wait_ge(S.ysq, t + 1)
                mean_eps(stat[:, 2 + t:3 + t], stat[:, t:t + 1], D).then_inc(S.var3, 1)
            for t in range(TILES):
                dve.wait_ge(S.rstd3, t + 1)
                nc.vector.scalar_tensor_tensor(tok[:, t, :], h[:, t, :], stat[:, 4 + t:5 + t], slot(0)[:, 0:D],
                                               ALU.mult, ALU.mult).then_inc(S.fin_done, 1)

        @block.tensor
        def _(pe):
            mm = nc.tensor.matmul
            pe.wait_ge(S.ident_in, 16)
            pe.wait_ge(S.x0_in, 16)
            pe.wait_ge(S.x1_in, 16)
            for pair in range(KD // 2):
                if pair >= 2:
                    pe.wait_ge(S.xT_v if pair == 2 else S.xT_a, 2)
                for k in (2 * pair, 2 * pair + 1):
                    for t in range(TILES):
                        o = (k % 2) * SEQ + t * P
                        last = nc.tensor.transpose(bank[6 + pair % 2][:, o:o + P], h[:, t, k * P:(k + 1) * P], ident)
                last.then_inc(S.xT_ps, 1)

            def xT(k, t=None):
                return turned[:, k, :] if t is None else turned[:, k, t * P:(t + 1) * P]

            for k in range(KD):
                pe.wait_ge(win_in[k], 16)
                pe.wait_ge((S.xT_v, S.xT_a)[k // 2 % 2], 2 * (k // 4) + k % 2 + 1)
                a, z = k == 0, k == KD - 1

                def put(o, l, r, first):
                    return mm(o, l, r, start=a and first, stop=z, skip_group_check=True)

                w = w_in_sb[:, k, :]
                put(bank[2][0:2 * RANK, 0:SEQ], w[:, C_ZG:C_AQ], xT(k), True)
                for i, c0 in enumerate((C_GQ, C_GK)):
                    for pair in range(2):
                        put(bank[i][:, pair * SEQ:(pair + 1) * SEQ], w[:, c0 + pair * P:c0 + (pair + 1) * P], xT(k), pair == 0)
                for t in range(TILES):
                    put(bank[3 + t][:, :], xT(k, t), w[:, C_AQ:C_AK], True)
                    last = put(bank[5][:, t * SEQ:(t + 1) * SEQ], xT(k, t), w[:, C_AK:D_IN], t == 0)
                if z:
                    last.then_inc(S.pass1, 1)
                if k == 5:
                    pe.wait_ge(S.diag_done, 1)
                    for t in range(TILES):
                        rl = mm(bank[6][:, t * P:(t + 1) * P], ones, diag[:, t * P:(t + 1) * P], start=True, stop=True)
                    rl.then_inc(S.rms_ps, 1)

            def gates():
                pe.wait_ge(S.zg_sb, 1)
                pe.wait_ge(S.gqk_sb, 2)
                pe.wait_ge(S.const_in, 16 * 7)
                for g in range(4):
                    last = mm(bank[g // 2][:, (g % 2) * SEQ:(g % 2 + 1) * SEQ], wg[0:2 * RANK, g * P:(g + 1) * P],
                              zg[0:2 * RANK, :], start=True, stop=True)
                last.then_inc(S.gates_ps, 1)

            pe.wait_ge(S.rms_sb, 1)
            for k in range(KD):
                for t in range(TILES):
                    last = mm(bank[6 + t][:, :], xT(k, t), w_in_sb[:, k, C_GV:C_GR], start=k == 0, stop=k == KD - 1)
                last.then_inc(S.pass2, 1)
                if k == 0:
                    gates()
            pe.wait_ge(S.raw_sb, 3 * TILES)
            for k in range(KD):
                for t in range(TILES):
                    last = mm(bank[3 + t][:, :], xT(k, t), w_in_sb[:, k, C_GR:C_ZG], start=k == 0, stop=k == KD - 1)
                last.then_inc(S.pass3, 1)

            pe.wait_ge(S.rope_done, 1)
            for b in range(5):
                if b == 4:
                    pe.wait_ge(S.qkT_sb, 1)
                for t in range(TILES):
                    o = (b % 2) * SEQ + t * P
                    last = nc.tensor.transpose(bank[(5, 2, 5)[b // 2]][:, o:o + P], rot[:, t, b * P:(b + 1) * P], ident)
                if b != 0 and b != 2:
                    last.then_inc(S.qkT_ps, 1)

            def scores(hd):
                kv, b = divmod(hd, HEADS // KV_HEADS)
                if hd == 0:
                    pe.wait_ge(S.qkT_sb, 3)
                else:
                    pe.wait_ge(S.prob_done, 2 * (hd - 1))
                rows_ = slice(kv * DH, (kv + 1) * DH)
                for t in range(TILES):
                    last = mm(bank[(5, 2)[hd % 2]][:, t * SEQ:(t + 1) * SEQ], qkT[rows_, b, t * P:(t + 1) * P],
                              qkT[rows_, 4, :], start=True, stop=True)
                last.then_inc(S.score_ps, 1)

            def turn_weights(hd):
                pe.wait_ge(S.prob_done, 2 * hd + 2)
                if hd >= 2:
                    pe.wait_ge(S.probT_sb, hd - 1)
                else:
                    pe.wait_ge(S.gv_sb, TILES)
                for st in range(TILES):
                    for t in range(TILES):
                        o = st * SEQ + t * P
                        s = t * SEQ + st * P
                        last = nc.tensor.transpose(bank[6 + hd % 2][:, o:o + P], prob[:, hd % 2, s:s + P], ident)
                last.then_inc(S.probT_ps, 1)

            def values(hd):
                kv = hd // (HEADS // KV_HEADS)
                pe.wait_ge(S.probT_sb, hd + 1)
                if hd == 0:
                    pe.wait_ge(S.gates_sb, 1)
                for t in range(TILES):
                    for st in range(TILES):
                        last = mm(bank[t][:, hd * DH:(hd + 1) * DH], probT[:, hd % 2, st * SEQ + t * P:st * SEQ + (t + 1) * P],
                                  av[:, st, kv * DH:(kv + 1) * DH], start=st == 0, stop=st == TILES - 1)
                last.then_inc(S.oatt_ps, 1)

            OFF_DIAGONAL = ((0, 0, 64, 1, 0, 0), (0, 0, 128, 2, 0, 1), (0, 0, 128, 3, 0, 5), (1, 0, 64, 3, 0, 4),
                            (1, 64, 64, 2, 1, 4), (1, 0, 128, 1, 1, 2), (1, 0, 128, 0, 1, 5), (0, 64, 64, 0, 1, 0))

            def gla_scores(hd, half):
                pair, par = divmod(hd, 2)
                rows_ = slice(par * DK, (par + 1) * DK)

                def tokens(buf, d, c):
                    return buf[rows_, 2 * d + pair, c * CHUNK:(c + 1) * CHUNK]

                def place(st, lo, n, i):
                    return bank[3][lo:lo + n, st * SEQ + i * CHUNK:st * SEQ + (i + 1) * CHUNK]

                if half == 0:
                    if hd == 0:
                        pe.wait_ge(S.gla_ready, 6)
                        pe.wait_ge(S.kk_done, 1)
                        pe.wait_ge(S.swish_ps, TILES)
                    else:
                        pe.wait_ge(S.mix_done, hd)
                    for c in range(CHUNKS):
                        lo = (c % 2) * CHUNK
                        mm(place(c // 2, lo, CHUNK, c), tokens(gA, 0, c), tokens(gX, 0, c), start=True, stop=True)
                        last = mm(bank[4][lo:lo + CHUNK, c // 2 * CHUNK:(c // 2 + 1) * CHUNK], tokens(gA, 1, c), tokens(gX, 1, c),
                                  start=True, stop=True)
                else:
                    for st, lo, n, i, d, at in OFF_DIAGONAL:
                        keys = kk[rows_, 2 * d + pair, at:at + n // CHUNK, :].rearrange("p s i -> p (s i)")
                        last = mm(place(st, lo, n, i), keys, tokens(gB, d, i), start=True, stop=True)
                last.then_inc(S.mix_ps, 1)

            for i in range(HEADS + 2):
                if i < HEADS:
                    scores(i)
                    gla_scores(i // 2, i % 2)
                if 1 <= i <= HEADS:
                    turn_weights(i - 1)
                if i >= 2:
                    values(i - 2)

            pe.wait_ge(S.probT_sb, HEADS)
            for hd in range(GLA_HEADS):
                pe.wait_ge(S.mix_done, hd + 1)
                for t in range(TILES):
                    for st in range(TILES):
                        last = mm(bank[6 + t][:, hd * DV:(hd + 1) * DV], mix[hd][:, st * SEQ + t * P:st * SEQ + (t + 1) * P],
                                  gv[:, st, hd * DV:(hd + 1) * DV], start=st == 0, stop=st == TILES - 1)
            last.then_inc(S.ogla_ps, 1)

            def turn_heads(k0, done):
                for t, b in enumerate((5, 2)):
                    for k in range(4):
                        last = nc.tensor.transpose(bank[b][:, k * P:(k + 1) * P], tok[:, t, (k0 + k) * P:(k0 + k + 1) * P], ident)
                    last.then_inc(done, 1)

            pe.wait_ge(S.oatt_sb, TILES)
            turn_heads(4, S.attT_ps)
            pe.wait_ge(S.w_out_att_in, 16)
            for t in range(TILES):
                pe.wait_ge((S.attT_v, S.attT_a)[t], 1)
                for k in range(4):
                    for nb in range(2):
                        last = mm(bank[Y[2 * t + nb]][:, :], xT(4 + k, t), w_out_att[:, k, nb * 512:(nb + 1) * 512],
                                  start=k == 0, stop=False, skip_group_check=True)
            last.then_inc(S.att_used, 1)
            pe.wait_ge(S.ogla_sb, TILES)
            turn_heads(0, S.glaT_ps)
            pe.wait_ge(S.w_out_gla_in, 16)
            for t in range(TILES):
                pe.wait_ge((S.glaT_v, S.glaT_a)[t], 1)
                for k in range(4):
                    for nb in range(2):
                        last = mm(bank[Y[2 * t + nb]][:, :], xT(k, t), w_out_gla[:, k, nb * 512:(nb + 1) * 512],
                                  start=False, stop=k == 3, skip_group_check=True)
                last.then_inc(S.h_ps, 1)

            pe.wait_ge(S.wr_done, 1)
            for t in range(TILES):
                for half, b in enumerate(((5, 2), (6, 7))[t]):
                    pe.wait_ge(S.h_done, 2 * t + half + 1)
                    for k in range(4):
                        kb = half * 4 + k
                        last = nc.tensor.transpose(bank[b][:, k * P:(k + 1) * P], h[:, t, kb * P:(kb + 1) * P], ident)
                    last.then_inc(S.hT_ps, 1)
            for t in range(TILES):
                for k in range(KD):
                    if k % 4 == 0:
                        pe.wait_ge((S.hT_v, S.hT_a)[k // 4], t + 1)
                    last = mm(bank[5][:, t * EXPERTS:(t + 1) * EXPERTS], xT(k, t), wr_sb[:, k, :], start=k == 0, stop=k == KD - 1)
            last.then_inc(S.logit_ps, 1)
            pe.wait_ge(S.chosen_done, 1)
            mm(bank[2][:, 0:EXPERTS], before, chosen[:, 0, :], start=True, stop=True)
            mm(bank[2][:, EXPERTS:2 * EXPERTS], ones, chosen[:, 0, :], start=True, stop=False)
            mm(bank[2][:, EXPERTS:2 * EXPERTS], before, chosen[:, 1, :], start=False, stop=True)
            mm(bank[2][:, 2 * EXPERTS:3 * EXPERTS], ones, chosen[:, 0, :], start=True, stop=False)
            mm(bank[2][:, 2 * EXPERTS:3 * EXPERTS], ones, chosen[:, 1, :], start=False, stop=True).then_inc(S.rank_ps, 1)

            def start_rows():
                pe.wait_ge(S.tables_done, 1)
                for t in range(TILES):
                    last = nc.tensor.transpose(bank[7][0:EXPERTS, t * P:(t + 1) * P], gate_t[:, t, 0:EXPERTS], ident)
                last.then_inc(S.gateT_ps, 1)
                pe.wait_ge(S.gateT_sb, 1)
                for t in range(TILES):
                    for nb in range(2):
                        mm(bank[Y[2 * t + nb]][:, :], gateT[0:EXPERTS, t * P:(t + 1) * P], b2_sb[:, nb * 512:(nb + 1) * 512],
                           start=True, stop=False, skip_group_check=True)

            def gather(n):
                pe.wait_ge(S.onehot_ready, n + 1)
                pe.wait_ge(S.xg_ready, n)
                for k in range(KD):
                    for i in range(PARTS):
                        for t in range(TILES):
                            last = mm(bank[6][:, k * CAP:(k + 1) * CAP], parts[:, t, i, k * P:(k + 1) * P], onehot[:, t, :],
                                      start=i == 0 and t == 0, stop=i == PARTS - 1 and t == TILES - 1)
                last.then_inc(S.gathered, 1)

            def combine():
                for t in range(TILES):
                    for j in range(GROUPS):
                        last = mm(bank[Y[2 * t + j]][:, :], gatedT[j * CAP:(j + 1) * CAP, t, :], res[j * CAP:(j + 1) * CAP, :],
                                  start=False, stop=False, skip_group_check=True)
                return last

            def expert(n, q, it, first=False):
                loads = it * LOADS_PER_BODY
                pe.wait_ge(S.xg_ready, n + 1)
                pe.wait_ge(S.res_ready, n)
                for k in range(W1_CHUNKS):
                    c = q * PER_EXPERT + k
                    pe.wait_ge(slot_in[c % SLOTS], (loads + (c // SLOTS + 1)) * 16)
                    for j in range(GROUPS):
                        for g in range(2):
                            last = mm(bank[(2, 5)[g]][j * CAP:(j + 1) * CAP, :], xg[:, k * CAP:(k + 1) * CAP],
                                      slot(c)[:, g * FF + j * FG:g * FF + (j + 1) * FG], start=k == 0, stop=False,
                                      skip_group_check=True)
                    last.then_inc(S.chunk_used, 1)
                pe.wait_ge(b1_in[q % 2], (it * (UNROLL // 2) + (q // 2 + 1)) * 16)
                for g in range(2):
                    last = mm(bank[(2, 5)[g]][:, :], split_sb, b1_sb[0:GROUPS, q % 2, g * FG:(g + 1) * FG], start=False, stop=True,
                              skip_group_check=True)
                last.then_inc(S.w1_done, 1)
                if first:
                    start_rows()
                else:
                    combine().then_inc(S.combined, 1)
                gather(n + 1)
                pe.wait_ge(S.gated_ready, n + 1)
                pe.wait_ge(S.hidT_sb, n)
                for t in range(TILES):
                    last = nc.tensor.transpose(bank[7][:, t * P:(t + 1) * P], gated[:, t, :], ident)
                last.then_inc(S.gatedT_ps, 1)
                pe.wait_ge(S.hid_ready, n + 1)
                pe.wait_ge(S.gatedT_sb, n + 1)
                for s in range(SUB):
                    last = nc.tensor.transpose(bank[7][:, s * P:(s + 1) * P], hid[:, s * P:(s + 1) * P], ident)
                last.then_inc(S.hidT_ps, 1)
                pe.wait_ge(S.hidT_sb, n + 1)
                for s in range(W2_CHUNKS):
                    c = q * PER_EXPERT + W1_CHUNKS + s
                    pe.wait_ge(slot_in[c % SLOTS], (loads + (c // SLOTS + 1)) * 16)
                    for half in range(GROUPS):
                        for j in range(GROUPS):
                            last = mm(bank[2][j * CAP:(j + 1) * CAP, :], hidT[:, s, half * CAP:(half + 1) * CAP],
                                      w2_slot(c)[:, half, j * 512:(j + 1) * 512], start=s == 0 and half == 0,
                                      stop=s == SUB - 1 and half == GROUPS - 1, skip_group_check=True)
                    last.then_inc(S.chunk_used, 1)

            for t in range(TILES):
                pe.wait_ge(S.part2, t + 1)
            gather(0)
            for q in range(UNROLL):
                expert(q, q, 0, first=q == 0)
            bodies = EXPERTS // UNROLL
            pe.wait_ge(S.extra_done, 1)
            rounds = pe.value_load(extra[0:1, 0:1], min_val=0, max_val=ROUNDS - 1)
            with pe.Fori(1, rounds * bodies + bodies) as it:
                for q in range(UNROLL):
                    expert(it * UNROLL + q, q, it)
            pe.wait_ge(S.res_ready, rounds * EXPERTS + EXPERTS)
            for t in range(TILES):
                for j in range(GROUPS):
                    last = mm(bank[Y[2 * t + j]][:, :], gatedT[j * CAP:(j + 1) * CAP, t, :], res[j * CAP:(j + 1) * CAP, :],
                              start=False, stop=True, skip_group_check=True)
                last.then_inc(S.combined, 1)


def kernel(x, mix_norm_g, w_in, w_gate_f, b_gate_f, w_gate_b, b_gate_b, gla_head_g, q_norm_g, k_norm_g,
           w_out, ffn_norm_g, w_router, b_router, w1, b1, w2, b2, final_norm_g):
    import concourse.bacc as bacc
    from concourse.bass_utils import run_bass_kernel_spmd

    def by_partition(v):
        return np.asarray(v).reshape(-1, P).T

    gate_w = np.zeros((2 * RANK, 2 * GLA_QK), np.float32)
    gate_w[0:RANK, 0:GLA_QK] = np.asarray(w_gate_f)[0]
    gate_w[RANK:, GLA_QK:] = np.asarray(w_gate_b)[0]
    columns = np.concatenate([by_partition(v) for v in (mix_norm_g, ffn_norm_g, b_gate_f, b_gate_b)], 1)
    rows = np.concatenate([np.asarray(v).reshape(-1) for v in (q_norm_g, k_norm_g, gla_head_g, b_router)])
    consts = {k: np.concatenate(v, 1).astype(np.float32) for k, v in shape_constants().items()}
    i = np.arange(P)
    arrays = {
        "x": np.asarray(x)[0],
        "w_in": np.asarray(w_in)[0],
        "w_out": np.asarray(w_out)[0],
        "w_router": np.asarray(w_router)[0].reshape(KD, P, EXPERTS).transpose(1, 0, 2).reshape(P, KD * EXPERTS),
        "w1": np.asarray(w1)[0],
        "b1": np.asarray(b1)[0],
        "w2": np.asarray(w2)[0],
        "b2": np.asarray(b2)[0],
        "gate_w": gate_w,
        "columns": columns,
        "rows": np.broadcast_to(rows, (P, rows.size)),
        "final_g": np.broadcast_to(np.asarray(final_norm_g), (P, D)),
        "c_keep": consts["c_keep"],
        "c_front": consts["c_front"],
        "later": ((i % CHUNK)[:, None] > np.arange(CHUNK)[None, :]).astype(np.int32),
        "split": (i[None, :] // CAP == np.arange(GROUPS)[:, None]).astype(np.float32),
    }
    nc = bacc.Bacc("TRN2", target_bir_lowering=False, num_devices=1)
    feeds, aps = {}, {}
    for name, a in arrays.items():
        a = np.ascontiguousarray(a)
        feeds[f"in_{name}_dram"] = a
        aps[name] = nc.dram_tensor(f"in_{name}_dram", a.shape, mybir.dt.from_np(a.dtype), kind="ExternalInput").ap()
    aps["out"] = nc.dram_tensor("out_dram", (SEQ, D), F32, kind="ExternalOutput").ap()
    encoder_layer(nc, **aps)
    r = run_bass_kernel_spmd(nc, [feeds], core_ids=[0])
    return r.results[0]["out_dram"].reshape(1, SEQ, D)
```

```python
from contextlib import ExitStack

import numpy as np

import concourse.bass as bass
from concourse import mybir

F32 = mybir.dt.float32
I32 = mybir.dt.int32
U32 = mybir.dt.uint32
BF16 = mybir.dt.bfloat16
ALU = mybir.AluOpType
ACT = mybir.ActivationFunctionType
AX = mybir.AxisListType

P = 128
SEQ = 256
TILES = SEQ // P
D = 1024
KD = D // P
EPS = 1e-6
GRID_W = 64

GLA_HEADS, DK, DV, RANK, CHUNK = 4, 64, 128, 16, 64
GLA_NORMALIZER = 16.0
CHUNKS = SEQ // CHUNK
HEADS, KV_HEADS, DH = 8, 2, 64
ROPE_THETA = 10000.0
EXPERTS, TOP_K, FF = 32, 4, 1024
ALPHA, LIMIT = 1.702, 7.0

GLA_QK, GLA_V, ATT_Q, ATT_KV = GLA_HEADS * DK, GLA_HEADS * DV, HEADS * DH, KV_HEADS * DH
C_GQ = 0
C_GK = C_GQ + GLA_QK
C_GV = C_GK + GLA_QK
C_GR = C_GV + GLA_V
C_ZG = C_GR + GLA_V
C_AQ = C_ZG + 2 * RANK
C_AK = C_AQ + ATT_Q
C_AV = C_AK + ATT_KV
D_IN = C_AV + ATT_KV

CAP = 64
GROUPS = P // CAP
ROUNDS = SEQ // CAP
FG = FF // GROUPS
SUB = FG // P
SLOTS = 16
SLOT = 2048
B1_ROWS = (32, 64)
FIN_G_ROW = 96
WORK = 14080
EARLY = 4
EARLY_AT = 37
PEELED = EARLY_AT + EARLY + SLOTS
W1_CHUNKS = KD
W2_CHUNKS = SUB
PER_EXPERT = W1_CHUNKS + W2_CHUNKS
UNROLL = 4
PER_BODY = UNROLL * PER_EXPERT
assert PER_BODY % SLOTS == 0 and EXPERTS % UNROLL == 0 and GROUPS * 1024 == SLOT
LOADS_PER_BODY = PER_BODY // SLOTS
assert all(c % PER_EXPERT for c in range(EARLY_AT, EARLY_AT + EARLY))
TABLE = ROUNDS * EXPERTS + UNROLL
ATT_PAIRS = HEADS // KV_HEADS
PARTS = 3


def shape_constants():
    p = np.arange(P)
    ident = np.eye(P)
    iota = np.tile(np.arange(CAP), (P, GROUPS))
    before = (p[:, None] < p[None, :]) * 1.0
    ones = np.ones((P, P))
    keep = np.tile((np.arange(2 * SEQ) % CHUNK != 0) * 1.0, (P, 1))
    half = DH // 4
    inv = ROPE_THETA ** (-np.arange(half, dtype=np.float32) / np.float32(half))
    token = np.arange(TILES)[None, :] * P + p[:, None]
    ang = np.stack([token // GRID_W, token % GRID_W], -1)[..., None].astype(np.float32) * inv.astype(np.float32)
    cos = np.cos(ang.astype(np.float32))
    sin = np.sin(ang.astype(np.float32))
    cos = np.stack([cos, cos], 3).reshape(P, TILES * DH)
    sin = np.stack([-sin, sin], 3).reshape(P, TILES * DH)
    return {
        "c_keep": [ident, iota, before, ones],
        "c_front": [keep, cos, sin],
    }


def encoder_layer(nc, x, w_in, w_out, w_router, w1, b1, w2, b2, gate_w, columns, rows, final_g,
                  c_keep, c_front, later, split, out):
    ctx = ExitStack()
    with ctx:
        def sb(name, shape, dt=F32):
            return ctx.enter_context(nc.sbuf_tensor(name, shape, dt))[tuple(slice(None) for _ in shape)]

        def sem(name):
            return ctx.enter_context(nc.semaphore(name))

        ring = sb("ring", [P, SLOTS * SLOT])
        h = sb("h", [P, TILES, D])
        tok = sb("tok", [P, TILES, D])
        ckeep = sb("ckeep", [P, 4 * P])
        ident, iota, before, ones = (ckeep[:, i * P:(i + 1) * P] for i in range(4))
        biases = sb("biases", [P, D])
        b2_sb = biases[0:EXPERTS, :]
        b1_sb = [biases[r:r + GROUPS, :] for r in B1_ROWS]
        split_sb = sb("split_sb", [P, P])
        wr_sb = sb("wr_sb", [P, KD, EXPERTS])
        col = sb("col", [P, 2 * KD + 4])
        mix_g, ffn_g, gate_b = col[:, 0:KD], col[:, KD:2 * KD], col[:, 2 * KD:2 * KD + 4]
        later_sb = sb("later_sb", [P, CHUNK], I32)
        stat = sb("stat", [P, 144])
        extra = sb("extra", [1, 4], I32)
        fin_g = biases[FIN_G_ROW:FIN_G_ROW + 1, :]
        work = sb("work", [P, WORK])

        class Carve:

            def __init__(self, base, start=0):
                self.base, self.at = base, start

            def __call__(self, *shape):
                n = int(np.prod(shape))
                piece = self.base[:, self.at:self.at + n]
                self.at += n
                if len(shape) == 2:
                    piece = piece.rearrange("p (a b) -> p a b", b=shape[1])
                elif len(shape) == 3:
                    piece = piece.rearrange("p (a b c) -> p a b c", b=shape[1], c=shape[2])
                return piece

        front = Carve(work)
        turned = front(KD, SEQ)
        gqk = front(2, 2 * SEQ)
        zg = front(SEQ)
        wg = front(4 * P)
        cfront = front(2 * SEQ + 2 * TILES * DH)
        keep = cfront[:, 0:2 * SEQ]
        cos = cfront[:, 2 * SEQ:2 * SEQ + TILES * DH].rearrange("p (t d) -> p t d", d=DH)
        sin = cfront[:, 2 * SEQ + TILES * DH:2 * SEQ + 2 * TILES * DH].rearrange("p (t d) -> p t d", d=DH)
        QK = ATT_Q + ATT_KV
        at_raw = front.at
        raw = front(TILES, QK)
        at_rot = front.at
        rot = front(TILES, QK)
        swp = front(TILES, QK)
        tab = front(2, 2, TILES * DH)
        qkT = front(5, SEQ)
        av = front(TILES, ATT_KV)
        gv = front(TILES, GLA_V)
        at_sg = front.at
        sg = front(TILES, GLA_V)
        att2 = front(2, 2 * SEQ)
        row = front(2 * DH + DV + EXPERTS)
        q_g, k_g, head_g, router_b = row[:, 0:DH], row[:, DH:2 * DH], row[:, 2 * DH:2 * DH + DV], row[:, 2 * DH + DV:]
        assert front.at <= WORK
        reuse = Carve(work, at_raw)
        att01 = reuse(2, 2 * SEQ)
        reuse = Carve(work, at_sg)
        diag = reuse(SEQ)
        rms = reuse(SEQ)
        reuse = Carve(work, at_rot)
        prob = reuse(2, 2 * SEQ)
        probT = reuse(2, 2 * SEQ)
        mix = [att01[:, 0, :], att01[:, 1, :], att2[:, 0, :], att2[:, 1, :]]
        scratch = Carve(ring, 10 * SLOT)
        gA, gM, gB, gX = (scratch(4, SEQ) for _ in range(4))
        decayed = Carve(ring, KD * D_IN)
        kk = decayed(4, 7, CHUNK)
        assert decayed.at <= 10 * SLOT
        w_in_sb = ring[:, 0:KD * D_IN].rearrange("p (k n) -> p k n", n=D_IN)
        w_out_att = ring[:, 12 * SLOT:14 * SLOT].rearrange("p (k n) -> p k n", n=D)
        w_out_gla = ring[:, 14 * SLOT:16 * SLOT].rearrange("p (k n) -> p k n", n=D)

        early = [work[:, KD * SEQ + i * SLOT:KD * SEQ + (i + 1) * SLOT] for i in range(EARLY)]

        back = Carve(work)
        logit = back(TILES, EXPERTS)
        top = back(TILES, 8)
        topi = back(TILES * 8)
        topf = back(TILES, 8)
        chosen = back(TILES * EXPERTS // 2).bitcast(BF16).rearrange("p (t e) -> p t e", e=EXPERTS)
        before_b = back(P // 2).bitcast(BF16)
        ones_b = back(P // 2).bitcast(BF16)
        weight = back(TILES, EXPERTS)
        rank = back(TILES, EXPERTS)
        rank_t = back(TILES, TABLE)
        gate_t = back(TILES, TABLE)
        onehot = back(TILES * CAP // 2).bitcast(BF16).rearrange("p (t c) -> p t c", c=CAP)
        gated = back(TILES, P)
        at_gatedT = back.at
        gatedT = back(TILES, P)
        xg = back(KD * CAP)
        assert back.at <= KD * SEQ
        reuse = Carve(work, at_gatedT)
        hit = reuse(TILES, TOP_K * EXPERTS)
        back = Carve(work, KD * SEQ + EARLY * SLOT)
        at_glu = back.at
        glu = back(FG)
        lin = back(FG)
        sig = back(FG)
        hidT = back(SUB, P)
        part0 = back(TILES * D // 2).bitcast(BF16).rearrange("p (t d) -> p t d", d=D)
        gateT = back(SEQ)
        res = back(D // GROUPS)
        reuse = Carve(work, at_glu)
        left = reuse(TILES, D)
        assert back.at <= WORK
        parts12 = tok.bitcast(BF16).rearrange("p t (i d) -> p t i d", i=PARTS - 1)
        parts = [[part0[:, t, :]] + [parts12[:, t, i, :] for i in range(PARTS - 1)] for t in range(TILES)]

        bank = [ctx.enter_context(nc.psum_tensor(f"bank{i}", [P, 512], F32))[:, :] for i in range(8)]

        names = """x0_in x1_in ident_in col_in const_in w_out_att_in w_out_gla_in fin_g_in fin_g_ps stored
            sq_done var_done rstd_done xT_ps xT_v xT_a diag_done rms_ps rms_sb pass1 pass2 pass3
            zg_sb gqk_sb raw_sb raw_sq hvar_done hrstd_done rope_done wr_done
            gates_ps gates_sb gabs gln arg_done exp_done gla_ready kk_done
            gv_sb gr_sig swish_ps sg_done qkT_ps qkT_sb
            score_ps nmax_done prob_done prob_normed probT_ps probT_a probT_v attT_ps attT_sb att_used
            backward_ps mix_ps mix_a mix_done ogla_ps ogla_sq ogla_var ogla_rstd ogla_sb
            glaT_ps glaT_v glaT_a h_ps h_done hsq var2 rstd2 hT_ps hT_v hT_a
            n2_done part0 left1 part1 part2
            logit_ps top_done count_masks wexp_done chosen_done rank_ps count_ps tables_done gateT_ps gateT_sb extra_done
            onehot_ready gathered xg_ready glu_ready sig_ready hid_ready combined
            gated_ready gatedT_ps gatedT_sb hidT_ps hidT_sb res_ready chunk_used
            y_done y_gained ysq ysum var3 rstd3 fin_a fin_v
            dve_step pool_step""".split()
        S = type("Semaphores", (), {n: sem(n) for n in names})
        win_in = [sem(f"win_in{k}") for k in range(KD)]
        slot_in = [sem(f"slot_in{s}") for s in range(SLOTS)]
        early_in = [sem(f"early_in{s}") for s in range(EARLY)]
        b1_in = [sem(f"b1_in{i}") for i in range(2)]

        Y = (0, 1, 3, 4)
        PAIR_BANKS = ((5, 2), (6, 7))
        block = ctx.enter_context(nc.Block())

        def slot_of(c):
            return (c - EARLY) % SLOTS

        def first_slot_of(c):
            return c % SLOTS

        def slot(s):
            return ring[:, s * SLOT:(s + 1) * SLOT]

        def by_half(chunk):
            return chunk.rearrange("p (j n) -> p j n", n=D)

        @block.sync
        def _(sp):
            sp.dma_start(h[:, 0, :], x[0:P, :]).then_inc(S.x0_in, 16)
            sp.dma_start(ckeep, c_keep).then_inc(S.ident_in, 16)
            sp.dma_start(h[:, 1, :], x[P:SEQ, :]).then_inc(S.x1_in, 16)
            sp.dma_start(col, columns).then_inc(S.col_in, 16)
            for k in range(KD):
                sp.dma_start(w_in_sb[:, k, :], w_in[k * P:(k + 1) * P, :]).then_inc(win_in[k], 16)
                if k == 2:
                    sp.dma_start(cfront, c_front).then_inc(S.const_in, 16)
                    sp.dma_start(row, rows).then_inc(S.const_in, 16)
                    sp.dma_start(wg[0:2 * RANK, :], gate_w).then_inc(S.const_in, 16)
            sp.dma_start(later_sb, later).then_inc(S.const_in, 16)
            sp.dma_start(wr_sb, w_router.rearrange("p (k e) -> p k e", e=EXPERTS)).then_inc(S.const_in, 16)
            for r in B1_ROWS:
                sp.dma_start(split_sb[r:r + GROUPS, :], split).then_inc(S.const_in, 16)
            sp.dma_start(b2_sb, b2).then_inc(S.const_in, 16)
            sp.dma_start(fin_g, final_g).then_inc(S.fin_g_in, 16)
            def load_b1(n, e):
                sp.dma_start(b1_sb[n % 2].rearrange("j (g f) -> j g f", g=2),
                             b1[e].rearrange("(g j f) -> j g f", g=2, j=GROUPS)).then_inc(b1_in[n % 2], 16)

            load_b1(0, 0)
            load_b1(1, 1)
            for kv in range(KV_HEADS):
                sp.dma_start(w_out_att[kv * DH:(kv + 1) * DH, :, :],
                             w_out[GLA_V + kv * 4 * DH:GLA_V + (kv + 1) * 4 * DH, :].rearrange("(b p) n -> p b n", p=DH))\
                    .then_inc(S.w_out_att_in, 16)
            sp.dma_start(w_out_gla, w_out[0:GLA_V, :].rearrange("(k p) n -> p k n", p=P)).then_inc(S.w_out_gla_in, 16)

            def load(to, loaded, e, r):
                if r < W1_CHUNKS:
                    sp.dma_start(to, w1[e, r * P:(r + 1) * P, :]).then_inc(loaded, 16)
                else:
                    s = r - W1_CHUNKS
                    sp.dma_start(by_half(to), w2[e].rearrange("(j s p) n -> s p j n", j=GROUPS, p=P)[s]).then_inc(loaded, 16)

            def first_ring(s):
                load(slot(s), slot_in[s], s // PER_EXPERT, s % PER_EXPERT)

            def load_early(i):
                load(early[i], early_in[i], (EARLY_AT + i) // PER_EXPERT, (EARLY_AT + i) % PER_EXPERT)

            for s in range(9):
                sp.wait_ge(S.pass3, min(KD, ((s + 1) * SLOT - 1) // D_IN + 1))
                first_ring(s)
            sp.wait_ge(S.kk_done, 1)
            load_early(0)
            sp.wait_ge(S.mix_ps, 2)
            for s in range(9, 12):
                first_ring(s)
            sp.wait_ge(S.attT_ps, ATT_PAIRS)
            for i in range(1, EARLY):
                load_early(i)
            sp.wait_ge(S.att_used, 1)
            for s in range(12, 14):
                first_ring(s)
            sp.wait_ge(S.h_ps, TILES)
            for s in range(14, SLOTS):
                first_ring(s)
            sp.wait_ge(S.extra_done, 1)

            rounds = sp.value_load(extra[0:1, 0:1], min_val=0, max_val=ROUNDS - 1)

            def refill(it, used, e):
                c = SLOTS + used
                q, r = divmod(c, PER_EXPERT)
                if r == 0:
                    sp.wait_ge(S.chunk_used, it * PER_BODY + ((q - 2) * PER_EXPERT + W1_CHUNKS))
                    load_b1(q, e)
                sp.wait_ge(S.chunk_used, it * PER_BODY + (used + 1))
                load(slot(slot_of(c)), slot_in[slot_of(c)], e, r)

            def refill_first(c, s, behind):
                q, r = divmod(c, PER_EXPERT)
                sp.wait_ge(S.chunk_used, c - behind + 1)
                if r == 0:
                    sp.wait_ge(S.chunk_used, (q - 2) * PER_EXPERT + W1_CHUNKS)
                    load_b1(q, q)
                load(slot(s), slot_in[s], q, r)

            for c in range(SLOTS, EARLY_AT):
                refill_first(c, first_slot_of(c), SLOTS)
            for c in range(EARLY_AT + EARLY, PEELED):
                refill_first(c, slot_of(c), SLOTS + EARLY)

            start = PEELED - SLOTS
            bodies = EXPERTS // UNROLL
            whole = (EXPERTS * PER_EXPERT - PEELED) // PER_BODY
            with sp.Fori(0, rounds * bodies + whole) as it:
                for used in range(start, start + PER_BODY):
                    refill(it, used, (it * UNROLL + (SLOTS + used) // PER_EXPERT) % EXPERTS)
            last = rounds * bodies + whole
            for used in range(start, (bodies - whole) * PER_BODY - SLOTS):
                refill(last, used, whole * UNROLL + (SLOTS + used) // PER_EXPERT)
            for t in range(TILES):
                for nb in range(2):
                    cols = slice(nb * 512, (nb + 1) * 512)
                    sp.wait_ge((S.fin_a, S.fin_v)[nb], t + 1)
                    sp.dma_start(out[t * P:(t + 1) * P, cols], tok[:, t, cols]).then_inc(S.stored, 16)
            sp.wait_ge(S.stored, 16 * 2 * TILES)

        @block.gpsimd
        def _(pool):
            minus_half = stat[:, 64:96]
            pool.memset(minus_half, -0.5).then_inc(S.pool_step, 1)
            pool.wait_ge(S.pool_step, 1)

            def rsqrt(to, of, n):
                return pool.tensor_tensor(to, of, minus_half[:, 0:n], ALU.pow)

            for t in range(TILES):
                pool.wait_ge(S.var_done, t + 1)
                rsqrt(stat[:, 4 + t:5 + t], stat[:, 2 + t:3 + t], 1).then_inc(S.rstd_done, 1)
            pool.wait_ge(S.const_in, 16 * 8)
            pool.wait_ge(S.col_in, 16)
            pool.tensor_tensor(wr_sb, wr_sb, ffn_g.rearrange("p (k o) -> p k o", o=1).broadcast_to([P, KD, EXPERTS]), ALU.mult)\
                .then_inc(S.wr_done, 1)
            pool.wait_ge(S.hvar_done, 1)
            rsqrt(stat[:, 28:48], stat[:, 8:28], 20).then_inc(S.hrstd_done, 1)
            pool.wait_ge(S.swish_ps, TILES)
            sg8 = sg.rearrange("p t (h d) -> p (t h) d", d=DV)
            pool.tensor_tensor(sg8, sg8, head_g.rearrange("p (o d) -> p o d", o=1).broadcast_to([P, TILES * GLA_HEADS, DV]),
                               ALU.mult).then_inc(S.sg_done, 1)
            pool.wait_ge(S.ogla_var, 1)
            rsqrt(stat[:, 56:64], stat[:, 48:56], 8).then_inc(S.ogla_rstd, 1)
            for t in range(TILES):
                pool.wait_ge(S.var2, t + 1)
                rsqrt(stat[:, 4 + t:5 + t], stat[:, 2 + t:3 + t], 1).then_inc(S.rstd2, 1)
                if t == 0:
                    pool.wait_ge(S.n2_done, 1)
                    pool.wait_ge(S.part0, 1)
                    pool.tensor_tensor(left[:, 0, :], tok[:, 0, :], parts[0][0], ALU.subtract).then_inc(S.left1, 1)
            for t in range(TILES):
                pool.wait_ge(S.part1, t + 1)
                pool.tensor_tensor(parts[t][2], left[:, t, :], parts[t][1], ALU.subtract).then_inc(S.part2, 1)
            for t in range(TILES):
                pool.wait_ge(S.var3, t + 1)
                rsqrt(stat[:, 4 + t:5 + t], stat[:, 2 + t:3 + t], 1).then_inc(S.rstd3, 1)

        @block.scalar
        def _(act):
            act.wait_ge(S.x0_in, 16)
            nc.scalar.activation(rot.rearrange("p a b -> p (a b)")[:, 0:D], h[:, 0, :], ACT.Square,
                                 accum_out=stat[:, 0:1]).then_inc(S.sq_done, 1)
            act.wait_ge(S.col_in, 16)
            for k in (2, 3, 6, 7):
                act.wait_ge(S.xT_ps, k // 2 + 1)
                nc.scalar.activation(turned[:, k, :], bank[7][:, (k % 2) * SEQ:(k % 2 + 1) * SEQ], ACT.Copy,
                                     scale=mix_g[:, k:k + 1]).then_inc(S.xT_a, 1)
            act.wait_ge(S.rms_ps, 1)
            nc.scalar.activation(rms, bank[6][:, 0:SEQ], ACT.Copy).then_inc(S.rms_sb, 1)

            act.wait_ge(S.rstd_done, TILES)
            act.wait_ge(S.pass1, 1)
            for t in range(TILES):
                inv = stat[:, 4 + t:5 + t]
                nc.scalar.activation(raw[:, t, 0:ATT_Q].rearrange("p (b k d) -> p k b d", k=KV_HEADS, d=DH),
                                     bank[3 + t][:, :].rearrange("p (k b d) -> p k b d", k=KV_HEADS, d=DH), ACT.Copy,
                                     scale=inv).then_inc(S.raw_sb, 1)
            for t in range(TILES):
                inv = stat[:, 4 + t:5 + t]
                nc.scalar.activation(raw[:, t, ATT_Q:QK], bank[5][:, t * SEQ:t * SEQ + ATT_KV], ACT.Copy,
                                     scale=inv).then_inc(S.raw_sb, 1)
                nc.scalar.activation(av[:, t, :], bank[5][:, t * SEQ + ATT_KV:(t + 1) * SEQ], ACT.Copy,
                                     scale=inv).then_inc(S.raw_sb, 1)
            act.wait_ge(S.gates_sb, 1)
            nc.scalar.activation(gA, gM, ACT.Abs).then_inc(S.gabs, 1)
            act.wait_ge(S.gabs, 1)
            nc.scalar.activation(gA, gA, ACT.Exp, scale=-1.0).then_inc(S.gabs, 1)
            act.wait_ge(S.gabs, 2)
            nc.scalar.activation(gA, gA, ACT.Ln, bias=1.0).then_inc(S.gln, 1)
            act.wait_ge(S.raw_sb, 3 * TILES)
            nc.scalar.activation(rot, raw, ACT.Square).then_inc(S.raw_sq, 1)
            act.wait_ge(S.arg_done, 1)
            nc.scalar.activation(gX, gA, ACT.Exp, scale=1.0 / GLA_NORMALIZER).then_inc(S.exp_done, 1)
            act.wait_ge(S.exp_done, 1)
            nc.scalar.activation(gA, gA, ACT.Exp, scale=-1.0 / GLA_NORMALIZER).then_inc(S.exp_done, 1)
            act.wait_ge(S.arg_done, 2)
            nc.scalar.activation(gB, gB, ACT.Exp, scale=1.0 / GLA_NORMALIZER).then_inc(S.exp_done, 1)
            nc.scalar.activation(gM, gM, ACT.Exp, scale=1.0 / GLA_NORMALIZER).then_inc(S.exp_done, 1)
            act.wait_ge(S.pass2, KD)
            for t in range(TILES):
                nc.scalar.activation(gv[:, t, :], bank[6 + t][:, :], ACT.Copy, scale=stat[:, 4 + t:5 + t]).then_inc(S.gv_sb, 1)
            act.wait_ge(S.pass3, KD)
            for t in range(TILES):
                nc.scalar.activation(sg[:, t, :], bank[3 + t][:, :], ACT.Sigmoid, scale=stat[:, 4 + t:5 + t]).then_inc(S.gr_sig, 1)

            def weights_out(i):
                act.wait_ge(S.probT_ps, i + 1)
                if i >= 1:
                    act.wait_ge(S.attT_ps, i)
                nc.scalar.activation(probT[:, 0, :], bank[PAIR_BANKS[i % 2][0]][:, :], ACT.Copy).then_inc(S.probT_a, 1)

            def gla_scores(pair):
                act.wait_ge(S.mix_ps, pair + 1)
                nc.scalar.activation(mix[2 * pair], bank[3][:, :], ACT.Copy).then_inc(S.mix_a, 1)

            for i in range(ATT_PAIRS):
                if i == 2:
                    gla_scores(0)
                if i >= 1:
                    weights_out(i - 1)
                act.wait_ge(S.nmax_done, i + 1)
                if i >= 1:
                    act.wait_ge(S.probT_ps, i)
                for kv in range(KV_HEADS):
                    for t in range(TILES):
                        c = 4 * i + 2 * kv + t
                        nc.scalar.activation(prob[:, kv, t * SEQ:(t + 1) * SEQ], bank[PAIR_BANKS[i % 2][kv]][:, t * SEQ:(t + 1) * SEQ],
                                             ACT.Exp, bias=stat[:, 96 + c:97 + c], accum_out=stat[:, 112 + c:113 + c])\
                            .then_inc(S.prob_done, 1)
            gla_scores(1)
            weights_out(ATT_PAIRS - 1)
            for j in range(2):
                act.wait_ge(S.attT_ps, 2 * j + 2)
                nc.scalar.activation(turned[:, 4 + 2 * j:6 + 2 * j, :], bank[j][:, :].rearrange("p (b t) -> p b t", t=SEQ),
                                     ACT.Copy).then_inc(S.attT_sb, 1)

            act.wait_ge(S.ogla_ps, 1)
            for t in range(TILES):
                nc.scalar.activation(tok[:, t, 0:GLA_V], bank[3 + t][:, :], ACT.Square).then_inc(S.ogla_sq, 1)
            act.wait_ge(S.glaT_ps, 2)
            nc.scalar.activation(turned[:, 0:4, P:SEQ], bank[2][:, :].rearrange("p (k t) -> p k t", t=P),
                                 ACT.Copy).then_inc(S.glaT_a, 1)

            for t in range(TILES):
                act.wait_ge(S.h_done, 2 * t + 2)
                nc.scalar.activation(left[:, t, :], h[:, t, :], ACT.Square, accum_out=stat[:, t:t + 1]).then_inc(S.hsq, 1)
                if t == 0:
                    act.wait_ge(S.rstd2, 1)
                    nc.scalar.activation(parts[0][0], h[:, 0, :], ACT.Copy, scale=stat[:, 4:5]).then_inc(S.part0, 1)
                act.wait_ge(S.hT_ps, 2 * t + 2)
                nc.scalar.activation(turned[:, 4:8, t * P:(t + 1) * P], bank[(1, 4)[t]][:, :].rearrange("p (k t) -> p k t", t=P),
                                     ACT.Copy).then_inc(S.hT_a, 1)
            act.wait_ge(S.rstd2, 2)
            nc.scalar.activation(parts[1][0], h[:, 1, :], ACT.Copy, scale=stat[:, 5:6]).then_inc(S.part0, 1)
            for t in range(TILES):
                act.wait_ge(S.left1, t + 1)
                nc.scalar.activation(parts[t][1], left[:, t, :], ACT.Copy).then_inc(S.part1, 1)
            act.wait_ge(S.logit_ps, 1)
            nc.scalar.activation(before_b, before, ACT.Copy).then_inc(S.count_masks, 1)
            nc.scalar.activation(ones_b, ones, ACT.Copy).then_inc(S.count_masks, 1)
            act.wait_ge(S.top_done, 1)
            for t in range(TILES):
                nc.scalar.activation(weight[:, t, :], logit[:, t, :], ACT.Exp, bias=stat[:, 6 + t:7 + t])\
                    .then_inc(S.wexp_done, 1)

            def expert(n):
                act.wait_ge(S.glu_ready, n + 1)
                nc.scalar.activation(sig, glu, ACT.Sigmoid, scale=ALPHA).then_inc(S.sig_ready, 1)
                act.wait_ge(S.hidT_ps, n + 1)
                nc.scalar.activation(hidT, bank[5][:, :].rearrange("p (s q) -> p s q", q=P), ACT.Copy)\
                    .then_inc(S.hidT_sb, 1)
                act.wait_ge(S.gatedT_ps, n + 1)
                nc.scalar.activation(gatedT, bank[7][:, 0:SEQ].rearrange("p (t q) -> p t q", q=P), ACT.Copy)\
                    .then_inc(S.gatedT_sb, 1)
                act.wait_ge(S.chunk_used, (n + 1) * PER_EXPERT)
                nc.scalar.activation(res, bank[2][:, :], ACT.Copy).then_inc(S.res_ready, 1)

            for n in range(UNROLL):
                expert(n)
            bodies = EXPERTS // UNROLL
            act.wait_ge(S.extra_done, 1)
            rounds = act.value_load(extra[0:1, 0:1], min_val=0, max_val=ROUNDS - 1)
            with act.Fori(1, rounds * bodies + bodies) as it:
                for q in range(UNROLL):
                    expert(it * UNROLL + q)

            for t in range(TILES):
                for nb in range(2):
                    act.wait_ge(S.y_done, 2 * t + nb + 1)
                    nc.scalar.activation(left[:, t, nb * 512:(nb + 1) * 512], h[:, t, nb * 512:(nb + 1) * 512], ACT.Square,
                                         accum_out=stat[:, 8 + 2 * t + nb:9 + 2 * t + nb]).then_inc(S.ysq, 1)
            for t in range(TILES):
                act.wait_ge(S.rstd3, t + 1)
                act.wait_ge(S.y_gained, t + 1)
                nc.scalar.activation(tok[:, t, 0:512], tok[:, t, 0:512], ACT.Copy, scale=stat[:, 4 + t:5 + t]).then_inc(S.fin_a, 1)

        @block.vector
        def _(dve):
            steps = [0]

            def step(ins):
                steps[0] += 1
                ins.then_inc(S.dve_step, 1)
                dve.wait_ge(S.dve_step, steps[0])

            def mean_eps(out_, in_, n):
                return nc.vector.tensor_scalar(out_, in_, 1.0 / n, EPS, ALU.mult, ALU.add)

            dve.wait_ge(S.x1_in, 16)
            step(nc.vector.scalar_tensor_tensor(swp.rearrange("p a b -> p (a b)")[:, 0:D], h[:, 1, :], 1.0, h[:, 1, :],
                                                ALU.mult, ALU.mult, accum_out=stat[:, 1:2]))
            dve.wait_ge(S.sq_done, 1)
            for t in range(TILES):
                mean_eps(stat[:, 2 + t:3 + t], stat[:, t:t + 1], D).then_inc(S.var_done, 1)
            dve.wait_ge(S.col_in, 16)
            for k in (0, 1, 4, 5):
                dve.wait_ge(S.xT_ps, k // 2 + 1)
                nc.vector.tensor_scalar(turned[:, k, :], bank[6][:, (k % 2) * SEQ:(k % 2 + 1) * SEQ], mix_g[:, k:k + 1], None,
                                        ALU.mult).then_inc(S.xT_v, 1)
            dve.wait_ge(S.rstd_done, TILES)
            dve.wait_ge(S.ident_in, 16)
            for t in range(TILES):
                last = nc.vector.tensor_scalar(diag[:, t * P:(t + 1) * P], ident, stat[:, 4 + t:5 + t], None, ALU.mult)
            last.then_inc(S.diag_done, 1)
            dve.wait_ge(S.const_in, 16 * 8)
            for i, g in enumerate((q_g, k_g)):
                scale = DH ** -0.5 if i == 0 else 1.0
                for t in range(TILES):
                    nc.vector.scalar_tensor_tensor(tab[:, i, 0, t * DH:(t + 1) * DH], cos[:, t, :], scale, g,
                                                   ALU.mult, ALU.mult)
                    gs = g.rearrange("p (a f d) -> p a f d", a=2, f=2)
                    for f in range(2):
                        last = nc.vector.scalar_tensor_tensor(
                            tab[:, i, 1, t * DH:(t + 1) * DH].rearrange("p (a f d) -> p a f d", a=2, f=2)[:, :, f, :],
                            sin[:, t, :].rearrange("p (a f d) -> p a f d", a=2, f=2)[:, :, f, :], scale,
                            gs[:, :, 1 - f, :], ALU.mult, ALU.mult)
            step(last)

            dve.wait_ge(S.pass1, 1)
            dve.wait_ge(S.rms_sb, 1)
            nc.vector.tensor_tensor(zg[0:2 * RANK, :], bank[2][0:2 * RANK, 0:SEQ], rms[0:2 * RANK, :], ALU.mult).then_inc(S.zg_sb, 1)
            rms2 = rms.rearrange("p (o t) -> p o t", o=1).broadcast_to([P, 2, SEQ])
            for i, scale in enumerate((DK ** -0.5, 1.0)):
                nc.vector.scalar_tensor_tensor(gqk[:, i, :].rearrange("p (g t) -> p g t", g=2),
                                               bank[i][:, :].rearrange("p (g t) -> p g t", g=2), scale, rms2,
                                               ALU.mult, ALU.mult).then_inc(S.gqk_sb, 1)
            dve.wait_ge(S.gates_ps, 1)
            for g in range(4):
                last = nc.vector.tensor_scalar(gM[:, g, :], bank[g // 2][:, (g % 2) * SEQ:(g % 2 + 1) * SEQ],
                                               gate_b[:, g:g + 1], None, ALU.add)
            last.then_inc(S.gates_sb, 1)
            NH = HEADS + KV_HEADS
            dve.wait_ge(S.gln, 1)
            step(nc.vector.scalar_tensor_tensor(gM, gM, 0.0, gA, ALU.min, ALU.subtract))
            flat = [t.rearrange("p g t -> p (g t)") for t in (gM, gB, gA)]
            half = 2 * SEQ
            nc.vector.tensor_tensor_scan(flat[1][:, 0:half], keep, flat[0][:, 0:half], 0.0, ALU.mult, ALU.add)
            step(nc.vector.tensor_tensor_scan(flat[1][:, 2 * half - 1:half - 1:-1], keep, flat[0][:, 2 * half - 1:half - 1:-1],
                                              0.0, ALU.mult, ALU.add))

            def chunked(buf, direction):
                return buf[:, 2 * direction:2 * direction + 2, :].rearrange("p g (c i) -> p (g c) i", i=CHUNK)

            mid = (CHUNK // 2 - 1, CHUNK // 2)
            edge = (CHUNK - 1, 0)
            shape = [P, 2 * CHUNKS, CHUNK]
            for d in range(2):
                b = chunked(gB, d)
                last = nc.vector.tensor_tensor(chunked(gA, d), b, b[:, :, mid[d]:mid[d] + 1].broadcast_to(shape), ALU.subtract)
            last.then_inc(S.arg_done, 1)
            for d in range(2):
                b = chunked(gB, d)
                last = nc.vector.tensor_tensor(chunked(gM, d), b[:, :, edge[d]:edge[d] + 1].broadcast_to(shape), b, ALU.subtract)
            last.then_inc(S.arg_done, 1)

            dve.wait_ge(S.raw_sq, 1)
            step(nc.vector.tensor_reduce(stat[:, 28:48], rot.rearrange("p t (h d) -> p (t h) d", d=DH), AX.X, ALU.add))
            mean_eps(stat[:, 8:28], stat[:, 28:48], DH).then_inc(S.hvar_done, 1)
            tabs = tab.rearrange("p i s (t d) -> p i s t d", d=DH)
            for t in range(TILES):
                for i, (h0, n) in enumerate(((0, HEADS), (HEADS, KV_HEADS))):
                    src = raw[:, t, h0 * DH:(h0 + n) * DH].rearrange("p (h d) -> p h d", d=DH)
                    dst = rot[:, t, h0 * DH:(h0 + n) * DH].rearrange("p (h d) -> p h d", d=DH)
                    sw = swp[:, t, h0 * DH:(h0 + n) * DH].rearrange("p (h d) -> p h d", d=DH)
                    nc.vector.tensor_tensor(dst, src, tabs[:, i, 0, t:t + 1, :].broadcast_to([P, n, DH]), ALU.mult)
                    for f in range(2):
                        part = sw.rearrange("p h (a f d) -> p h a f d", a=2, f=2)[:, :, :, f, :]
                        other = src.rearrange("p h (a f d) -> p h a f d", a=2, f=2)[:, :, :, 1 - f, :]
                        table = tabs[:, i, 1, t:t + 1, :].rearrange("p o (a f d) -> p o a f d", a=2, f=2)[:, :, :, f, :]
                        last = nc.vector.tensor_tensor(part, other, table.broadcast_to([P, n, 2, DH // 4]), ALU.mult)
            step(last)
            step(nc.vector.tensor_tensor(rot, rot, swp, ALU.add))
            dve.wait_ge(S.hrstd_done, 1)
            nc.vector.tensor_tensor(rot.rearrange("p t (h d) -> p (t h) d", d=DH), rot.rearrange("p t (h d) -> p (t h) d", d=DH),
                                    stat[:, 28:48].rearrange("p (h o) -> p h o", o=1).broadcast_to([P, TILES * NH, DH]),
                                    ALU.mult).then_inc(S.rope_done, 1)

            q2, k2 = gqk[:, 0, :], gqk[:, 1, :]
            dve.wait_ge(S.gqk_sb, 2)

            def pairs(buf, d):
                return buf[:, 2 * d:2 * d + 2, :].rearrange("p g t -> p (g t)")

            dve.wait_ge(S.exp_done, 4)
            for d in range(2):
                nc.vector.tensor_tensor(pairs(gX, d), pairs(gX, d), q2, ALU.mult).then_inc(S.gla_ready, 1)
                nc.vector.tensor_tensor(pairs(gA, d), pairs(gA, d), k2, ALU.mult).then_inc(S.gla_ready, 1)
            dec = stat[:, 128:128 + 4 * CHUNKS]
            for d in range(2):
                last = nc.vector.tensor_copy(dec[:, 8 * d:8 * d + 8].rearrange("p (c o) -> p c o", o=1),
                                             chunked(gB, d)[:, :, edge[d]:edge[d] + 1])
            step(last)
            for d in range(2):
                nc.vector.tensor_tensor(pairs(gB, d), pairs(gB, d), q2, ALU.mult).then_inc(S.gla_ready, 1)
            k4 = k2.rearrange("p (g c i) -> p g c i", g=2, i=CHUNK)
            for d in range(2):
                last = nc.vector.tensor_tensor(kk[:, 2 * d:2 * d + 2, :, :].rearrange("p g s i -> p g s i")[:, :, 0:5:2, :],
                                               gM[:, 2 * d:2 * d + 2, :].rearrange("p g (c i) -> p g c i", i=CHUNK)[:, :, d:d + 3, :],
                                               k4[:, :, d:d + 3, :], ALU.mult)
            step(last)
            dec4 = dec.rearrange("p (d g c) -> p d g c", d=2, g=2)

            def carry(d, to, of, c):
                return nc.vector.tensor_tensor(kk[:, 2 * d:2 * d + 2, to, :], kk[:, 2 * d:2 * d + 2, of, :],
                                               dec4[:, d, :, c:c + 1].broadcast_to([P, 2, CHUNK]), ALU.mult)

            carry(0, 1, 0, 1)
            carry(0, 6, 2, 2)
            carry(1, 5, 2, 1)
            step(carry(1, 3, 4, 2))
            carry(0, 5, 1, 2)
            carry(1, 6, 3, 1).then_inc(S.kk_done, 1)

            for i, b in enumerate((5, 2, 6)):
                dve.wait_ge(S.qkT_ps, i + 1)
                n = 2 if i < 2 else 1
                nc.vector.tensor_copy(qkT[:, 2 * i:2 * i + n, :],
                                      bank[b][:, 0:n * SEQ].rearrange("p (b t) -> p b t", t=SEQ)).then_inc(S.qkT_sb, 1)

            def row_maxima(i):
                dve.wait_ge(S.score_ps, i + 1)
                nm = stat[:, 96 + 4 * i:100 + 4 * i]
                for kv in range(KV_HEADS):
                    last = nc.vector.tensor_reduce(nm[:, 2 * kv:2 * kv + 2],
                                                   bank[PAIR_BANKS[i % 2][kv]][:, :].rearrange("p (t s) -> p t s", s=SEQ), AX.X, ALU.max)
                step(last)
                nc.vector.tensor_scalar(nm, nm, -1.0, None, ALU.mult).then_inc(S.nmax_done, 1)

            def normalise(i):
                dve.wait_ge(S.prob_done, 4 * i + 4)
                sums = stat[:, 112 + 4 * i:116 + 4 * i]
                step(nc.vector.reciprocal(sums, sums))
                for kv in range(KV_HEADS):
                    for t in range(TILES):
                        w = prob[:, kv, t * SEQ:(t + 1) * SEQ]
                        last = nc.vector.tensor_scalar(w, w, sums[:, 2 * kv + t:2 * kv + t + 1], None, ALU.mult)
                last.then_inc(S.prob_normed, 1)

            def weights_out(i):
                dve.wait_ge(S.probT_ps, i + 1)
                if i >= 1:
                    dve.wait_ge(S.attT_ps, i)
                nc.vector.tensor_copy(probT[:, 1, :], bank[PAIR_BANKS[i % 2][1]][:, :]).then_inc(S.probT_v, 1)

            def gla_scores(pair):
                dve.wait_ge(S.mix_ps, pair + 1)
                step(nc.vector.tensor_copy(mix[2 * pair + 1], bank[4][:, :]))
                dve.wait_ge(S.mix_a, pair + 1)
                for head in range(2):
                    blocks = mix[2 * pair + head].rearrange("p (s c i) -> p s c i", s=TILES, i=CHUNK)
                    for odd in range(2):
                        rows_ = slice(odd * CHUNK, (odd + 1) * CHUNK)
                        for st in range(TILES):
                            c = (2 * head + st) * CHUNK
                            last = nc.vector.copy_predicated(blocks[rows_, st, 2 * st + odd, :], later_sb[rows_, :],
                                                             bank[1][rows_, c:c + CHUNK])
                last.then_inc(S.mix_done, 1)

            for t in range(TILES):
                dve.wait_ge(S.gr_sig, t + 1)
                nc.vector.scalar_tensor_tensor(sg[:, t, :], bank[3 + t][:, :], stat[:, 4 + t:5 + t], sg[:, t, :],
                                               ALU.mult, ALU.mult).then_inc(S.swish_ps, 1)
            row_maxima(0)
            normalise(0)
            for i in range(1, ATT_PAIRS):
                if i == 2:
                    gla_scores(0)
                row_maxima(i)
                weights_out(i - 1)
                normalise(i)
            gla_scores(1)
            weights_out(ATT_PAIRS - 1)

            dve.wait_ge(S.ogla_sq, TILES)
            g8 = tok[:, :, 0:GLA_V].rearrange("p t (h d) -> p t h d", d=DV)
            for t in range(TILES):
                last = nc.vector.tensor_reduce(stat[:, 56 + 4 * t:60 + 4 * t], g8[:, t, :, :], AX.X, ALU.add)
            step(last)
            mean_eps(stat[:, 48:56], stat[:, 56:64], DV).then_inc(S.ogla_var, 1)
            dve.wait_ge(S.ogla_rstd, 1)
            dve.wait_ge(S.sg_done, 1)
            for t in range(TILES):
                last = nc.vector.tensor_tensor(g8[:, t, :, :], bank[3 + t][:, :].rearrange("p (h d) -> p h d", d=DV),
                                               stat[:, 56 + 4 * t:60 + 4 * t].rearrange("p (h o) -> p h o", o=1)
                                               .broadcast_to([P, GLA_HEADS, DV]), ALU.mult)
            step(last)
            for t in range(TILES):
                nc.vector.tensor_tensor(tok[:, t, 0:GLA_V], tok[:, t, 0:GLA_V], sg[:, t, :], ALU.mult)\
                    .then_inc(S.ogla_sb, 1)
            dve.wait_ge(S.glaT_ps, 1)
            nc.vector.tensor_copy(turned[:, 0:4, 0:P], bank[5][:, :].rearrange("p (k t) -> p k t", t=P)).then_inc(S.glaT_v, 1)

            def turned_out(t):
                dve.wait_ge(S.hT_ps, 2 * t + 1)
                nc.vector.tensor_copy(turned[:, 0:4, t * P:(t + 1) * P], bank[(0, 7)[t]][:, :].rearrange("p (k t) -> p k t", t=P))\
                    .then_inc(S.hT_v, 1)

            for t in range(TILES):
                dve.wait_ge(S.h_ps, t + 1)
                for nb in range(2):
                    nc.vector.tensor_tensor(h[:, t, nb * 512:(nb + 1) * 512], bank[Y[2 * t + nb]][:, :],
                                            h[:, t, nb * 512:(nb + 1) * 512], ALU.add).then_inc(S.h_done, 1)
                if t == 1:
                    turned_out(1)
                dve.wait_ge(S.hsq, t + 1)
                mean_eps(stat[:, 2 + t:3 + t], stat[:, t:t + 1], D).then_inc(S.var2, 1)
                if t == 0:
                    dve.wait_ge(S.rstd2, 1)
                    nc.vector.tensor_scalar(tok[:, 0, :], h[:, 0, :], stat[:, 4:5], None, ALU.mult).then_inc(S.n2_done, 1)
                if t == 0:
                    turned_out(0)
            dve.wait_ge(S.rstd2, 2)
            step(nc.vector.tensor_scalar(tok[:, 1, :], h[:, 1, :], stat[:, 5:6], None, ALU.mult))
            dve.wait_ge(S.part0, 2)
            dve.wait_ge(S.left1, 1)
            nc.vector.tensor_tensor(left[:, 1, :], tok[:, 1, :], parts[1][0], ALU.subtract).then_inc(S.left1, 1)

            dve.wait_ge(S.logit_ps, 1)
            dve.wait_ge(S.rstd2, TILES)
            for t in range(TILES):
                last = nc.vector.scalar_tensor_tensor(logit[:, t, :], bank[6][:, t * EXPERTS:(t + 1) * EXPERTS],
                                                      stat[:, 4 + t:5 + t], router_b, ALU.mult, ALU.add)
            step(last)
            for t in range(TILES):
                last = nc.vector.max(top[:, t, :], logit[:, t, :])
            step(last)
            for t in range(TILES):
                last = nc.vector.tensor_scalar(stat[:, 6 + t:7 + t], top[:, t, 0:1], -1.0, None, ALU.mult)
            last.then_inc(S.top_done, 1)
            topu = topi.bitcast(U32).rearrange("p (t k) -> p t k", k=8)
            for t in range(TILES):
                last = nc.vector.max_index(topu[:, t, :], top[:, t, :], logit[:, t, :])
            step(last)
            step(nc.vector.tensor_copy(topf, topu))
            for t in range(TILES):
                last = nc.vector.tensor_tensor(hit[:, t, :].rearrange("p (k e) -> p k e", e=EXPERTS),
                                               iota[:, 0:EXPERTS].rearrange("p (o e) -> p o e", o=1).broadcast_to([P, TOP_K, EXPERTS]),
                                               topf[:, t, 0:TOP_K].rearrange("p (k o) -> p k o", o=1).broadcast_to([P, TOP_K, EXPERTS]),
                                               ALU.is_equal)
            step(last)
            for t in range(TILES):
                last = nc.vector.tensor_reduce(chosen[:, t, :], hit[:, t, :].rearrange("p (k e) -> p e k", e=EXPERTS), AX.X, ALU.max)
            last.then_inc(S.chosen_done, 1)
            step(nc.vector.memset(rank_t, -1.0))
            dve.wait_ge(S.rank_ps, 1)
            ranks = bank[0][:, 0:TILES * EXPERTS].rearrange("p (t e) -> p t e", e=EXPERTS)
            step(nc.vector.scalar_tensor_tensor(rank, ranks, 1.0, chosen, ALU.add, ALU.mult))
            step(nc.vector.tensor_scalar(rank_t[:, :, 0:EXPERTS], rank, -1.0, None, ALU.add))

            def tables():
                dve.wait_ge(S.wexp_done, TILES)
                step(nc.vector.tensor_tensor(weight, weight, chosen, ALU.mult))
                step(nc.vector.tensor_reduce(stat[:, 8:10], weight, AX.X, ALU.add))
                step(nc.vector.reciprocal(stat[:, 10:12], stat[:, 8:10]))
                step(nc.vector.memset(gate_t, 0.0))
                for t in range(TILES):
                    for r in range(ROUNDS):
                        last = nc.vector.tensor_scalar(gate_t[:, t, r * EXPERTS:(r + 1) * EXPERTS], weight[:, t, :],
                                                       stat[:, 10 + t:11 + t], None, ALU.mult)
                last.then_inc(S.tables_done, 1)
                dve.wait_ge(S.tables_done, 1)

            def later_rounds():
                for r in range(1, ROUNDS):
                    last = nc.vector.tensor_scalar(rank_t[:, :, r * EXPERTS:(r + 1) * EXPERTS], rank, -1.0 - CAP * r, None, ALU.add)
                step(last)
                dve.wait_ge(S.count_ps, 1)
                step(nc.vector.tensor_reduce(stat[0:1, 12:13], bank[1][0:1, 0:EXPERTS], AX.X, ALU.max))
                for r in range(1, ROUNDS):
                    last = nc.vector.tensor_scalar(stat[0:1, 12 + r:13 + r], stat[0:1, 12:13], CAP * r + 0.5, None, ALU.is_gt)
                step(last)
                step(nc.vector.tensor_reduce(stat[0:1, 16:17], stat[0:1, 13:12 + ROUNDS], AX.X, ALU.add))
                nc.vector.tensor_copy(extra[0:1, 0:1], stat[0:1, 16:17]).then_inc(S.extra_done, 1)

            def gather_mask(n):
                for t in range(TILES):
                    last = nc.vector.tensor_scalar(onehot[:, t, :], iota[:, 0:CAP], rank_t[:, t, bass.ds(n, 1)], None,
                                                   ALU.is_equal)
                last.then_inc(S.onehot_ready, 1)

            def gathered_out(n):
                dve.wait_ge(S.gathered, n + 1)
                nc.vector.tensor_tensor(xg.rearrange("p (k c) -> p k c", c=CAP), bank[6][:, :].rearrange("p (k c) -> p k c", c=CAP),
                                        ffn_g.rearrange("p (k o) -> p k o", o=1).broadcast_to([P, KD, CAP]), ALU.mult)\
                    .then_inc(S.xg_ready, 1)

            def expert(n):
                dve.wait_ge(S.gatedT_ps, n)
                for t in range(TILES):
                    last = nc.vector.tensor_scalar(gated[:, t, :], iota, rank_t[:, t, bass.ds(n, 1)],
                                                   gate_t[:, t, bass.ds(n, 1)], ALU.is_equal, ALU.mult)
                last.then_inc(S.gated_ready, 1)
                dve.wait_ge(S.gathered, n + 1)
                gather_mask(n + 1)
                dve.wait_ge(S.chunk_used, n * PER_EXPERT + W1_CHUNKS)
                nc.vector.tensor_scalar(glu, bank[2][:, :], LIMIT, None, ALU.min).then_inc(S.glu_ready, 1)
                nc.vector.tensor_scalar(lin, bank[5][:, :], LIMIT, -LIMIT, ALU.min, ALU.max).then_inc(S.dve_step, 1)
                dve.wait_ge(S.dve_step, n * 2 + (base + 1))
                nc.vector.scalar_tensor_tensor(lin, lin, 1.0, glu, ALU.add, ALU.mult).then_inc(S.dve_step, 1)
                dve.wait_ge(S.dve_step, n * 2 + (base + 2))
                dve.wait_ge(S.sig_ready, n + 1)
                nc.vector.tensor_tensor(lin, lin, sig, ALU.mult).then_inc(S.hid_ready, 1)
                gathered_out(n + 1)

            gather_mask(0)
            tables()
            gathered_out(0)
            later_rounds()
            dve.wait_ge(S.gateT_ps, 1)
            nc.vector.tensor_copy(gateT[0:EXPERTS, :], bank[7][0:EXPERTS, 0:SEQ]).then_inc(S.gateT_sb, 1)
            base = steps[0]
            for n in range(UNROLL):
                expert(n)
            bodies = EXPERTS // UNROLL
            dve.wait_ge(S.extra_done, 1)
            rounds = dve.value_load(extra[0:1, 0:1], min_val=0, max_val=ROUNDS - 1)
            with dve.Fori(1, rounds * bodies + bodies) as it:
                for q in range(UNROLL):
                    expert(it * UNROLL + q)

            for t in range(TILES):
                dve.wait_ge(S.combined, rounds * (TILES * EXPERTS) + (TILES * (EXPERTS - 1) + t + 1))
                for nb in range(2):
                    nc.vector.tensor_tensor(h[:, t, nb * 512:(nb + 1) * 512], bank[Y[2 * t + nb]][:, :],
                                            h[:, t, nb * 512:(nb + 1) * 512], ALU.add).then_inc(S.y_done, 1)
            for t in range(TILES):
                if t == 0:
                    dve.wait_ge(S.fin_g_ps, 1)
                dve.wait_ge(S.y_done, 2 * t + 2)
                for nb in range(2):
                    cols = slice(nb * 512, (nb + 1) * 512)
                    last = nc.vector.tensor_tensor(tok[:, t, cols], h[:, t, cols], bank[5 + nb][:, :], ALU.mult)
                last.then_inc(S.y_gained, 1)
                dve.wait_ge(S.ysq, 2 * t + 2)
                nc.vector.tensor_tensor(stat[:, t:t + 1], stat[:, 8 + 2 * t:9 + 2 * t], stat[:, 9 + 2 * t:10 + 2 * t], ALU.add)\
                    .then_inc(S.ysum, 1)
                dve.wait_ge(S.ysum, t + 1)
                mean_eps(stat[:, 2 + t:3 + t], stat[:, t:t + 1], D).then_inc(S.var3, 1)
            for t in range(TILES):
                dve.wait_ge(S.rstd3, t + 1)
                dve.wait_ge(S.y_gained, t + 1)
                nc.vector.tensor_scalar(tok[:, t, 512:D], tok[:, t, 512:D], stat[:, 4 + t:5 + t], None, ALU.mult)\
                    .then_inc(S.fin_v, 1)

        @block.tensor
        def _(pe):
            mm = nc.tensor.matmul
            pe.wait_ge(S.ident_in, 16)
            pe.wait_ge(S.x0_in, 16)
            pe.wait_ge(S.x1_in, 16)
            for pair in range(KD // 2):
                if pair >= 2:
                    pe.wait_ge(S.xT_v if pair == 2 else S.xT_a, 2)
                for k in (2 * pair, 2 * pair + 1):
                    for t in range(TILES):
                        o = (k % 2) * SEQ + t * P
                        last = nc.tensor.transpose(bank[6 + pair % 2][:, o:o + P], h[:, t, k * P:(k + 1) * P], ident)
                last.then_inc(S.xT_ps, 1)

            def xT(k, t=None):
                return turned[:, k, :] if t is None else turned[:, k, t * P:(t + 1) * P]

            for k in range(KD):
                pe.wait_ge(win_in[k], 16)
                pe.wait_ge((S.xT_v, S.xT_a)[k // 2 % 2], 2 * (k // 4) + k % 2 + 1)
                a, z = k == 0, k == KD - 1

                def put(o, l, r, first):
                    return mm(o, l, r, start=a and first, stop=z, skip_group_check=True)

                w = w_in_sb[:, k, :]
                put(bank[2][0:2 * RANK, 0:SEQ], w[:, C_ZG:C_AQ], xT(k), True)
                for i, c0 in enumerate((C_GQ, C_GK)):
                    for pair in range(2):
                        put(bank[i][:, pair * SEQ:(pair + 1) * SEQ], w[:, c0 + pair * P:c0 + (pair + 1) * P], xT(k), pair == 0)
                for t in range(TILES):
                    put(bank[3 + t][:, :], xT(k, t), w[:, C_AQ:C_AK], True)
                    last = put(bank[5][:, t * SEQ:(t + 1) * SEQ], xT(k, t), w[:, C_AK:D_IN], t == 0)
                if z:
                    last.then_inc(S.pass1, 1)
                if k == 5:
                    pe.wait_ge(S.diag_done, 1)
                    for t in range(TILES):
                        rl = mm(bank[6][:, t * P:(t + 1) * P], ones, diag[:, t * P:(t + 1) * P], start=True, stop=True)
                    rl.then_inc(S.rms_ps, 1)

            def gates():
                pe.wait_ge(S.zg_sb, 1)
                pe.wait_ge(S.gqk_sb, 2)
                pe.wait_ge(S.const_in, 16 * 8)
                for g in range(4):
                    last = mm(bank[g // 2][:, (g % 2) * SEQ:(g % 2 + 1) * SEQ], wg[0:2 * RANK, g * P:(g + 1) * P],
                              zg[0:2 * RANK, :], start=True, stop=True)
                last.then_inc(S.gates_ps, 1)

            pe.wait_ge(S.rms_sb, 1)
            for k in range(KD):
                for t in range(TILES):
                    last = mm(bank[6 + t][:, :], xT(k, t), w_in_sb[:, k, C_GV:C_GR], start=k == 0, stop=k == KD - 1)
                last.then_inc(S.pass2, 1)
                if k == 0:
                    gates()
            def turn_qk():
                pe.wait_ge(S.rope_done, 1)
                pe.wait_ge(S.gv_sb, TILES)
                for b in range(5):
                    for t in range(TILES):
                        o = (b % 2) * SEQ + t * P
                        last = nc.tensor.transpose(bank[(5, 2, 6)[b // 2]][:, o:o + P], rot[:, t, b * P:(b + 1) * P], ident)
                    if b in (1, 3, 4):
                        last.then_inc(S.qkT_ps, 1)

            pe.wait_ge(S.raw_sb, 3 * TILES)
            for k in range(KD):
                for t in range(TILES):
                    last = mm(bank[3 + t][:, :], xT(k, t), w_in_sb[:, k, C_GR:C_ZG], start=k == 0, stop=k == KD - 1)
                last.then_inc(S.pass3, 1)
                if k == KD - 3:
                    turn_qk()

            def scores(i):
                if i == 0:
                    pe.wait_ge(S.qkT_sb, 3)
                elif i >= 2:
                    pe.wait_ge(S.probT_a, i - 1)
                    pe.wait_ge(S.probT_v, i - 1)
                for t in range(TILES):
                    for kv in range(KV_HEADS):
                        rows_ = slice(kv * DH, (kv + 1) * DH)
                        last = mm(bank[PAIR_BANKS[i % 2][kv]][:, t * SEQ:(t + 1) * SEQ], qkT[rows_, i, t * P:(t + 1) * P],
                                  qkT[rows_, 4, :], start=True, stop=True)
                last.then_inc(S.score_ps, 1)

            def turn_weights(i):
                pe.wait_ge(S.prob_normed, i + 1)
                for kv in range(KV_HEADS):
                    for st in range(TILES):
                        for t in range(TILES):
                            o = st * SEQ + t * P
                            s = t * SEQ + st * P
                            last = nc.tensor.transpose(bank[PAIR_BANKS[i % 2][kv]][:, o:o + P], prob[:, kv, s:s + P], ident)
                last.then_inc(S.probT_ps, 1)

            def values(i):
                pe.wait_ge(S.probT_a, i + 1)
                pe.wait_ge(S.probT_v, i + 1)
                if i == 2:
                    pe.wait_ge(S.mix_done, 2)
                for st in range(TILES):
                    for kv in range(KV_HEADS):
                        last = mm(bank[i // 2][kv * DH:(kv + 1) * DH, (i % 2) * SEQ:(i % 2 + 1) * SEQ],
                                  av[:, st, kv * DH:(kv + 1) * DH], probT[:, kv, st * SEQ:(st + 1) * SEQ],
                                  start=st == 0, stop=st == TILES - 1, skip_group_check=True)
                last.then_inc(S.attT_ps, 1)

            OFF_DIAGONAL = ((0, 0, 64, 1, 0, 0), (0, 0, 128, 2, 0, 1), (0, 0, 128, 3, 0, 5), (1, 0, 64, 3, 0, 4),
                            (1, 64, 64, 2, 1, 4), (1, 0, 128, 1, 1, 2), (1, 0, 128, 0, 1, 5), (0, 64, 64, 0, 1, 0))

            def head_rows(odd):
                return slice(odd * DK, (odd + 1) * DK)

            def chunk_of(buf, odd, d, pair, c):
                return buf[head_rows(odd), 2 * d + pair, c * CHUNK:(c + 1) * CHUNK]

            def place(odd, st, lo, n, i):
                return bank[3 + odd][lo:lo + n, st * SEQ + i * CHUNK:st * SEQ + (i + 1) * CHUNK]

            def diagonal(pair, back):
                fwd = 1 - back
                for c in range(CHUNKS):
                    lo = (c % 2) * CHUNK
                    g = (2 * back + c // 2) * CHUNK
                    backward = mm(bank[1][lo:lo + CHUNK, g:g + CHUNK], chunk_of(gA, back, 1, pair, c), chunk_of(gX, back, 1, pair, c),
                                  start=True, stop=True)
                    if back == 0 and c == CHUNKS - 1:
                        backward.then_inc(S.backward_ps, 1)
                    last = mm(place(fwd, c // 2, lo, CHUNK, c), chunk_of(gA, fwd, 0, pair, c), chunk_of(gX, fwd, 0, pair, c),
                              start=True, stop=True)
                return last

            def gla_first(pair):
                if pair == 0:
                    pe.wait_ge(S.gla_ready, 6)
                    pe.wait_ge(S.kk_done, 1)
                    pe.wait_ge(S.swish_ps, TILES)
                else:
                    pe.wait_ge(S.mix_done, pair)
                diagonal(pair, 0)

            def gla_second(pair):
                for st, lo, n, i, d, at in OFF_DIAGONAL:
                    for odd in range(2):
                        keys = kk[head_rows(odd), 2 * d + pair, at:at + n // CHUNK, :].rearrange("p s i -> p (s i)")
                        mm(place(odd, st, lo, n, i), keys, chunk_of(gB, odd, d, pair, i), start=True, stop=True)
                pe.wait_ge(S.backward_ps, pair + 1)
                diagonal(pair, 1).then_inc(S.mix_ps, 1)

            def gla_outputs(hd):
                for t in range(TILES):
                    for st in range(TILES):
                        last = mm(bank[3 + t][:, hd * DV:(hd + 1) * DV], mix[hd][:, st * SEQ + t * P:st * SEQ + (t + 1) * P],
                                  gv[:, st, hd * DV:(hd + 1) * DV], start=st == 0, stop=st == TILES - 1)
                return last

            scores(0)
            gla_first(0)
            scores(1)
            turn_weights(0)
            gla_second(0)
            values(0)
            scores(2)
            turn_weights(1)
            gla_first(1)
            values(1)
            scores(3)
            turn_weights(2)
            gla_second(1)
            turn_weights(3)
            values(2)
            gla_outputs(0)
            gla_outputs(1)
            values(3)
            gla_outputs(2)
            gla_outputs(3).then_inc(S.ogla_ps, 1)

            def turn_heads(k0, done):
                for t, b in enumerate((5, 2)):
                    for k in range(4):
                        last = nc.tensor.transpose(bank[b][:, k * P:(k + 1) * P], tok[:, t, (k0 + k) * P:(k0 + k + 1) * P], ident)
                    last.then_inc(done, 1)

            def turn_h(t):
                for half, b in enumerate(((0, 1), (7, 4))[t]):
                    pe.wait_ge(S.h_done, 2 * t + half + 1)
                    for k in range(4):
                        kb = half * 4 + k
                        last = nc.tensor.transpose(bank[b][:, k * P:(k + 1) * P], h[:, t, kb * P:(kb + 1) * P], ident)
                    last.then_inc(S.hT_ps, 1)

            def router(t):
                for k in range(KD):
                    if k % 4 == 0:
                        pe.wait_ge((S.hT_v, S.hT_a)[k // 4], t + 1)
                    last = mm(bank[6][:, t * EXPERTS:(t + 1) * EXPERTS], xT(k, t), wr_sb[:, k, :], start=k == 0, stop=k == KD - 1)
                return last

            pe.wait_ge(S.w_out_att_in, 32)
            pe.wait_ge(S.attT_sb, 2)
            for t in range(TILES):
                if t == 1:
                    pe.wait_ge(S.ogla_sb, TILES)
                for k in range(4):
                    for nb in range(2):
                        last = mm(bank[Y[2 * t + nb]][:, :], xT(4 + k, t), w_out_att[:, k, nb * 512:(nb + 1) * 512],
                                  start=k == 0, stop=False, skip_group_check=True)
            last.then_inc(S.att_used, 1)
            pe.wait_ge(S.ogla_sb, TILES)
            turn_heads(0, S.glaT_ps)
            pe.wait_ge(S.w_out_gla_in, 16)
            for t in range(TILES):
                pe.wait_ge((S.glaT_v, S.glaT_a)[t], 1)
                for k in range(4):
                    if t == 1 and k == 2:
                        turn_h(0)
                    for nb in range(2):
                        last = mm(bank[Y[2 * t + nb]][:, :], xT(k, t), w_out_gla[:, k, nb * 512:(nb + 1) * 512],
                                  start=False, stop=k == 3, skip_group_check=True)
                last.then_inc(S.h_ps, 1)

            def split_of(n):
                return split_sb[B1_ROWS[n]:B1_ROWS[n] + GROUPS, :]

            def start_hidden(g, q):
                mm(bank[(2, 5)[g]][:, :], split_of(q % 2), b1_sb[q % 2][:, g * FG:(g + 1) * FG], start=True, stop=False,
                   skip_group_check=True)

            pe.wait_ge(S.wr_done, 1)
            router(0)
            turn_h(1)
            pe.wait_ge(b1_in[0], 16)
            start_hidden(1, 0)
            last = router(1)
            last.then_inc(S.logit_ps, 1)
            start_hidden(0, 0)

            pe.wait_ge(S.count_masks, 2)
            pe.wait_ge(S.chosen_done, 1)
            mm(bank[0][:, 0:EXPERTS], before_b, chosen[:, 0, :], start=True, stop=True)
            mm(bank[0][:, EXPERTS:2 * EXPERTS], ones_b, chosen[:, 0, :], start=True, stop=False)
            mm(bank[0][:, EXPERTS:2 * EXPERTS], before_b, chosen[:, 1, :], start=False, stop=True).then_inc(S.rank_ps, 1)
            mm(bank[1][:, 0:EXPERTS], ones_b, chosen[:, 0, :], start=True, stop=False)
            mm(bank[1][:, 0:EXPERTS], ones_b, chosen[:, 1, :], start=False, stop=True).then_inc(S.count_ps, 1)

            def turn_gates():
                pe.wait_ge(S.tables_done, 1)
                for t in range(TILES):
                    last = nc.tensor.transpose(bank[7][0:EXPERTS, t * P:(t + 1) * P], gate_t[:, t, 0:EXPERTS], ident)
                last.then_inc(S.gateT_ps, 1)

            def start_row(i):
                t, nb = divmod(i, 2)
                if i == 0:
                    pe.wait_ge(S.gateT_sb, 1)
                    pe.wait_ge(S.extra_done, 1)
                mm(bank[Y[i]][:, :], gateT[0:EXPERTS, t * P:(t + 1) * P], b2_sb[:, nb * 512:(nb + 1) * 512],
                   start=True, stop=False, skip_group_check=True)

            def gather(n):
                pe.wait_ge(S.onehot_ready, n + 1)
                pe.wait_ge(S.xg_ready, n)
                for k in range(KD):
                    for i in range(PARTS):
                        for t in range(TILES):
                            last = mm(bank[6][:, k * CAP:(k + 1) * CAP], parts[t][i][:, k * P:(k + 1) * P], onehot[:, t, :],
                                      start=i == 0 and t == 0, stop=i == PARTS - 1 and t == TILES - 1)
                last.then_inc(S.gathered, 1)

            def combine(i, stop=False):
                t, j = divmod(i, 2)
                last = mm(bank[Y[i]][:, :], gatedT[j * CAP:(j + 1) * CAP, t, :], res[j * CAP:(j + 1) * CAP, :],
                          start=False, stop=stop, skip_group_check=True)
                if j == 1:
                    last.then_inc(S.combined, 1)

            def loaded(q, r, it):
                c = q * PER_EXPERT + r
                first = isinstance(it, int)
                if first and c < EARLY_AT:
                    pe.wait_ge(slot_in[first_slot_of(c)], (c // SLOTS + 1) * 16)
                    return slot(first_slot_of(c))
                if first and c < EARLY_AT + EARLY:
                    pe.wait_ge(early_in[c - EARLY_AT], 16)
                    return early[c - EARLY_AT]
                pe.wait_ge(slot_in[slot_of(c)], (it * LOADS_PER_BODY + ((c - EARLY) // SLOTS + 1)) * 16)
                return slot(slot_of(c))

            def expert(n, q, it, first=False, second=False):
                if not first:
                    pe.wait_ge(b1_in[q % 2], (it * (UNROLL // 2) + (q // 2 + 1)) * 16)
                    start_hidden(1, q)
                    pe.wait_ge(S.res_ready, n)
                    start_hidden(0, q)
                pe.wait_ge(S.xg_ready, n + 1)
                for k in range(W1_CHUNKS):
                    chunk = loaded(q, k, it)
                    for j in range(GROUPS):
                        for g in range(2):
                            last = mm(bank[(2, 5)[g]][j * CAP:(j + 1) * CAP, :], xg[:, k * CAP:(k + 1) * CAP],
                                      chunk[:, g * FF + j * FG:g * FF + (j + 1) * FG], start=False, stop=k == KD - 1,
                                      skip_group_check=True)
                    last.then_inc(S.chunk_used, 1)
                    if second and k % 2 == 0:
                        start_row(k // 2)
                    if not first and k % 2 == 1:
                        combine(k // 2)
                gather(n + 1)
                pe.wait_ge(S.hid_ready, n + 1)
                for s in range(SUB):
                    last = nc.tensor.transpose(bank[5][:, s * P:(s + 1) * P], lin[:, s * P:(s + 1) * P], ident)
                last.then_inc(S.hidT_ps, 1)
                pe.wait_ge(S.gated_ready, n + 1)
                if first:
                    pe.wait_ge(S.gateT_sb, 1)
                else:
                    pe.wait_ge(S.gatedT_sb, n)
                for t in range(TILES):
                    last = nc.tensor.transpose(bank[7][:, t * P:(t + 1) * P], gated[:, t, :], ident)
                last.then_inc(S.gatedT_ps, 1)
                pe.wait_ge(S.hidT_sb, n + 1)
                for s in range(W2_CHUNKS):
                    chunk = by_half(loaded(q, W1_CHUNKS + s, it))
                    for half in range(GROUPS):
                        for j in range(GROUPS):
                            last = mm(bank[2][j * CAP:(j + 1) * CAP, :], hidT[:, s, half * CAP:(half + 1) * CAP],
                                      chunk[:, half, j * 512:(j + 1) * 512], start=s == 0 and half == 0,
                                      stop=s == SUB - 1 and half == GROUPS - 1, skip_group_check=True)
                    last.then_inc(S.chunk_used, 1)

            for t in range(TILES):
                pe.wait_ge(S.part2, t + 1)
            gather(0)
            turn_gates()
            for q in range(UNROLL):
                expert(q, q, 0, first=q == 0, second=q == 1)
            bodies = EXPERTS // UNROLL
            pe.wait_ge(S.extra_done, 1)
            rounds = pe.value_load(extra[0:1, 0:1], min_val=0, max_val=ROUNDS - 1)
            with pe.Fori(1, rounds * bodies + bodies) as it:
                for q in range(UNROLL):
                    expert(it * UNROLL + q, q, it)
            pe.wait_ge(S.res_ready, rounds * EXPERTS + EXPERTS)
            for i in range(4):
                combine(i, stop=True)
            pe.wait_ge(S.fin_g_in, 16)
            pe.wait_ge(S.xg_ready, rounds * EXPERTS + (EXPERTS + 1))
            for nb in range(2):
                last = mm(bank[5 + nb][:, :], ones[FIN_G_ROW:FIN_G_ROW + 1, :], fin_g[:, nb * 512:(nb + 1) * 512],
                          start=True, stop=True)
            last.then_inc(S.fin_g_ps, 1)


def kernel(x, mix_norm_g, w_in, w_gate_f, b_gate_f, w_gate_b, b_gate_b, gla_head_g, q_norm_g, k_norm_g,
           w_out, ffn_norm_g, w_router, b_router, w1, b1, w2, b2, final_norm_g):
    import concourse.bacc as bacc
    from concourse.bass_utils import run_bass_kernel_spmd

    def by_partition(v):
        return np.asarray(v).reshape(-1, P).T

    gate_w = np.zeros((2 * RANK, 2 * GLA_QK), np.float32)
    gate_w[0:RANK, 0:GLA_QK] = np.asarray(w_gate_f)[0]
    gate_w[RANK:, GLA_QK:] = np.asarray(w_gate_b)[0]
    columns = np.concatenate([by_partition(v) for v in (mix_norm_g, ffn_norm_g, b_gate_f, b_gate_b)], 1)
    rows = np.concatenate([np.asarray(v).reshape(-1) for v in (q_norm_g, k_norm_g, gla_head_g, b_router)])
    consts = {k: np.concatenate(v, 1).astype(np.float32) for k, v in shape_constants().items()}
    i = np.arange(P)
    arrays = {
        "x": np.asarray(x)[0],
        "w_in": np.asarray(w_in)[0],
        "w_out": np.asarray(w_out)[0],
        "w_router": np.asarray(w_router)[0].reshape(KD, P, EXPERTS).transpose(1, 0, 2).reshape(P, KD * EXPERTS),
        "w1": np.asarray(w1)[0],
        "b1": np.asarray(b1)[0],
        "w2": np.asarray(w2)[0],
        "b2": np.asarray(b2)[0],
        "gate_w": gate_w,
        "columns": columns,
        "rows": np.broadcast_to(rows, (P, rows.size)),
        "final_g": np.asarray(final_norm_g)[None, :],
        "c_keep": consts["c_keep"],
        "c_front": consts["c_front"],
        "later": ((i % CHUNK)[:, None] > np.arange(CHUNK)[None, :]).astype(np.int32),
        "split": (i[None, :] // CAP == np.arange(GROUPS)[:, None]).astype(np.float32),
    }
    nc = bacc.Bacc("TRN2", target_bir_lowering=False, num_devices=1)
    feeds, aps = {}, {}
    for name, a in arrays.items():
        a = np.ascontiguousarray(a)
        feeds[f"in_{name}_dram"] = a
        aps[name] = nc.dram_tensor(f"in_{name}_dram", a.shape, mybir.dt.from_np(a.dtype), kind="ExternalInput").ap()
    aps["out"] = nc.dram_tensor("out_dram", (SEQ, D), F32, kind="ExternalOutput").ap()
    encoder_layer(nc, **aps)
    r = run_bass_kernel_spmd(nc, [feeds], core_ids=[0])
    return r.results[0]["out_dram"].reshape(1, SEQ, D)
```
